# Optimizing a Trainium2 kernel written in Bass

```python
import jax, jax.numpy as jnp
from jax import lax
import numpy as np

D_MODEL = 1024
BATCH = 1
SEQ = 512
DEPTH = 2

CHUNK = 64
N_MIXERS = 2
N_MLSTM = (DEPTH + 1) // 2
N_RGLRU = DEPTH // 2

ML_HEADS = 8
ML_QK_DIM = D_MODEL // 2 // ML_HEADS
ML_V_DIM = D_MODEL // ML_HEADS
ML_QK = ML_HEADS * ML_QK_DIM
ML_V = ML_HEADS * ML_V_DIM
ML_IN = 2 * ML_QK + 2 * ML_V + 2 * ML_HEADS
GATE_CAP = 15.0
ML_M_INIT = -1e30

LRU_WIDTH = D_MODEL
LRU_BLOCKS = 4
LRU_BLOCK = LRU_WIDTH // LRU_BLOCKS
CONV_WIDTH = 4
LRU_C = 8.0

_FF_RAW = -(-8 * D_MODEL // 3)
D_FF = -(-_FF_RAW // 256) * 256

EPS = 1e-6

kernel_name = "hybrid_mlstm_rglru_trunk"

def rms_norm(x, g):
    xf = x.astype(jnp.float32)
    y = xf * lax.rsqrt(jnp.mean(xf * xf, axis=-1, keepdims=True) + EPS)
    return (y * g.astype(jnp.float32)).astype(x.dtype)

def soft_cap(z):
    return GATE_CAP * jnp.tanh(z / GATE_CAP)

def mlstm_mixer(x, w_in, b_if, head_norm, w_out):
    B, S, _ = x.shape
    H, dk, dv, L = ML_HEADS, ML_QK_DIM, ML_V_DIM, CHUNK
    NC = S // L
    proj = x @ w_in
    q, k, v, o, g = jnp.split(proj, [ML_QK, 2 * ML_QK, 2 * ML_QK + ML_V, 2 * ML_QK + 2 * ML_V], axis=-1)
    g = soft_cap(g.astype(jnp.float32) + b_if.astype(jnp.float32))
    log_i = g[..., :H]
    log_f = jax.nn.log_sigmoid(g[..., H:])

    def to_chunks(t, d):
        return t.astype(jnp.float32).reshape(B, NC, L, H, d).transpose(1, 0, 3, 2, 4)

    qc = to_chunks(q, dk) * (dk ** -0.5)
    kc = to_chunks(k, dk)
    vc = to_chunks(v, dv)
    li = log_i.reshape(B, NC, L, H).transpose(1, 0, 3, 2)
    lf = log_f.reshape(B, NC, L, H).transpose(1, 0, 3, 2)
    causal = jnp.tril(jnp.ones((L, L), dtype=bool))

    def step(carry, inp):
        C, n, m = carry
        qb, kb, vb, lib, lfb = inp
        b = jnp.cumsum(lfb, axis=-1)
        D = b[..., :, None] - b[..., None, :] + lib[..., None, :]
        D = jnp.where(causal, D, -jnp.inf)
        inter = b + m[..., None]
        m_t = jnp.maximum(jnp.max(D, axis=-1), inter)
        P = jnp.exp(D - m_t[..., None]) * jnp.einsum('bhld,bhsd->bhls', qb, kb)
        w_inter = jnp.exp(inter - m_t)
        num = jnp.einsum('bhls,bhsv->bhlv', P, vb) + w_inter[..., None] * jnp.einsum('bhld,bhdv->bhlv', qb, C)
        den = jnp.sum(P, axis=-1) + w_inter * jnp.einsum('bhld,bhd->bhl', qb, n)
        den = jnp.maximum(jnp.abs(den), jnp.exp(-m_t))
        h = num / den[..., None]
        g_tot = b[..., -1]
        a = g_tot[..., None] - b + lib
        m_new = jnp.maximum(g_tot + m, jnp.max(a, axis=-1))
        decay = jnp.exp(g_tot + m - m_new)
        wk = jnp.exp(a - m_new[..., None])[..., None] * kb
        C_new = decay[..., None, None] * C + jnp.einsum('bhsd,bhsv->bhdv', wk, vb)
        n_new = decay[..., None] * n + jnp.sum(wk, axis=2)
        return (C_new, n_new, m_new), h

    carry0 = (jnp.zeros((B, H, dk, dv), jnp.float32),
              jnp.zeros((B, H, dk), jnp.float32),
              jnp.full((B, H), ML_M_INIT, jnp.float32))
    _, hs = lax.scan(step, carry0, (qc, kc, vc, li, lf))
    hs = hs.transpose(1, 0, 3, 2, 4).reshape(B, S, H, dv)
    hs = hs * lax.rsqrt(jnp.mean(hs * hs, axis=-1, keepdims=True) + EPS)
    hs = hs * head_norm.astype(jnp.float32).reshape(H, dv)
    y = hs.reshape(B, S, ML_V) * jax.nn.sigmoid(o.astype(jnp.float32))
    return y.astype(x.dtype) @ w_out

def causal_depthwise_conv(u, w, bias):
    C = u.shape[-1]
    out = lax.conv_general_dilated(
        u, w[:, None, :].astype(u.dtype), window_strides=(1,), padding=[(CONV_WIDTH - 1, 0)],
        dimension_numbers=('NWC', 'WIO', 'NWC'), feature_group_count=C)
    return out + bias.astype(u.dtype)

def rglru_mixer(x, w_in, conv_w, conv_b, w_gate_a, b_gate_a, w_gate_x, b_gate_x, lam, w_out):
    B, S, _ = x.shape
    proj = x @ w_in
    gate_branch, u = proj[..., :LRU_WIDTH], proj[..., LRU_WIDTH:]
    u = causal_depthwise_conv(u, conv_w, conv_b)
    ub = u.reshape(B, S, LRU_BLOCKS, LRU_BLOCK)
    r = jax.nn.sigmoid((jnp.einsum('bsnc,ncd->bsnd', ub, w_gate_a).reshape(B, S, LRU_WIDTH)
                        + b_gate_a).astype(jnp.float32))
    i = jax.nn.sigmoid((jnp.einsum('bsnc,ncd->bsnd', ub, w_gate_x).reshape(B, S, LRU_WIDTH)
                        + b_gate_x).astype(jnp.float32))
    log_a = LRU_C * r * jax.nn.log_sigmoid(lam.astype(jnp.float32))
    a = jnp.exp(log_a)
    mult = jnp.sqrt(-jnp.expm1(2.0 * log_a))
    b = mult * i * u.astype(jnp.float32)

    def combine(lhs, rhs):
        a1, b1 = lhs
        a2, b2 = rhs
        return a1 * a2, a2 * b1 + b2

    _, h = lax.associative_scan(combine, (a, b), axis=1)
    y = h * jax.nn.gelu(gate_branch.astype(jnp.float32))
    return y.astype(x.dtype) @ w_out

def swiglu(x, w_gate, w_up, w_down):
    return (jax.nn.silu(x @ w_gate) * (x @ w_up)) @ w_down

def setup_inputs(seed: int = 0) -> dict:
    key = jax.random.key(seed)
    ks = jax.random.split(key, 24)
    f32 = jnp.float32

    def nrm(k, shape, fan_in):
        return jax.random.normal(k, shape, f32) * (fan_in ** -0.5)

    def gain(k, shape):
        return 1.0 + 0.05 * jax.random.normal(k, shape, f32)

    x = jax.random.normal(ks[0], (BATCH, SEQ, D_MODEL), f32)
    ml_w_in = nrm(ks[1], (N_MLSTM, D_MODEL, ML_IN), D_MODEL)
    b_i = 0.1 * jax.random.normal(ks[2], (N_MLSTM, ML_HEADS), f32)
    b_f = 3.0 + 3.0 * jax.random.uniform(ks[3], (N_MLSTM, ML_HEADS), f32)
    ml_b_if = jnp.concatenate([b_i, b_f], axis=-1)
    ml_head_norm = gain(ks[4], (N_MLSTM, ML_V))
    ml_w_out = nrm(ks[5], (N_MLSTM, ML_V, D_MODEL), ML_V)
    lru_w_in = nrm(ks[6], (N_RGLRU, D_MODEL, 2 * LRU_WIDTH), D_MODEL)
    lru_conv_w = nrm(ks[7], (N_RGLRU, CONV_WIDTH, LRU_WIDTH), CONV_WIDTH)
    lru_conv_b = 0.02 * jax.random.normal(ks[8], (N_RGLRU, LRU_WIDTH), f32)
    lru_w_gate_a = nrm(ks[9], (N_RGLRU, LRU_BLOCKS, LRU_BLOCK, LRU_BLOCK), LRU_BLOCK)
    lru_b_gate_a = 0.02 * jax.random.normal(ks[10], (N_RGLRU, LRU_WIDTH), f32)
    lru_w_gate_x = nrm(ks[11], (N_RGLRU, LRU_BLOCKS, LRU_BLOCK, LRU_BLOCK), LRU_BLOCK)
    lru_b_gate_x = 0.02 * jax.random.normal(ks[12], (N_RGLRU, LRU_WIDTH), f32)
    u = jax.random.uniform(ks[13], (N_RGLRU, LRU_WIDTH), f32, minval=0.9, maxval=0.999)
    lru_lambda = jnp.log(u) - jnp.log1p(-u)
    lru_w_out = nrm(ks[14], (N_RGLRU, LRU_WIDTH, D_MODEL), LRU_WIDTH)
    norm_pre_mix = gain(ks[15], (DEPTH, D_MODEL))
    norm_post_mix = gain(ks[16], (DEPTH, D_MODEL))
    norm_pre_ffn = gain(ks[17], (DEPTH, D_MODEL))
    norm_post_ffn = gain(ks[18], (DEPTH, D_MODEL))
    ffn_w_gate = nrm(ks[19], (DEPTH, D_MODEL, D_FF), D_MODEL)
    ffn_w_up = nrm(ks[20], (DEPTH, D_MODEL, D_FF), D_MODEL)
    ffn_w_down = nrm(ks[21], (DEPTH, D_FF, D_MODEL), D_FF)
    return {
        "x": x,
        "ml_w_in": ml_w_in, "ml_b_if": ml_b_if, "ml_head_norm": ml_head_norm, "ml_w_out": ml_w_out,
        "lru_w_in": lru_w_in, "lru_conv_w": lru_conv_w, "lru_conv_b": lru_conv_b,
        "lru_w_gate_a": lru_w_gate_a, "lru_b_gate_a": lru_b_gate_a,
        "lru_w_gate_x": lru_w_gate_x, "lru_b_gate_x": lru_b_gate_x,
        "lru_lambda": lru_lambda, "lru_w_out": lru_w_out,
        "norm_pre_mix": norm_pre_mix, "norm_post_mix": norm_post_mix,
        "norm_pre_ffn": norm_pre_ffn, "norm_post_ffn": norm_post_ffn,
        "ffn_w_gate": ffn_w_gate, "ffn_w_up": ffn_w_up, "ffn_w_down": ffn_w_down,
    }

def reference(x, ml_w_in, ml_b_if, ml_head_norm, ml_w_out,
              lru_w_in, lru_conv_w, lru_conv_b, lru_w_gate_a, lru_b_gate_a,
              lru_w_gate_x, lru_b_gate_x, lru_lambda, lru_w_out,
              norm_pre_mix, norm_post_mix, norm_pre_ffn, norm_post_ffn,
              ffn_w_gate, ffn_w_up, ffn_w_down):
    h = x
    for layer in range(DEPTH):
        j = layer // N_MIXERS
        y = rms_norm(h, norm_pre_mix[layer])
        if layer % N_MIXERS == 0:
            y = mlstm_mixer(y, ml_w_in[j], ml_b_if[j], ml_head_norm[j], ml_w_out[j])
        else:
            y = rglru_mixer(y, lru_w_in[j], lru_conv_w[j], lru_conv_b[j],
                            lru_w_gate_a[j], lru_b_gate_a[j], lru_w_gate_x[j], lru_b_gate_x[j],
                            lru_lambda[j], lru_w_out[j])
        h = h + rms_norm(y, norm_post_mix[layer])
        y = swiglu(rms_norm(h, norm_pre_ffn[layer]), ffn_w_gate[layer], ffn_w_up[layer], ffn_w_down[layer])
        h = h + rms_norm(y, norm_post_ffn[layer])
    return h


_drawn_inputs = setup_inputs


def setup_inputs(seed=0):
    import zlib

    import numpy as np

    out = dict(_drawn_inputs(seed))
    spreads = {}
    factors = {'lru_b_gate_a': 22.691, 'lru_b_gate_x': 8.0}
    for name, (base, spread) in spreads.items():
        noise = np.random.default_rng([zlib.crc32(name.encode()), seed]).standard_normal(out[name].shape)
        drawn = base * np.exp(spread * noise) if base else spread * noise
        out[name] = __import__('jax').numpy.asarray(drawn.astype(out[name].dtype))
    for name, factor in factors.items():
        out[name] = (out[name] * factor).astype(out[name].dtype)
    return out
```

```python
from contextlib import ExitStack

import numpy as np
import concourse.bass as bass
import concourse.mybir as mybir

F32 = mybir.dt.float32
F32R = mybir.dt.float32r
ALU = mybir.AluOpType
ACT = mybir.ActivationFunctionType

P = 128
D = 1024
S = 512
KT = D // P
TT = S // P
HALF = S // 2
HEADS = 8
DK = 64
DV = 128
QK = HEADS * DK
VW = HEADS * DV
GATE_CAP = 15.0
LRU_C = 8.0
CONV = 4
FF = 2816
FT = FF // P
EPS = 1e-6
NEG = -1e30
BC = 256
FP = FF // BC
DKT = FT // 2

N_Q, N_K, N_V, N_O = 0, 2, 4, 8
N_MLOUT = 12
N_UP0 = 16
N_DOWN0 = N_UP0 + 2 * FP
N_U = N_DOWN0 + 2 * KT
N_GB0 = N_U + 4
N_GA, N_GX = N_GB0 + 1, N_GB0 + 2
N_GB1 = N_GX + 1
N_RGOUT = N_GB1 + 3
N_UP1 = N_RGOUT + 4
N_DOWN1 = N_UP1 + 2 * FP
N_END = N_DOWN1 + 2 * KT

V_PREMIX, V_POSTMIX, V_PREFFN, V_POSTFFN, V_HEAD, V_CONVW, V_CONVB, V_LAM, V_BA = (
    0, 16, 32, 48, 64, 72, 104, 112, 120)

ITEMS_OUT = [(0, 0, 1, 0, S), (1, 1, 1, 0, S), (2, 2, 1, 0, S), (3, 3, 1, 0, S),
             (0, 4, 2, 0, HALF), (1, 6, 2, 0, HALF), (2, 4, 2, HALF, HALF), (3, 6, 2, HALF, HALF)]
ITEMS_DOWN = [(m % 2, m, 1, 0, S) for m in range(7)] + [(1, 7, 1, 0, HALF), (2, 7, 1, HALF, HALF)]

RESULT_BANKS = [(0, 3), (4, 6), (1, 2), (0, 3)]


def build(nc, a, out):
    ctx = ExitStack()
    with ctx:
        free = [-(-nc.sbuf_base // 64) * 64]

        def sb(name, shape, dt=F32):
            size = int(np.prod(shape[1:])) * 4
            t = nc.alloc_sbuf_tensor_at(name, shape, dt, offset=free[0])
            free[0] += -(-size // 32) * 32
            return t

        vt = sb("vt", [P, P])
        vx = sb("vx", [P, KT])
        ident = sb("ident", [P, P])
        ones = sb("ones", [P, P])
        small = sb("small", [P, 32])
        expo = sb("expo", [P, 8])
        bif = sb("bif", [P, 2])
        h = sb("h", [P, KT, S])
        xs_at = free[0]
        xsh = sb("xsh", [P, KT, S], F32R)
        xsl = sb("xsl", [P, KT, S], F32R)
        y = sb("y", [P, KT, S])
        raw = [sb(f"raw{s}", [P, 2048]) for s in range(2)]
        wh = [sb(f"wh{s}", [P, 2048], F32R) for s in range(2)]
        wl = [sb(f"wl{s}", [P, 2048], F32R) for s in range(2)]
        sqy = sb("sqy", [P, S])
        accy = sb("accy", [P, S])
        hsq = sb("hsq", [P, KT, HALF])
        diag = sb("diag", [P, 2, P])
        sil = sb("sil", [P, 2, S])
        prod = sb("prod", [P, 2, S])
        region = free[0]
        acth = sb("acth", [P, FT, S], F32R)
        actl = sb("actl", [P, FT, S], F32R)
        assert free[0] <= nc.sbuf_usable_end, (free[0], nc.sbuf_usable_end)
        end = free[0]
        free[0] = region
        qT = sb("qT", [P, QK // P, S])
        kT = sb("kT", [P, QK // P, S])
        v = sb("v", [P, TT, HEADS, DV + 1])
        sigo = sb("sigo", [P, KT, S])
        z = sb("z", [HEADS, S])
        ct = sb("ct", [P, TT, HEADS])
        emt = sb("emt", [P, TT, HEADS])
        mask = sb("mask", [P, P])
        sel = sb("sel", [HEADS, HEADS, P])
        early = free[0]
        masked = [sb(f"masked{i}", [P, TT, P]) for i in range(2)]
        dec = [sb(f"dec{i}", [P, 1280]) for i in range(2)]
        pt = [sb(f"pt{i}", [P, 1280]) for i in range(2)]
        nsc = [sb(f"nsc{i}", [P, TT, DV]) for i in range(2)]
        ymix = [sb(f"ymix{i}", [P, S]) for i in range(2)]
        den = sb("den", [P, 2, 4, TT])
        assert free[0] <= end, (free[0], end)
        free[0] = early
        xin = sb("xin", [P, TT, D])
        vrow = sb("vrow", [P, P])
        vrow2 = sb("vrow2", [KT, P])
        gw = sb("gw", [P, KT, 40])
        assert free[0] <= end
        free[0] = early
        tg, ge, gy, gl_, gd, gi, gli, glf, gB, gm, gc, gem, gz = (
            sb(f"g{i}", [40, S]) for i in range(13))
        assert free[0] <= end + 0
        free[0] = region
        upad = sb("upad", [P, KT, CONV - 1 + S + 1])
        uc = sb("uc", [P, KT, S])
        at_uch = free[0]
        uch = sb("uch", [P, KT, S], F32R)
        ucl = sb("ucl", [P, KT, S], F32R)
        gel = sb("gel", [P, KT, S])
        sgi = sb("sgi", [P, 2, S])
        lamc = sb("lamc", [P, 6, KT])
        assert free[0] <= end, (free[0], end)
        free[0] = at_uch
        la = sb("la", [P, KT, S])
        lt = sb("lt", [P, KT, S])
        free[0] = xs_at
        outT = sb("outT", [P, TT, D])

        bank = [ctx.enter_context(nc.psum_tensor(f"bank{i}", [P, 512], F32))[:, :] for i in range(8)]
        M = bank[:4]
        SUM = bank[4:6]
        ROW = bank[6:8]

        def sem(name):
            return ctx.enter_context(nc.semaphore(name))

        x_in = [sem(f"x_in{j}") for j in range(TT)]
        vec_in = sem("vec_in")
        gw_in = sem("gw_in")
        stored = sem("stored")
        raw_in = [sem("raw_in0"), sem("raw_in1")]
        hi_done = sem("hi_done")
        lo_done = sem("lo_done")
        w_used = sem("w_used")
        consts = sem("consts")
        cz = sem("cz")
        vT_done = sem("vT_done")
        v_ready = sem("v_ready")
        xT_done = sem("xT_done")
        hx_v = sem("hx_v")
        hx_a = sem("hx_a")
        xsum = sem("xsum")
        item_done = sem("item_done")
        item_out = sem("item_out")
        item_acc = sem("item_acc")
        ysum = sem("ysum")
        ymean = sem("ymean")
        yroot = sem("yroot")
        ydiag = sem("ydiag")
        yrow = sem("yrow")
        yscaled = sem("yscaled")
        h_up = sem("h_up")
        h_sq = sem("h_sq")
        hsum = sem("hsum")
        hmean = sem("hmean")
        hroot = sem("hroot")
        hdiag = sem("hdiag")
        hrow = sem("hrow")
        xf = sem("xf")
        xh = sem("xh")
        xl_v = sem("xl_v")
        xl_p = sem("xl_p")
        gate_done = sem("gate_done")
        up_done = sem("up_done")
        silu = sem("silu")
        prod_done = sem("prod_done")
        act_h = sem("act_h")
        act_l = sem("act_l")
        in_done = sem("in_done")
        in_v = sem("in_v")
        in_a = sem("in_a")
        gates_mm = sem("gates_mm")
        g_a = sem("g_a")
        g_v = sem("g_v")
        gT = sem("gT")
        gT_out = sem("gT_out")
        mrow = sem("mrow")
        msk = sem("msk")
        decs = sem("decs")
        score = sem("score")
        ptd = sem("ptd")
        pv = sem("pv")
        nsq = sem("nsq")
        dens = sem("dens")
        mroot = sem("mroot")
        nscd = sem("nscd")
        nT = sem("nT")
        ym = sem("ym")
        ymh = sem("ymh")
        yml = sem("yml")
        u_done = sem("u_done")
        u_out = sem("u_out")
        upz = sem("upz")
        conv = sem("conv")
        uh = sem("uh")
        ul = sem("ul")
        gb_done = sem("gb_done")
        gb_out = sem("gb_out")
        ga_done = sem("ga_done")
        ga_out = sem("ga_out")
        iu = sem("iu")
        ab = sem("ab")
        rsq = sem("rsq")
        one_a2 = sem("one_a2")
        roots = sem("roots")
        den_step = sem("den_step")
        ry = sem("ry")
        ryh = sem("ryh")
        ryl = sem("ryl")
        lam_a = sem("lam_a")
        lam_v = sem("lam_v")
        oT = sem("oT")
        oc_v = sem("oc_v")
        oc_a = sem("oc_a")

        block = ctx.enter_context(nc.Block())

        def kview(t, c=BC):
            n = KT if c == BC else DKT
            return t[:, 0:n * c].rearrange("p (k c) -> p k c", c=c)

        def rows(w):
            return w.rearrange("(k p) c -> p k c", p=P)

        w_in = rows(a["ml_w_in"][0])
        w_mlout = rows(a["ml_w_out"][0])
        w_lru = rows(a["lru_w_in"][0])
        w_rgout = rows(a["lru_w_out"][0])
        w_ga = rows(a["lru_w_gate_a"][0].rearrange("n c d -> (n c) d"))
        w_gx = rows(a["lru_w_gate_x"][0].rearrange("n c d -> (n c) d"))
        items_before = [0, 8, 17, 25]
        done_before = [0, 4, 5, 9]
        first_block = [N_MLOUT, N_DOWN0, N_RGOUT, N_DOWN1]

        def item_ready(bd, i):
            n, base = first_block[bd], done_before[bd]
            if bd % 2 == 0:
                return [(item_done, base + 1), (w_used, n + 1), (item_done, base + 2), (w_used, n + 2),
                        (item_done, base + 3), (item_done, base + 4), (w_used, n + 3), (w_used, n + 4)][i]
            return (item_done, base + 1) if i == 7 else (w_used, n + 2 * i + 2) if i < 7 else (w_used, n + 16)

        def in_ready(i):
            if i < 2:
                return in_done, i + 1
            if i < 4:
                return w_used, i - 1
            b = (i - 4) // 2
            return (in_done, 3 + b) if i % 2 == 0 else (w_used, N_K + b + 1)

        def u_ready(i):
            if i < 2:
                return u_done, i + 1
            if i < 4:
                return w_used, N_U + i - 1
            b = (i - 4) // 2
            return (u_done, 3 + b) if i % 2 == 0 else (w_used, N_U + 3 + b)

        def gb_ready(g, m):
            return (gb_done, g + 1) if m == 0 else (w_used, N_GB0 + 1 if g == 0 else N_GB1 + g)

        def ga_ready(m, g):
            return (ga_done, 2 * m + g + 1) if m < KT - 1 else (w_used, N_GA + g + 1)

        def gate_ready(layer, b, j, m):
            nu = (N_UP0, N_UP1)[layer]
            if m == 0:
                return (gate_done, up_done)[b], FP * layer + 1 + j
            return w_used, nu + 2 * j + b + 1
        accs_before = [0, 13, 23, 36]

        def acc_ops(items):
            return sum(it[2] for it in items)

        @block.sync
        def _(sp):
            def load(n, src, c=BC, slot=None, wait=None, landed=None):
                s = n % 2 if slot is None else slot
                if wait is None:
                    wait = n - 1 if n >= 2 else None
                if wait is not None:
                    sp.wait_ge(lo_done, wait)
                sp.dma_start(kview(raw[s], c), src).then_inc(raw_in[s], 16)

            x = a["x"][0].rearrange("(j p) d -> p j d", p=P)
            for j in range(TT):
                sp.dma_start(xin[:, j, :], x[:, j, :]).then_inc(x_in[j], 16)
            for n in range(12):
                load(n, w_in[:, :, n * BC:(n + 1) * BC])
            for n in range(4):
                load(N_MLOUT + n, w_mlout[:, :, n * BC:(n + 1) * BC])

            def ffn(layer, nu, nd):
                wg, wu = rows(a["ffn_w_gate"][layer]), rows(a["ffn_w_up"][layer])
                wd = rows(a["ffn_w_down"][layer])
                with sp.Fori(0, FP) as j:
                    load(0, wg[:, :, bass.ds(j * BC, BC)], slot=0, wait=nu + 2 * j - 1)
                    load(1, wu[:, :, bass.ds(j * BC, BC)], slot=1, wait=nu + 2 * j)
                with sp.Fori(0, KT) as m:
                    load(0, wd[:, 0:DKT, bass.ds(m * P, P)], c=P, slot=0, wait=nd + 2 * m - 1)
                    load(1, wd[:, DKT:FT, bass.ds(m * P, P)], c=P, slot=1, wait=nd + 2 * m)

            ffn(0, N_UP0, N_DOWN0)
            for n in range(4):
                load(N_U + n, w_lru[:, :, D + n * BC:D + (n + 1) * BC])
            load(N_GB0, w_lru[:, :, 0:BC])
            load(N_GA, w_ga)
            load(N_GX, w_gx)
            for n in range(3):
                load(N_GB1 + n, w_lru[:, :, (n + 1) * BC:(n + 2) * BC])
            for n in range(4):
                load(N_RGOUT + n, w_rgout[:, :, n * BC:(n + 1) * BC])
            ffn(1, N_UP1, N_DOWN1)
            o = out[0].rearrange("(j p) d -> p j d", p=P)
            for j in range(TT):
                sp.wait_ge(oc_v, j + 1)
                sp.wait_ge(oc_a, j + 1)
                sp.dma_start(o[:, j, :], outT[:, j, :]).then_inc(stored, 16)
            sp.wait_ge(stored, 16 * TT)

        @block.scalar
        def _(act):
            def hi(n, c=2048, slot=None, landed=None, used=None):
                s = n % 2 if slot is None else slot
                act.wait_ge(raw_in[s], 16 * (n // 2 + 1) if landed is None else landed)
                if used is None:
                    used = n - 1 if n >= 2 else None
                if used is not None:
                    act.wait_ge(w_used, used)
                act.activation(wh[s][:, 0:c], raw[s][:, 0:c], ACT.Copy).then_inc(hi_done, 1)

            def item(bd, i, bk, m0, nm, t0, nt, acc):
                act.wait_ge(*item_ready(bd, i))
                src = bank[bk][:, 0:nm * nt].rearrange("p (m t) -> p m t", m=nm)
                sq = sqy[:, 0:nm * nt].rearrange("p (m t) -> p m t", m=nm)
                act.activation(y[:, m0, t0:t0 + nt] if nm == 1 else y[:, m0:m0 + nm, t0:t0 + nt],
                               bank[bk][:, 0:nt] if nm == 1 else src, ACT.Copy)
                act.wait_ge(item_acc, acc)
                act.activation(sqy[:, 0:nt] if nm == 1 else sq,
                               bank[bk][:, 0:nt] if nm == 1 else src, ACT.Square).then_inc(item_out, 1)

            def items(bd, which, lst):
                for i in which:
                    item(bd, i, *lst[i],
                         accs_before[bd] + 1 + acc_ops(lst[:i]))

            def squares_h(bd, q):
                if q == 1 or bd:
                    act.wait_ge(hsum, 2 * bd + q + 0)
                for k in range(KT):
                    act.wait_ge(h_up, 16 * bd + 8 * q + k + 1)
                    act.activation(hsq[:, k, :], h[:, k, q * HALF:(q + 1) * HALF],
                                   ACT.Square).then_inc(h_sq, 1)

            def xs_hi(p, q):
                for k in range(KT):
                    act.wait_ge(xf, 16 * p + 8 * q + k + 1)
                    act.activation(xsh[:, k, q * HALF:(q + 1) * HALF], y[:, k, q * HALF:(q + 1) * HALF],
                                   ACT.Copy).then_inc(xh, 1)

            def ffn(layer, nu, nd):
                base = 22 * layer
                for q in range(2):
                    act.wait_ge(*gate_ready(layer, 0, 0, q))
                    if layer or q:
                        act.wait_ge(prod_done, base + q)
                    act.activation(sil[:, :, 0:HALF], bank[2 * q][:, :].rearrange("p (m t) -> p m t", m=2),
                                   ACT.Silu).then_inc(silu, 1)
                with act.Fori(1, FP) as j:
                    hi(0, slot=0, landed=16 * (nu // 2 + 1) + 16 * j, used=nu - 1 + 2 * j)
                    hi(1, slot=1, landed=16 * (nu // 2 + 1) + 16 * j, used=nu + 2 * j)
                    for m in range(2):
                        act.wait_ge(*gate_ready(layer, 0, j, m))
                        act.wait_ge(prod_done, base + 2 * j)
                        act.activation(sil[:, m, :], bank[m][:, :], ACT.Silu).then_inc(silu, 1)
                c = DKT * P
                hi(nd, c)
                hi(nd + 1, c)
                bd = 2 * layer + 1
                with act.Fori(0, 3) as i:
                    for t in range(2):
                        hi(0, c, slot=0, landed=16 * ((nd + 2) // 2 + 1 + t) + 32 * i, used=nd + 1 + 2 * t + 4 * i)
                        hi(1, c, slot=1, landed=16 * ((nd + 2) // 2 + 1 + t) + 32 * i, used=nd + 2 + 2 * t + 4 * i)
                        down_item(bd, i, t)
                hi(nd + 14, c)
                hi(nd + 15, c)
                items(bd, [6], ITEMS_DOWN)

            def down_item(bd, i, t):
                act.wait_ge(w_used, first_block[bd] + 4 * i + 2 * t + 2)
                act.activation(y[:, bass.ds(2 * i + t, 1), :].rearrange("p a t -> p (a t)"), bank[t][:, :], ACT.Copy)
                act.wait_ge(item_acc, accs_before[bd] + 1 + 2 * i + t)
                act.activation(sqy[:, :], bank[t][:, :], ACT.Square).then_inc(item_out, 1)

            def boundary(bd, lst, n):
                a_items = [i for i in range(len(lst)) if lst[i][4] == HALF and lst[i][3] == 0]
                b_items = [i for i in range(len(lst)) if lst[i][4] == HALF and lst[i][3] == HALF]
                items(bd, a_items + b_items[:-1], lst)
                hi(n)
                squares_h(bd, 0)
                items(bd, b_items[-1:], lst)
                hi(n + 1)
                xs_hi(bd + 1, 0)
                squares_h(bd, 1)
                xs_hi(bd + 1, 1)

            def vec(ap, row, n):
                act.dma_start(vrow[row:row + n, :], ap).then_inc(vec_in, 16)

            vec(a["norm_pre_mix"].rearrange("l (k p) -> (l k) p", p=P), V_PREMIX, 16)
            vec(a["norm_post_mix"].rearrange("l (k p) -> (l k) p", p=P), V_POSTMIX, 16)
            vec(a["norm_pre_ffn"].rearrange("l (k p) -> (l k) p", p=P), V_PREFFN, 16)
            vec(a["norm_post_ffn"].rearrange("l (k p) -> (l k) p", p=P), V_POSTFFN, 16)
            vec(a["ml_head_norm"].rearrange("l (k p) -> (l k) p", p=P), V_HEAD, 8)
            vec(a["lru_conv_w"].rearrange("l j (k p) -> (l j k) p", p=P), V_CONVW, 32)
            vec(a["lru_conv_b"].rearrange("l (k p) -> (l k) p", p=P), V_CONVB, 8)
            vec(a["lru_lambda"].rearrange("l (k p) -> (l k) p", p=P), V_LAM, 8)
            vec(a["lru_b_gate_a"].rearrange("l (k p) -> (l k) p", p=P), V_BA, 8)
            act.dma_start(vrow2[:, :], a["lru_b_gate_x"].rearrange("l (k p) -> (l k) p", p=P)).then_inc(vec_in, 16)
            act.wait_ge(cz, 2)
            gcol = 2 * QK + 2 * VW
            act.dma_start(gw[:, :, 0:8], w_in[:, :, gcol:gcol + 8]).then_inc(gw_in, 16)
            act.dma_start(gw[:, :, 32:40], w_in[:, :, gcol + 8:gcol + 16]).then_inc(gw_in, 16)
            act.dma_start(bif[0:8, 0:1], a["ml_b_if"][0, 0:8].rearrange("(p o) -> p o", o=1)).then_inc(gw_in, 16)
            act.dma_start(bif[32:40, 0:1], a["ml_b_if"][0, 8:16].rearrange("(p o) -> p o", o=1)).then_inc(gw_in, 16)
            for j in range(TT):
                act.wait_ge(x_in[j], 16)
                act.activation(y[:, 2 * j:2 * j + 2, :], xin[:, j, :].rearrange("p (a t) -> p a t", a=2),
                               ACT.Square, accum_out=small[:, 16 + j:17 + j]).then_inc(xsum, 1)
            hi(0)
            for k in range(1, KT, 2):
                act.wait_ge(xT_done, k + 1)
                act.activation(h[:, k, :], bank[k][:, :], ACT.Copy).then_inc(hx_a, 1)
            xs_hi(0, 0)
            hi(1)
            xs_hi(0, 1)
            hi(2)
            act.wait_ge(gates_mm, 1)
            act.wait_ge(g_v, 1)
            act.activation(tg[:, :], SUM[0][0:40, :], ACT.Tanh, bias=bif[0:40, 1:2], scale=1.0 / GATE_CAP).then_inc(g_a, 1)
            act.wait_ge(g_a, 1)
            act.activation(ge[0:8, :], tg[32:40, :], ACT.Exp, scale=-GATE_CAP).then_inc(g_a, 1)
            hi(3)
            act.wait_ge(g_v, 2)
            act.activation(gl_[0:8, :], gy[0:8, :], ACT.Ln).then_inc(g_a, 1)
            act.wait_ge(g_a, 3)
            act.activation(gi[0:8, :], gl_[0:8, :], ACT.Exp, scale=-1.0).then_inc(g_a, 1)
            hi(4)
            act.wait_ge(g_v, 5)
            act.activation(gem[0:8, :], gm[0:8, :], ACT.Exp, scale=-2.0).then_inc(g_a, 1)
            for n in range(5, 12):
                hi(n)
            for i in range(8):
                if i == 2:
                    hi(12)
                act.wait_ge(*in_ready(16 + i))
                act.activation(sigo[:, i, :], bank[i % 4][:, :], ACT.Sigmoid).then_inc(in_a, 1)
            hi(13)
            OFF = [0, 512, 1024, 896]

            def decays(t):
                act.wait_ge(msk, t + 1)
                if t >= 2:
                    act.wait_ge(ptd, t - 1)
                for i in range(TT):
                    act.activation(dec[t % 2][:, OFF[i]:OFF[i] + P], masked[t % 2][:, i, :], ACT.Exp,
                                   bias=ct[:, i, t:t + 1])
                for i in range(TT - 1):
                    last = act.activation(dec[t % 2][:, OFF[i] + P:OFF[i] + S - P * i],
                                          SUM[t % 2][:, (i + 1) * P:S], ACT.Exp, bias=ct[:, i, t:t + 1])
                last.then_inc(decs, 1)

            def square_nums(t):
                act.wait_ge(pv, t + 1)
                if t >= 2:
                    act.wait_ge(dens, t - 1)
                for j in range(TT):
                    src = ROW[j // 2][:, (j % 2) * (DV + 1):(j % 2) * (DV + 1) + DV]
                    last = act.activation(hsq[:, j, 0:DV], src, ACT.Square, scale=float(DV) ** -0.5,
                                          accum_out=den[:, t % 2, 0, j:j + 1])
                last.then_inc(nsq, 1)

            def mix_hi(t):
                act.wait_ge(ym, t + 1)
                act.activation(xsh[:, t, :], ymix[t % 2][:, :], ACT.Copy).then_inc(ymh, 1)

            act.wait_ge(gT_out, 1)
            for t in range(HEADS + 2):
                if t < HEADS:
                    decays(t)
                if 1 <= t <= HEADS:
                    square_nums(t - 1)
                if t >= 2:
                    mix_hi(t - 2)
            items(0, [0, 1], ITEMS_OUT)
            hi(14)
            items(0, [2, 3], ITEMS_OUT)
            hi(15)
            boundary(0, ITEMS_OUT, N_UP0)
            ffn(0, N_UP0, N_DOWN0)
            boundary(1, ITEMS_DOWN, N_U)
            CW3 = V_CONVW + 3 * KT

            def u_evac(k0, nk, t0, nt, bk, i):
                act.wait_ge(*u_ready(i))
                for m in range(nk):
                    k, src = k0 + m, bank[bk][:, m * nt:(m + 1) * nt]
                    act.activation(upad[:, k, CONV - 1 + t0:CONV - 1 + t0 + nt], src, ACT.Copy)
                    last = act.activation(uc[:, k, t0:t0 + nt], src, ACT.Identity,
                                          scale=vt[:, CW3 + k:CW3 + k + 1],
                                          bias=vt[:, V_CONVB + k:V_CONVB + k + 1])
                last.then_inc(u_out, 1)

            def u_hi(k):
                act.wait_ge(conv, 3 * k + 3)
                act.activation(uch[:, k, :], uc[:, k, :], ACT.Copy).then_inc(uh, 1)

            act.wait_ge(lam_v, 1)
            act.activation(lamc[:, 1, :], lamc[:, 0, :], ACT.Exp, scale=-1.0).then_inc(lam_a, 1)
            act.wait_ge(lam_v, 2)
            act.activation(lamc[:, 3, :], lamc[:, 2, :], ACT.Ln).then_inc(lam_a, 1)
            u_evac(0, 2, 0, HALF, 0, 0)
            u_evac(2, 2, 0, HALF, 1, 1)
            u_evac(0, 2, HALF, HALF, 2, 2)
            hi(N_U + 2)
            u_evac(2, 2, HALF, HALF, 3, 3)
            hi(N_U + 3)
            for k in range(4):
                u_hi(k)
            for k in (4, 5):
                u_evac(k, 1, 0, S, k - 4, k)
            hi(N_GB0)
            for k in (6, 7):
                u_evac(k, 1, 0, S, k - 4, k)
            hi(N_GA)
            for k in range(4, 8):
                u_hi(k)

            def gelu(g, b0):
                for m in range(2):
                    act.wait_ge(*gb_ready(g, m))
                    act.activation(gel[:, 2 * g + m, :], bank[b0 + m][:, :], ACT.Gelu_apprx_tanh).then_inc(gb_out, 1)

            gelu(0, 0)
            hi(N_GX)
            for m in range(KT):
                act.wait_ge(*ga_ready(m, 0))
                act.activation(y[:, m, :], bank[2 + 2 * (m % 2)][:, :], ACT.Sigmoid,
                               bias=vt[:, V_BA + m:V_BA + m + 1]).then_inc(ga_out, 1)
                act.wait_ge(*ga_ready(m, 1))
                if m >= 2:
                    act.wait_ge(iu, m - 1)
                act.activation(sgi[:, m % 2, :], bank[3 + 2 * (m % 2)][:, :], ACT.Sigmoid,
                               bias=vx[:, m:m + 1]).then_inc(ga_out, 1)
            hi(N_GB1)
            hi(N_GB1 + 1)
            act.wait_ge(lam_v, 3)
            act.wait_ge(w_used, N_GX + 1)
            act.wait_ge(ga_out, 2 * KT)
            for m in range(KT):
                act.activation(la[:, m, :], y[:, m, :], ACT.Exp, scale=lamc[:, 4, m:m + 1])
                act.activation(lt[:, m, :], y[:, m, :], ACT.Tanh, scale=lamc[:, 5, m:m + 1]).then_inc(ab, 1)
            for m in range(0, KT, 4):
                act.wait_ge(one_a2, m + 4)
                act.activation(lt[:, m:m + 4, :], lt[:, m:m + 4, :], ACT.Sqrt).then_inc(roots, 1)
            for g in range(1, 4):
                gelu(g, [None, 0, 2, 0][g])
                if g == 1:
                    hi(N_GB1 + 2)
                if g == 2:
                    hi(N_RGOUT)
            hi(N_RGOUT + 1)
            for m in range(KT):
                act.wait_ge(ry, m + 1)
                act.activation(xsh[:, m, :], lt[:, m, :], ACT.Copy).then_inc(ryh, 1)
            items(2, [0, 1], ITEMS_OUT)
            hi(N_RGOUT + 2)
            items(2, [2, 3], ITEMS_OUT)
            hi(N_RGOUT + 3)
            boundary(2, ITEMS_OUT, N_UP1)
            ffn(1, N_UP1, N_DOWN1)
            items(3, [7, 8], ITEMS_DOWN)
            for j in range(TT):
                act.wait_ge(oT, 2 * j + 2)
                act.activation(outT[:, j, 512:1024], bank[RESULT_BANKS[j][1]][:, :], ACT.Copy).then_inc(oc_a, 1)

        @block.gpsimd
        def _(pool):
            def lo(n, c=2048, slot=None, count=None):
                s = n % 2 if slot is None else slot
                pool.wait_ge(hi_done, n + 1 if count is None else count)
                pool.tensor_tensor(wl[s][:, 0:c], raw[s][:, 0:c], wh[s][:, 0:c].bitcast(F32),
                                   ALU.subtract).then_inc(lo_done, 1)

            def root(dst, src, n, mean, mean_at, done):
                pool.wait_ge(mean, mean_at)
                pool.tensor_tensor(dst, src, expo[:, 0:n], ALU.pow).then_inc(done, 1)

            def ysq(bd, q):
                root(small[:, 4 + 2 * q:6 + 2 * q], small[:, 2 * q:2 * q + 2], 2, ymean, 2 * bd + q + 1, yroot)

            def hsqr(p, q):
                root(small[:, 12 + 2 * q:14 + 2 * q], small[:, 8 + 2 * q:10 + 2 * q], 2, hmean, 2 * p + q + 1, hroot)

            def residual(bd, q):
                for k in range(KT):
                    pool.wait_ge(yscaled, 16 * bd + 8 * q + k + 1)
                    t = slice(q * HALF, (q + 1) * HALF)
                    pool.tensor_tensor(h[:, k, t], h[:, k, t], y[:, k, t], ALU.add).then_inc(h_up, 1)

            def xs_lo(p, q):
                for k in range(1, KT, 2):
                    pool.wait_ge(xh, 16 * p + 8 * q + k + 1)
                    t = slice(q * HALF, (q + 1) * HALF)
                    pool.tensor_tensor(xsl[:, k, t], y[:, k, t], xsh[:, k, t].bitcast(F32),
                                       ALU.subtract).then_inc(xl_p, 1)

            def boundary(bd):
                ysq(bd, 0)
                residual(bd, 0)
                hsqr(bd + 1, 0)
                ysq(bd, 1)
                xs_lo(bd + 1, 0)
                residual(bd, 1)
                hsqr(bd + 1, 1)
                xs_lo(bd + 1, 1)

            def ffn(nu, nd):
                with pool.Fori(1, FP) as j:
                    lo(0, slot=0, count=nu + 2 * j + 1)
                    lo(1, slot=1, count=nu + 2 * j + 2)
                with pool.Fori(0, KT) as m:
                    lo(0, DKT * P, slot=0, count=nd + 2 * m + 1)
                    lo(1, DKT * P, slot=1, count=nd + 2 * m + 2)

            pool.memset(gw[:, :, :], 0.0).then_inc(cz, 1)
            pool.memset(bif[:, :], 0.0).then_inc(cz, 1)
            pool.memset(ident[:, :], 0.0).then_inc(consts, 1)
            pool.memset(ones[:, :], 1.0).then_inc(consts, 1)
            pool.memset(expo[:, :], -0.5).then_inc(consts, 1)
            pool.memset(mask[:, :], 0.0).then_inc(consts, 1)
            pool.memset(sel[:, :, :], 0.0).then_inc(consts, 1)
            pool.memset(v[:, :, :, DV:DV + 1], 1.0).then_inc(consts, 1)
            pool.wait_ge(consts, 6)
            pool.affine_select(out=ident[:, :], in_=ident[:, :], compare_op=ALU.not_equal, fill=1.0, base=0,
                               pattern=[[-1, P]], channel_multiplier=1).then_inc(consts, 1)
            pool.affine_select(out=mask[:, :], in_=mask[:, :], compare_op=ALU.is_ge, fill=NEG, base=0,
                               pattern=[[1, P]], channel_multiplier=-1).then_inc(consts, 1)
            pool.affine_select(out=sel[:, :, :], in_=sel[:, :, :], compare_op=ALU.not_equal, fill=1.0, base=0,
                               pattern=[[-1, HEADS], [0, P]], channel_multiplier=1).then_inc(consts, 1)
            lo(0)
            hsqr(0, 0)
            hsqr(0, 1)
            xs_lo(0, 0)
            lo(1)
            xs_lo(0, 1)
            for n in range(2, 14):
                lo(n)
            for t in range(HEADS + 2):
                if 1 <= t <= HEADS:
                    pool.wait_ge(dens, t)
                    pool.tensor_tensor(den[:, (t - 1) % 2, 3, :], den[:, (t - 1) % 2, 2, :], expo[:, 0:TT],
                                       ALU.pow).then_inc(mroot, 1)
                if t >= 2:
                    pool.wait_ge(ymh, t - 1)
                    pool.tensor_tensor(xsl[:, t - 2, :], ymix[t % 2][:, :], xsh[:, t - 2, :].bitcast(F32),
                                       ALU.subtract).then_inc(yml, 1)
            lo(14)
            lo(15)
            boundary(0)
            ffn(N_UP0, N_DOWN0)
            boundary(1)
            lo(N_U + 2)
            lo(N_U + 3)

            def u_lo(k):
                pool.wait_ge(uh, k + 1)
                pool.tensor_tensor(ucl[:, k, :], uc[:, k, :], uch[:, k, :].bitcast(F32), ALU.subtract).then_inc(ul, 1)

            for k in range(4):
                u_lo(k)
            lo(N_GB0)
            lo(N_GA)
            for k in range(4, 8):
                u_lo(k)
            for n in range(N_GX, N_RGOUT + 2):
                lo(n)
            for m in range(KT):
                pool.wait_ge(ryh, m + 1)
                pool.tensor_tensor(xsl[:, m, :], lt[:, m, :], xsh[:, m, :].bitcast(F32), ALU.subtract).then_inc(ryl, 1)
            lo(N_RGOUT + 2)
            lo(N_RGOUT + 3)
            boundary(2)
            ffn(N_UP1, N_DOWN1)
            ysq(3, 0)
            residual(3, 0)
            ysq(3, 1)
            residual(3, 1)

        @block.vector
        def _(dve):
            def lo(n):
                s = n % 2
                dve.wait_ge(hi_done, n + 1)
                dve.tensor_tensor(wl[s][:, :], raw[s][:, :], wh[s][:, :].bitcast(F32), ALU.subtract).then_inc(lo_done, 1)

            def mean(dst, src, done):
                dve.tensor_scalar(dst, src, 1.0 / D, EPS, ALU.mult, ALU.add).then_inc(done, 1)

            def to_diag(col, wait, at, done, free, free_at):
                dve.wait_ge(wait, at)
                if free is not None:
                    dve.wait_ge(free, free_at)
                dve.tensor_scalar(diag[:, 0, :], ident[:, :], small[:, col:col + 1], None, ALU.mult)
                dve.tensor_scalar(diag[:, 1, :], ident[:, :], small[:, col + 1:col + 2], None, ALU.mult).then_inc(done, 1)

            def clear_acc(bd):
                if bd:
                    dve.wait_ge(ysum, 2 * bd)
                dve.memset(accy[:, :], 0.0).then_inc(item_acc, 1)

            def accumulate(bd, i, lst):
                _, m0, nm, t0, nt = lst[i]
                dve.wait_ge(item_out, items_before[bd] + i + 1)
                for m in range(nm):
                    dve.wait_ge(item_acc, accs_before[bd] + 1 + acc_ops(lst[:i]) + m)
                    dve.tensor_tensor(accy[:, t0:t0 + nt], accy[:, t0:t0 + nt], sqy[:, m * nt:(m + 1) * nt],
                                      ALU.add).then_inc(item_acc, 1)

            def ymeans(bd, q):
                dve.wait_ge(ysum, 2 * bd + q + 1)
                mean(small[:, 2 * q:2 * q + 2], SUM[q][:, 0:2], ymean)

            def scale_y(bd, q, g):
                dve.wait_ge(yrow, 2 * bd + q + 1)
                t = slice(q * HALF, (q + 1) * HALF)
                for k in range(KT):
                    dve.scalar_tensor_tensor(out=y[:, k, t], in0=y[:, k, t], scalar=vt[:, g + k:g + k + 1],
                                             in1=ROW[q][:, 0:HALF], op0=ALU.mult, op1=ALU.mult).then_inc(yscaled, 1)

            def hmeans(bd, q):
                dve.wait_ge(hsum, 2 * bd + q + 1)
                mean(small[:, 8 + 2 * q:10 + 2 * q], SUM[q][:, 4:6], hmean)

            def xs_build(p, q, g):
                dve.wait_ge(hrow, 2 * p + q + 1)
                t = slice(q * HALF, (q + 1) * HALF)

                def low(k):
                    dve.wait_ge(xh, 16 * p + 8 * q + k + 1)
                    dve.tensor_tensor(xsl[:, k, t], y[:, k, t], xsh[:, k, t].bitcast(F32),
                                      ALU.subtract).then_inc(xl_v, 1)
                for k in range(KT):
                    dve.scalar_tensor_tensor(out=y[:, k, t], in0=h[:, k, t], scalar=vt[:, g + k:g + k + 1],
                                             in1=ROW[q][:, HALF:S], op0=ALU.mult, op1=ALU.mult).then_inc(xf, 1)
                    if k >= 2 and k % 2 == 0:
                        low(k - 2)
                low(6)

            def boundary(bd, lst, n, g_post, g_pre):
                a_items = [i for i in range(len(lst)) if lst[i][4] == HALF and lst[i][3] == 0]
                b_items = [i for i in range(len(lst)) if lst[i][4] == HALF and lst[i][3] == HALF]
                for i in a_items:
                    accumulate(bd, i, lst)
                ymeans(bd, 0)
                to_diag(4, yroot, 2 * bd + 1, ydiag, hrow, 2 * bd + 2)
                for i in b_items[:-1]:
                    accumulate(bd, i, lst)
                scale_y(bd, 0, g_post)
                lo(n)
                accumulate(bd, b_items[-1], lst)
                hmeans(bd, 0)
                to_diag(12, hroot, 2 * bd + 3, hdiag, yrow, 2 * bd + 1)
                ymeans(bd, 1)
                xs_build(bd + 1, 0, g_pre)
                to_diag(6, yroot, 2 * bd + 2, ydiag, hrow, 2 * bd + 3)
                lo(n + 1)
                scale_y(bd, 1, g_post)
                hmeans(bd, 1)
                to_diag(14, hroot, 2 * bd + 4, hdiag, yrow, 2 * bd + 2)
                xs_build(bd + 1, 1, g_pre)

            def ffn(layer):
                base = 22 * layer

                def half(q):
                    t = slice(q * HALF, (q + 1) * HALF)
                    up = bank[2 * q + 1][:, :].rearrange("p (m t) -> p m t", m=2)
                    n = base + q + 1
                    dve.wait_ge(*gate_ready(layer, 1, 0, q))
                    dve.wait_ge(silu, n)
                    if q:
                        dve.wait_ge(act_l, n - 1)
                    dve.tensor_tensor(prod[:, :, 0:HALF], sil[:, :, 0:HALF], up, ALU.mult).then_inc(prod_done, 1)
                    dve.wait_ge(prod_done, n)
                    dve.tensor_copy(acth[:, 0:2, t], prod[:, :, 0:HALF]).then_inc(act_h, 1)
                    dve.wait_ge(act_h, n)
                    dve.tensor_tensor(actl[:, 0:2, t], prod[:, :, 0:HALF], acth[:, 0:2, t].bitcast(F32),
                                      ALU.subtract).then_inc(act_l, 1)

                half(0)
                half(1)
                with dve.Fori(1, FP) as j:
                    for m in range(2):
                        n = base + 2 * j + m + 1
                        dve.wait_ge(*gate_ready(layer, 1, j, m))
                        dve.wait_ge(silu, n)
                        dve.wait_ge(act_l, n - 1)
                        dve.tensor_tensor(prod[:, m, :], sil[:, m, :], bank[2 + m][:, :], ALU.mult).then_inc(prod_done, 1)
                        dst_h = acth[:, bass.ds(2 * j + m, 1), :].rearrange("p a t -> p (a t)")
                        dst_l = actl[:, bass.ds(2 * j + m, 1), :].rearrange("p a t -> p (a t)")
                        dve.wait_ge(prod_done, n)
                        dve.tensor_copy(dst_h, prod[:, m, :]).then_inc(act_h, 1)
                        dve.wait_ge(act_h, n)
                        dve.tensor_tensor(dst_l, prod[:, m, :], dst_h.bitcast(F32), ALU.subtract).then_inc(act_l, 1)
                bd = 2 * layer + 1
                clear_acc(bd)
                with dve.Fori(0, 6) as m:
                    dve.wait_ge(item_out, items_before[bd] + 1 + m)
                    dve.wait_ge(item_acc, accs_before[bd] + 1 + m)
                    dve.tensor_tensor(accy[:, :], accy[:, :], sqy[:, :], ALU.add).then_inc(item_acc, 1)
                accumulate(bd, 6, ITEMS_DOWN)

            dve.wait_ge(vT_done, 1)
            dve.tensor_copy(vt[:, :], ROW[0][:, 0:P])
            dve.tensor_copy(vx[:, :], ROW[0][:, P:P + KT]).then_inc(v_ready, 1)
            dve.wait_ge(v_ready, 1)
            for k in range(0, 6, 2):
                dve.wait_ge(xT_done, k + 1)
                dve.tensor_copy(h[:, k, :], bank[k][:, :]).then_inc(hx_v, 1)
            dve.wait_ge(xT_done, 7)
            dve.tensor_copy(h[:, 6, :], bank[6][:, :]).then_inc(hx_v, 1)
            for q in range(2):
                dve.wait_ge(xsum, 2 * q + 2)
                mean(small[:, 8 + 2 * q:10 + 2 * q], small[:, 16 + 2 * q:18 + 2 * q], hmean)
            dve.wait_ge(gw_in, 64)
            dve.tensor_scalar(bif[0:40, 1:2], bif[0:40, 0:1], 1.0 / GATE_CAP, None, ALU.mult).then_inc(g_v, 1)
            dve.wait_ge(consts, 9)
            dve.wait_ge(hx_a, 4)
            dve.wait_ge(hx_v, 4)
            to_diag(12, hroot, 1, hdiag, None, 0)
            xs_build(0, 0, V_PREMIX)
            to_diag(14, hroot, 2, hdiag, hrow, 1)
            xs_build(0, 1, V_PREMIX)

            def q_out(i):
                dve.wait_ge(*in_ready(i))
                q, m0 = i // 2, 2 * (i % 2)
                dve.tensor_scalar(qT[:, m0:m0 + 2, q * HALF:(q + 1) * HALF],
                                  bank[i][:, :].rearrange("p (m t) -> p m t", m=2), float(DK) ** -0.5, None,
                                  ALU.mult).then_inc(in_v, 1)

            for i in range(4):
                q_out(i)
            G = HEADS
            dve.wait_ge(g_a, 2)
            dve.tensor_scalar(gli[0:G, :], tg[0:G, :], GATE_CAP, None, ALU.mult)
            dve.tensor_scalar(gy[0:G, :], ge[0:G, :], 1.0, None, ALU.add).then_inc(g_v, 1)
            dve.memset(gz[0:G, :], 0.0)
            dve.wait_ge(g_v, 2)
            dve.scalar_tensor_tensor(out=gd[0:G, :], in0=gy[0:G, :], scalar=-1.0, in1=ge[0:G, :],
                                     op0=ALU.add, op1=ALU.subtract).then_inc(g_v, 1)
            dve.wait_ge(g_a, 4)
            dve.wait_ge(g_v, 3)
            dve.tensor_tensor(gd[0:G, :], gd[0:G, :], gi[0:G, :], ALU.mult).then_inc(gT, 1)
            dve.wait_ge(gT, 1)
            dve.tensor_tensor(glf[0:G, :], gd[0:G, :], gl_[0:G, :], ALU.subtract).then_inc(gT, 1)
            dve.wait_ge(gT, 2)
            dve.tensor_tensor_scan(out=gB[0:G, :], data0=glf[0:G, :], data1=gz[0:G, :], initial=0.0,
                                   op0=ALU.add, op1=ALU.add).then_inc(g_v, 1)
            dve.tensor_tensor_scan(out=gm[0:G, :], data0=glf[0:G, :], data1=gli[0:G, :], initial=NEG,
                                   op0=ALU.add, op1=ALU.max).then_inc(g_v, 1)
            dve.wait_ge(g_v, 5)
            dve.tensor_tensor(z[:, :], gB[0:G, :], gm[0:G, :], ALU.subtract)
            dve.tensor_tensor(gc[0:G, :], gli[0:G, :], gB[0:G, :], ALU.subtract).then_inc(g_v, 1)
            for i in range(4, 8):
                dve.wait_ge(*in_ready(i))
                dve.tensor_copy(kT[:, i - 4, :], bank[i - 4][:, :]).then_inc(in_v, 1)
            dve.wait_ge(gT, 3)
            dve.tensor_copy(ct[:, :, :], SUM[1][:, 0:32].rearrange("p (j h) -> p j h", j=TT))
            dve.tensor_copy(emt[:, :, :], SUM[1][:, 32:64].rearrange("p (j h) -> p j h", j=TT)).then_inc(gT_out, 1)
            for i in range(8, 16):
                dve.wait_ge(*in_ready(i))
                blk, b = (i - 8) // 2, (i - 8) % 2
                for j in range(2):
                    last = dve.tensor_copy(v[:, 2 * b + j, 2 * blk:2 * blk + 2, 0:DV],
                                           bank[i % 4][:, j * 256:(j + 1) * 256].rearrange("p (h d) -> p h d", h=2))
                last.then_inc(in_v, 1)
            OFF = [0, 512, 1024, 896]

            def add_mask(t):
                dve.wait_ge(mrow, t + 1)
                if t >= 2:
                    dve.wait_ge(decs, t - 1)
                dve.tensor_tensor(masked[t % 2][:, :, :], SUM[t % 2][:, :].rearrange("p (j l) -> p j l", j=TT),
                                  mask[:, None, :].to_broadcast([P, TT, P]), ALU.add).then_inc(msk, 1)

            def weigh(t):
                dve.wait_ge(decs, t + 1)
                dve.wait_ge(score, t + 1)
                if t >= 2:
                    dve.wait_ge(pv, t - 1)
                dve.tensor_tensor(pt[t % 2][:, 0:512], dec[t % 2][:, 0:512], M[0][:, :], ALU.mult)
                dve.tensor_tensor(pt[t % 2][:, 512:1024], dec[t % 2][:, 512:1024], M[1][:, :], ALU.mult)
                dve.tensor_tensor(pt[t % 2][:, 1024:1280], dec[t % 2][:, 1024:1280], M[2][:, 0:256],
                                  ALU.mult).then_inc(ptd, 1)

            def denominators(t):
                dve.wait_ge(nsq, t + 1)
                if t >= 2:
                    dve.wait_ge(nscd, t - 1)
                d = den[:, t % 2]
                for b in range(2):
                    src = ROW[b][:, 0:2 * (DV + 1)].rearrange("p (j c) -> p j c", j=2)[:, :, DV]
                    last = dve.tensor_copy(d[:, 1, 2 * b:2 * b + 2], src)
                last.then_inc(den_step, 1)
                dve.wait_ge(den_step, 3 * t + 1)
                dve.tensor_tensor(d[:, 1, :], d[:, 1, :], d[:, 1, :], ALU.mult).then_inc(den_step, 1)
                dve.wait_ge(den_step, 3 * t + 2)
                dve.tensor_tensor(d[:, 1, :], d[:, 1, :], emt[:, :, t], ALU.max).then_inc(den_step, 1)
                dve.wait_ge(den_step, 3 * t + 3)
                dve.scalar_tensor_tensor(out=d[:, 2, :], in0=d[:, 1, :], scalar=EPS, in1=d[:, 0, :],
                                         op0=ALU.mult, op1=ALU.add).then_inc(dens, 1)

            def normalise(t):
                dve.wait_ge(mroot, t + 1)
                if t >= 2:
                    dve.wait_ge(nT, t - 1)
                for j in range(TT):
                    src = ROW[j // 2][:, (j % 2) * (DV + 1):(j % 2) * (DV + 1) + DV]
                    last = dve.tensor_scalar(nsc[t % 2][:, j, :], src, den[:, t % 2, 3, j:j + 1], None, ALU.mult)
                last.then_inc(nscd, 1)

            def gate_out(t):
                dve.wait_ge(nT, t + 1)
                if t == 0:
                    dve.wait_ge(in_a, 8)
                if t >= 2:
                    dve.wait_ge(yml, t - 1)
                dve.scalar_tensor_tensor(out=ymix[t % 2][:, :], in0=M[3][:, :], scalar=vt[:, V_HEAD + t:V_HEAD + t + 1],
                                         in1=sigo[:, t, :], op0=ALU.mult, op1=ALU.mult).then_inc(ym, 1)

            for t in range(HEADS + 2):
                if t < HEADS:
                    add_mask(t)
                if 1 <= t <= HEADS:
                    denominators(t - 1)
                    normalise(t - 1)
                if t < HEADS:
                    weigh(t)
                if t >= 2:
                    gate_out(t - 2)
            clear_acc(0)
            for i in range(4):
                accumulate(0, i, ITEMS_OUT)
            boundary(0, ITEMS_OUT, N_UP0, V_POSTMIX, V_PREFFN)
            ffn(0)
            boundary(1, ITEMS_DOWN, N_U, V_POSTFFN, V_PREMIX + KT)
            dve.scalar_tensor_tensor(out=lamc[:, 0, :], in0=vt[:, V_LAM:V_LAM + KT], scalar=-1.0,
                                     in1=vt[:, V_LAM:V_LAM + KT], op0=ALU.mult, op1=ALU.max).then_inc(lam_v, 1)
            dve.wait_ge(lam_a, 1)
            dve.tensor_scalar(lamc[:, 2, :], lamc[:, 1, :], 1.0, None, ALU.add).then_inc(lam_v, 1)
            dve.memset(upad[:, :, 0:CONV - 1], 0.0).then_inc(upz, 1)
            dve.wait_ge(upz, 1)

            def convolve(k, ready):
                dve.wait_ge(u_out, ready)
                for j in range(CONV - 1):
                    if j:
                        dve.wait_ge(conv, 3 * k + j)
                    w = V_CONVW + j * KT + k
                    dve.scalar_tensor_tensor(out=uc[:, k, :], in0=upad[:, k, j:j + S], scalar=vt[:, w:w + 1],
                                             in1=uc[:, k, :], op0=ALU.mult, op1=ALU.add).then_inc(conv, 1)

            for k in range(KT):
                convolve(k, 3 if k < 2 else 4 if k < 4 else k + 1)
            dve.wait_ge(lam_a, 2)
            dve.reciprocal(lamc[:, 4, :], lamc[:, 2, :])
            dve.scalar_tensor_tensor(out=lamc[:, 5, :], in0=lamc[:, 2, :], scalar=-1.0, in1=lamc[:, 1, :],
                                     op0=ALU.add, op1=ALU.subtract).then_inc(upz, 1)
            dve.wait_ge(upz, 2)
            dve.tensor_tensor(lamc[:, 4, :], lamc[:, 4, :], lamc[:, 5, :], ALU.mult).then_inc(upz, 1)
            dve.wait_ge(upz, 3)
            dve.tensor_tensor(lamc[:, 3, :], lamc[:, 4, :], lamc[:, 3, :], ALU.subtract).then_inc(upz, 1)
            dve.wait_ge(upz, 4)
            dve.scalar_tensor_tensor(out=lamc[:, 2, :], in0=vt[:, V_LAM:V_LAM + KT], scalar=0.0, in1=lamc[:, 3, :],
                                     op0=ALU.min, op1=ALU.add).then_inc(upz, 1)
            dve.wait_ge(upz, 5)
            dve.tensor_scalar(lamc[:, 4, :], lamc[:, 2, :], LRU_C, None, ALU.mult)
            dve.tensor_scalar(lamc[:, 5, :], lamc[:, 2, :], -LRU_C, None, ALU.mult).then_inc(lam_v, 1)
            for m in range(KT):
                dve.wait_ge(ga_out, 2 * m + 2)
                dve.wait_ge(ul, m + 1)
                dve.tensor_tensor(uc[:, m, :], uc[:, m, :], sgi[:, m % 2, :], ALU.mult).then_inc(iu, 1)
            for m in range(KT):
                dve.wait_ge(ab, m + 1)
                dve.tensor_tensor(y[:, m, :], la[:, m, :], la[:, m, :], ALU.mult).then_inc(rsq, 1)
                dve.wait_ge(rsq, m + 1)
                dve.scalar_tensor_tensor(out=lt[:, m, :], in0=y[:, m, :], scalar=1.0, in1=lt[:, m, :],
                                         op0=ALU.add, op1=ALU.mult).then_inc(one_a2, 1)
            for m in range(KT):
                dve.wait_ge(roots, m // 4 + 1)
                dve.wait_ge(iu, m + 1)
                dve.tensor_tensor(uc[:, m, :], lt[:, m, :], uc[:, m, :], ALU.mult).then_inc(rsq, 1)
                dve.wait_ge(rsq, KT + 2 * m + 1)
                dve.tensor_tensor_scan(out=y[:, m, :], data0=la[:, m, :], data1=uc[:, m, :], initial=0.0,
                                       op0=ALU.mult, op1=ALU.add).then_inc(rsq, 1)
                dve.wait_ge(rsq, KT + 2 * m + 2)
                dve.wait_ge(gb_out, m + 1)
                dve.tensor_tensor(lt[:, m, :], y[:, m, :], gel[:, m, :], ALU.mult).then_inc(ry, 1)
            clear_acc(2)
            for i in range(4):
                accumulate(2, i, ITEMS_OUT)
            boundary(2, ITEMS_OUT, N_UP1, V_POSTMIX + KT, V_PREFFN + KT)
            ffn(1)
            accumulate(3, 7, ITEMS_DOWN)
            ymeans(3, 0)
            to_diag(4, yroot, 7, ydiag, hrow, 8)
            scale_y(3, 0, V_POSTFFN + KT)
            accumulate(3, 8, ITEMS_DOWN)
            ymeans(3, 1)
            to_diag(6, yroot, 8, ydiag, yrow, 7)

            def result(j):
                dve.wait_ge(oT, 2 * j + 1)
                dve.tensor_copy(outT[:, j, 0:512], bank[RESULT_BANKS[j][0]][:, :]).then_inc(oc_v, 1)

            scale_y(3, 1, V_POSTFFN + KT)
            for j in range(TT):
                result(j)

        @block.tensor
        def _(pe):
            def products(dst, sh, sl, mh, ml, first, last):
                pe.matmul(dst, sh, mh, start=first, stop=False)
                pe.matmul(dst, sh, ml, start=False, stop=False)
                return pe.matmul(dst, sl, mh, start=False, stop=last)

            def split_block(n, mm, dst, t0, nt, ready=None):
                s = n % 2
                for k in range(KT):
                    if ready is not None:
                        ready(k)
                    c = slice(mm * P, (mm + 1) * P)
                    last = products(dst, kview(wh[s])[:, k, c], kview(wl[s])[:, k, c],
                                    xsh[:, k, t0:t0 + nt], xsl[:, k, t0:t0 + nt], k == 0, k == KT - 1)
                return last

            def full_block(n, banks, done, waits=None, ready=None):
                pe.wait_ge(lo_done, n + 1)
                for mm in range(2):
                    if waits is not None:
                        waits(mm)
                    last = split_block(n, mm, banks[mm], 0, S, ready if mm == 0 else None)
                    last.then_inc(w_used if mm else done, 1)

            def sum_y(bd, q, accs):
                pe.wait_ge(item_acc, accs)
                for j in range(2):
                    t = q * HALF + j * P
                    last = pe.matmul(SUM[q][:, j:j + 1], accy[:, t:t + P], ones[:, 0:1], start=(j == 0),
                                     stop=(j == 1), skip_group_check=True)
                last.then_inc(ysum, 1)

            def row_y(bd, q):
                pe.wait_ge(ydiag, 2 * bd + q + 1)
                pe.matmul(ROW[q][:, 0:HALF], ones[:, :], diag[:, :, :].rearrange("p a t -> p (a t)"),
                          start=True, stop=True).then_inc(yrow, 1)

            def sum_h(bd, q):
                for k in range(KT):
                    pe.wait_ge(h_sq, 16 * bd + 8 * q + k + 1)
                    for j in range(2):
                        last = pe.matmul(SUM[q][:, 4 + j:5 + j], hsq[:, k, j * P:(j + 1) * P], ones[:, 0:1],
                                         start=(k == 0 and j == 0), stop=(k == KT - 1), skip_group_check=True)
                last.then_inc(hsum, 1)

            def row_h(p, q):
                pe.wait_ge(hdiag, 2 * p + q + 1)
                pe.matmul(ROW[q][:, HALF:S], ones[:, :], diag[:, :, :].rearrange("p a t -> p (a t)"),
                          start=True, stop=True).then_inc(hrow, 1)

            def xs_ready(p, q):
                def ready(k):
                    if k % 2 == 0:
                        pe.wait_ge(xl_v, 8 * p + 4 * q + k // 2 + 1)
                    else:
                        pe.wait_ge(xl_p, 8 * p + 4 * q + k // 2 + 1)
                return ready

            def first_two(n, p, done, bd=None):
                dn = done if isinstance(done, tuple) else (done, done)
                for b in range(2):
                    pe.wait_ge(lo_done, n + b + 1)
                    for mm in range(2):
                        last = split_block(n + b, mm, M[b][:, mm * HALF:(mm + 1) * HALF], 0, HALF,
                                           xs_ready(p, 0) if b == 0 and mm == 0 else None)
                        if bd is not None and b == 0 and mm == 0:
                            row_y(bd, 1)
                    last.then_inc(dn[b], 1)
                if bd is not None:
                    sum_h(bd, 1)
                    row_h(p, 1)
                for b in range(2):
                    for mm in range(2):
                        last = split_block(n + b, mm, M[2 + b][:, mm * HALF:(mm + 1) * HALF], HALF, HALF,
                                           xs_ready(p, 1) if b == 0 and mm == 0 else None)
                    last.then_inc(w_used, 1)

            accs_after = {0: (ITEMS_OUT, 6, 8), 1: (ITEMS_DOWN, 8, 9), 2: (ITEMS_OUT, 6, 8), 3: (ITEMS_DOWN, 8, 9)}

            def sum_y_b(bd):
                lst, _, nb = accs_after[bd]
                sum_y(bd, 1, accs_before[bd] + 1 + acc_ops(lst[:nb]))

            def sum_y_a(bd):
                lst, na, _ = accs_after[bd]
                sum_y(bd, 0, accs_before[bd] + 1 + acc_ops(lst[:na]))

            def out_proj(bd, n, ready):
                base = items_before[bd]
                full_block(n, [M[0], M[1]], item_done, ready=ready)
                full_block(n + 1, [M[2], M[3]], item_done)
                for b in range(2):
                    pe.wait_ge(lo_done, n + 3 + b)
                    pe.wait_ge(item_out, base + b + 1)
                    for mm in range(2):
                        last = split_block(n + 2 + b, mm, M[b][:, mm * HALF:(mm + 1) * HALF], 0, HALF)
                    last.then_inc(item_done, 1)
                for b in range(2):
                    pe.wait_ge(item_out, base + b + 3)
                    for mm in range(2):
                        last = split_block(n + 2 + b, mm, M[2 + b][:, mm * HALF:(mm + 1) * HALF], HALF, HALF)
                        if b == 0 and mm == 0:
                            sum_y_a(bd)
                    last.then_inc(w_used, 1)
                    if b == 0:
                        row_y(bd, 0)
                sum_h(bd, 0)
                sum_y_b(bd)
                row_h(bd + 1, 0)

            def down_part(s, part, dst, t0, nt):
                for k in range(DKT):
                    kk = part * DKT + k
                    last = products(dst, kview(wh[s], P)[:, k, :], kview(wl[s], P)[:, k, :],
                                    acth[:, kk, t0:t0 + nt], actl[:, kk, t0:t0 + nt],
                                    kk == 0, kk == FT - 1)
                return last

            def ffn(layer, nu, nd):
                base = 22 * layer
                bd = 2 * layer + 1
                first_two(nu, bd, (gate_done, up_done), bd - 1)
                with pe.Fori(1, FP) as j:
                    for b, done in ((0, gate_done), (1, up_done)):
                        pe.wait_ge(lo_done, nu + 1 + b + 2 * j)
                        for mm in range(2):
                            if b == 0:
                                pe.wait_ge(silu, base + 2 * j - 1 + mm)
                                if mm:
                                    pe.wait_ge(prod_done, base + 2 * j - 1)
                            else:
                                pe.wait_ge(prod_done, base + 2 * j - 1 + mm)
                            for k in range(KT):
                                c = slice(mm * P, (mm + 1) * P)
                                last = products(M[2 * b + mm][:, :], kview(wh[b])[:, k, c], kview(wl[b])[:, k, c],
                                                xsh[:, k, :], xsl[:, k, :], k == 0, k == KT - 1)
                            last.then_inc(w_used if mm else done, 1)
                pe.wait_ge(silu, base + 22)
                pe.wait_ge(act_l, base + 20)
                it = items_before[bd]
                with pe.Fori(0, 3) as i:
                    for t in range(2):
                        pe.wait_ge(item_out, it - 1 + t + 2 * i)
                        for part in range(2):
                            pe.wait_ge(lo_done, nd + 1 + part + 2 * t + 4 * i)
                            if part:
                                pe.wait_ge(act_l, base + 22)
                            down_part(part, part, M[t][:, :], 0, S).then_inc(w_used, 1)
                pe.wait_ge(item_out, it + 5)
                for part in range(2):
                    pe.wait_ge(lo_done, nd + 13 + part)
                    down_part(part, part, M[0][:, :], 0, S).then_inc(w_used, 1)
                pe.wait_ge(item_out, it + 6)
                for part in range(2):
                    pe.wait_ge(lo_done, nd + 15 + part)
                    last = down_part(part, part, M[1][:, 0:HALF], 0, HALF)
                last.then_inc(item_done, 1)
                pe.wait_ge(prod_done, base + 22)
                down_part(0, 0, M[2][:, 0:HALF], HALF, HALF).then_inc(w_used, 1)
                sum_y_a(bd)
                down_part(1, 1, M[2][:, 0:HALF], HALF, HALF).then_inc(w_used, 1)
                row_y(bd, 0)
                if layer == 0:
                    sum_h(bd, 0)
                    sum_y_b(bd)
                    row_h(bd + 1, 0)

            pe.wait_ge(vec_in, 160)
            pe.wait_ge(consts, 9)
            pe.transpose(ROW[0][:, 0:P], vrow[:, :], ident[:, :])
            pe.transpose(ROW[0][:, P:P + KT], vrow2[:, :], ident[0:KT, 0:KT]).then_inc(vT_done, 1)
            for k in range(KT):
                if k == 6:
                    pe.wait_ge(v_ready, 1)
                for j in range(TT):
                    if k == 0:
                        pe.wait_ge(x_in[j], 16)
                    last = pe.transpose(bank[k][:, j * P:(j + 1) * P], xin[:, j, k * P:(k + 1) * P], ident[:, :])
                last.then_inc(xT_done, 1)
            pe.wait_ge(hx_v, 4)
            row_h(0, 0)
            pe.wait_ge(hx_a, 4)
            row_h(0, 1)
            first_two(N_Q, 0, in_done)
            pe.wait_ge(gw_in, 64)
            for k in range(KT):
                last = pe.matmul(SUM[0][0:40, :], gw[:, k, :], y[:, k, :], start=(k == 0), stop=(k == KT - 1))
            last.then_inc(gates_mm, 1)
            for b in range(2):
                full_block(N_K + b, [M[2 * b], M[2 * b + 1]], in_done,
                           waits=lambda mm, b=b: pe.wait_ge(in_v, 2 * b + mm + 1))
            pe.wait_ge(g_v, 6)
            pe.wait_ge(g_a, 5)
            for j in range(TT):
                pe.transpose(SUM[1][:, 8 * j:8 * j + 8], gc[0:8, j * P:(j + 1) * P], ident[0:8, 0:8])
            for j in range(TT):
                last = pe.transpose(SUM[1][:, 32 + 8 * j:40 + 8 * j], gem[0:8, j * P:(j + 1) * P], ident[0:8, 0:8])
            last.then_inc(gT, 1)
            for b in range(4):
                n = N_V + b
                pe.wait_ge(lo_done, n + 1)
                for bb in range(2):
                    i = 8 + 2 * b + bb
                    pe.wait_ge(in_v, i - 3)
                    for j in range(2):
                        for k in range(KT):
                            t = slice((2 * bb + j) * P, (2 * bb + j + 1) * P)
                            last = products(M[i % 4][:, j * 256:(j + 1) * 256], xsh[:, k, t], xsl[:, k, t],
                                            kview(wh[n % 2])[:, k, :], kview(wl[n % 2])[:, k, :],
                                            k == 0, k == KT - 1)
                    last.then_inc(w_used if bb else in_done, 1)
            for b in range(4):
                full_block(N_O + b, [M[2 * (b % 2)], M[2 * (b % 2) + 1]], in_done,
                           waits=lambda mm, b=b: (pe.wait_ge(in_v, 13 + 2 * b + mm) if b < 2
                                                  else pe.wait_ge(in_a, 2 * b + mm - 3)))
            OFF = [0, 512, 1024, 896]

            def scores(t):
                if t >= 2:
                    pe.wait_ge(decs, t - 1)
                pe.matmul(SUM[t % 2][:, :], sel[:, t, :], z[:, :], start=True, stop=True).then_inc(mrow, 1)
                if t:
                    pe.wait_ge(ptd, t)
                hp = slice(DK * (t % 2), DK * (t % 2) + DK)
                for i in (0, 1, 2, 3):
                    dst = [M[0][:, :], M[1][:, 0:384], M[2][:, 0:256], M[1][:, 384:512]][i]
                    last = pe.matmul(dst, kT[hp, t // 2, i * P:(i + 1) * P], qT[hp, t // 2, i * P:S],
                                     start=True, stop=True)
                last.then_inc(score, 1)

            def outputs(t):
                pe.wait_ge(ptd, t + 1)
                if t:
                    pe.wait_ge(nscd, t)
                for j in range(TT):
                    for i in range(j + 1):
                        o = OFF[i] + (j - i) * P
                        last = pe.matmul(ROW[j // 2][:, (j % 2) * (DV + 1):(j % 2 + 1) * (DV + 1)],
                                         pt[t % 2][:, o:o + P], v[:, i, t, :], start=(i == 0), stop=(i == j))
                last.then_inc(pv, 1)

            def turn(t):
                pe.wait_ge(nscd, t + 1)
                if t:
                    pe.wait_ge(ym, t)
                for j in range(TT):
                    last = pe.transpose(M[3][:, j * P:(j + 1) * P], nsc[t % 2][:, j, :], ident[:, :])
                last.then_inc(nT, 1)

            pe.wait_ge(in_a, 8)
            for t in range(HEADS + 2):
                if t < HEADS:
                    scores(t)
                if 1 <= t <= HEADS:
                    outputs(t - 1)
                if t >= 2:
                    turn(t - 2)
            out_proj(0, N_MLOUT, lambda k: pe.wait_ge(yml, k + 1))
            ffn(0, N_UP0, N_DOWN0)
            first_two(N_U, 2, u_done, 1)
            for b in range(2):
                full_block(N_U + 2 + b, [M[2 * b], M[2 * b + 1]], u_done,
                           waits=lambda mm, b=b: pe.wait_ge(u_out, 2 * b + mm + 1))
            full_block(N_GB0, [M[0], M[1]], gb_done, waits=lambda mm: pe.wait_ge(u_out, 5 + mm))
            pe.wait_ge(lo_done, N_GX + 1)
            pe.wait_ge(u_out, 8)
            for m in range(KT):
                pe.wait_ge(ul, 2 * (m // 2) + 2)
                for g, n in ((0, N_GA), (1, N_GX)):
                    if m >= 2:
                        pe.wait_ge(ga_out, 2 * (m - 2) + g + 1)
                    for k in range(2):
                        kk, c = 2 * (m // 2) + k, slice((m % 2) * P, (m % 2 + 1) * P)
                        last = products(bank[2 + g + 2 * (m % 2)][:, :], kview(wh[n % 2])[:, kk, c],
                                        kview(wl[n % 2])[:, kk, c], uch[:, kk, :], ucl[:, kk, :], k == 0, k == 1)
                    last.then_inc(w_used if m == KT - 1 else ga_done, 1)
            for b in range(3):
                def bank_read(mm, b=b):
                    if b == 1:
                        pe.wait_ge(ga_out, 16)
                    else:
                        pe.wait_ge(gb_out, (1 if b == 0 else 3) + mm)
                full_block(N_GB1 + b, [M[0], M[1]] if b != 1 else [M[2], M[3]], gb_done, waits=bank_read)
            out_ready = lambda k: pe.wait_ge(ryl, k + 1)
            pe.wait_ge(gb_out, 8)
            out_proj(2, N_RGOUT, out_ready)
            ffn(1, N_UP1, N_DOWN1)
            sum_y_b(3)
            for q in range(2):
                if q == 1:
                    row_y(3, 1)
                pe.wait_ge(h_up, 48 + 8 * q + 8)
                for jj in range(2):
                    j = 2 * q + jj
                    for b in range(2):
                        dst = RESULT_BANKS[j][b]
                        if j == 3:
                            pe.wait_ge(oc_v if b == 0 else oc_a, 1)
                        if j == 2:
                            pe.wait_ge(item_out, items_before[3] + 9)
                        for k in range(4):
                            last = pe.transpose(bank[dst][:, k * P:(k + 1) * P],
                                                h[:, 4 * b + k, j * P:(j + 1) * P], ident[:, :])
                        last.then_inc(oT, 1)


NAMES = ["x", "ml_w_in", "ml_b_if", "ml_head_norm", "ml_w_out", "lru_w_in", "lru_conv_w", "lru_conv_b",
         "lru_w_gate_a", "lru_b_gate_a", "lru_w_gate_x", "lru_b_gate_x", "lru_lambda", "lru_w_out",
         "norm_pre_mix", "norm_post_mix", "norm_pre_ffn", "norm_post_ffn",
         "ffn_w_gate", "ffn_w_up", "ffn_w_down"]


def kernel(**inputs):
    import numpy as _np
    import concourse.bacc as _bacc
    from concourse.bass_utils import run_bass_kernel_spmd as _run

    nc = _bacc.Bacc("TRN2", target_bir_lowering=False, num_devices=1, dynamic_dma_scratch_size=1024)
    arrays, aps = {}, {}
    for name in NAMES:
        arr = _np.ascontiguousarray(inputs[name])
        arrays[f"in_{name}"] = arr
        aps[name] = nc.dram_tensor(f"in_{name}", arr.shape, F32, kind="ExternalInput").ap()
    out = nc.dram_tensor("out_0", (1, S, D), F32, kind="ExternalOutput").ap()
    build(nc, aps, out)
    r = _run(nc, [arrays], core_ids=[0])
    return r.results[0]["out_0"]
```

```python
from contextlib import ExitStack

import numpy as np
import concourse.bass as bass
import concourse.mybir as mybir

F32 = mybir.dt.float32
F32R = mybir.dt.float32r
ALU = mybir.AluOpType
ACT = mybir.ActivationFunctionType

P = 128
D = 1024
S = 512
KT = D // P
TT = S // P
HALF = S // 2
HEADS = 8
DK = 64
DV = 128
QK = HEADS * DK
VW = HEADS * DV
GATE_CAP = 15.0
LRU_C = 8.0
CONV = 4
FF = 2816
FT = FF // P
EPS = 1e-6
NEG = -1e30
BC = 256
FP = FF // BC
DKT = FT // 2

N_Q, N_K, N_V, N_O = 0, 2, 4, 8
N_MLOUT = 12
N_UP0 = 16
N_DOWN0 = N_UP0 + 2 * FP
N_U = N_DOWN0 + 2 * KT
N_GB0 = N_U + 4
N_GA, N_GX = N_GB0 + 1, N_GB0 + 2
N_GB1 = N_GX + 1
N_RGOUT = N_GB1 + 3
N_UP1 = N_RGOUT + 4
N_DOWN1 = N_UP1 + 2 * FP
N_END = N_DOWN1 + 2 * KT

V_PREMIX, V_POSTMIX, V_PREFFN, V_POSTFFN, V_HEAD, V_CONVW, V_CONVB, V_LAM, V_BA = (
    0, 16, 32, 48, 64, 72, 104, 112, 120)

ITEMS_OUT = [(0, 0, 1, 0, S), (1, 1, 1, 0, S), (2, 2, 1, 0, S), (3, 3, 1, 0, S),
             (0, 4, 2, 0, HALF), (1, 6, 2, 0, HALF), (2, 4, 2, HALF, HALF), (3, 6, 2, HALF, HALF)]
ITEMS_DOWN = [(m % 2, m, 1, 0, S) for m in range(7)] + [(1, 7, 1, 0, HALF), (2, 7, 1, HALF, HALF)]

RESULT_BANKS = [(0, 3), (4, 6), (1, 2), (0, 3)]


def build(nc, a, out):
    ctx = ExitStack()
    with ctx:
        free = [-(-nc.sbuf_base // 64) * 64]

        def sb(name, shape, dt=F32):
            size = int(np.prod(shape[1:])) * 4
            t = nc.alloc_sbuf_tensor_at(name, shape, dt, offset=free[0])
            free[0] += -(-size // 32) * 32
            return t

        vt = sb("vt", [P, P])
        vx = sb("vx", [P, KT])
        ident = sb("ident", [P, P])
        ones = sb("ones", [P, P])
        small = sb("small", [P, 32])
        expo = sb("expo", [P, 8])
        bif = sb("bif", [P, 2])
        h = sb("h", [P, KT, S])
        xs_at = free[0]
        xsh = sb("xsh", [P, KT, S], F32R)
        xsl = sb("xsl", [P, KT, S], F32R)
        y = sb("y", [P, KT, S])
        raw = [sb(f"raw{s}", [P, 2048]) for s in range(2)]
        wh = [sb(f"wh{s}", [P, 2048], F32R) for s in range(2)]
        wl = [sb(f"wl{s}", [P, 2048], F32R) for s in range(2)]
        sqy = sb("sqy", [P, S])
        accy = sb("accy", [P, S])
        hsq = sb("hsq", [P, KT, HALF])
        diag = sb("diag", [P, 2, P])
        sil = sb("sil", [P, 2, S])
        prod = sb("prod", [P, 2, S])
        region = free[0]
        acth = sb("acth", [P, FT, S], F32R)
        actl = sb("actl", [P, FT, S], F32R)
        assert free[0] <= nc.sbuf_usable_end, (free[0], nc.sbuf_usable_end)
        end = free[0]
        free[0] = region
        qT = sb("qT", [P, QK // P, S])
        kT = sb("kT", [P, HEADS, S])
        v = sb("v", [P, TT, HEADS, DV + 1])
        sigo = sb("sigo", [P, KT, S])
        z = sb("z", [HEADS, S])
        ct = sb("ct", [P, TT, HEADS])
        emt = sb("emt", [P, TT, HEADS])
        mask = sb("mask", [P, P])
        sel = sb("sel", [HEADS, HEADS, P])
        early = free[0]
        masked = [sb(f"masked{i}", [P, TT, P]) for i in range(2)]
        dec = sb("dec", [P, 1280])
        pt = [sb(f"pt{i}", [P, 1280]) for i in range(2)]
        nsc = [sb(f"nsc{i}", [P, TT, DV]) for i in range(2)]
        den = sb("den", [P, 2, 4, TT])
        assert free[0] <= end, (free[0], end)
        free[0] = early
        xin = sb("xin", [P, TT, D])
        vrow = sb("vrow", [P, P])
        vrow2 = sb("vrow2", [KT, P])
        gw = sb("gw", [P, KT, 40])
        assert free[0] <= end
        free[0] = early
        ge, gy, gl_, gd, gi, gli, glf, gB, gm, gc, gem, gz = (
            sb(f"g{i}", [40, S]) for i in range(12))
        tg = sil[0:40, 0, :]
        assert free[0] <= end
        free[0] = region
        upad = sb("upad", [P, KT, CONV - 1 + S + 1])
        uc = sb("uc", [P, KT, S])
        at_uch = free[0]
        uch = sb("uch", [P, KT, S], F32R)
        ucl = sb("ucl", [P, KT, S], F32R)
        gel = sb("gel", [P, KT, S])
        sgi = sb("sgi", [P, 2, S])
        lamc = sb("lamc", [P, 6, KT])
        assert free[0] <= end, (free[0], end)
        free[0] = at_uch
        la = sb("la", [P, KT, S])
        lt = sb("lt", [P, KT, S])
        free[0] = xs_at
        outT = sb("outT", [P, TT, D])

        bank = [ctx.enter_context(nc.psum_tensor(f"bank{i}", [P, 512], F32))[:, :] for i in range(8)]
        M = bank[:4]
        SUM = bank[4:6]
        ROW = bank[6:8]

        def sem(name):
            return ctx.enter_context(nc.semaphore(name))

        x_in = [sem(f"x_in{j}") for j in range(TT)]
        vec_in = sem("vec_in")
        gw_in = sem("gw_in")
        stored = sem("stored")
        raw_in = [sem("raw_in0"), sem("raw_in1")]
        hi_done = sem("hi_done")
        lo_done = sem("lo_done")
        w_used = sem("w_used")
        consts = sem("consts")
        cz = sem("cz")
        vT_done = sem("vT_done")
        v_ready = sem("v_ready")
        xT_done = sem("xT_done")
        hx_v = sem("hx_v")
        hx_a = sem("hx_a")
        xsum = sem("xsum")
        item_done = sem("item_done")
        item_out = sem("item_out")
        item_acc = sem("item_acc")
        ysum = sem("ysum")
        ymean = sem("ymean")
        yroot = sem("yroot")
        ydiag = sem("ydiag")
        yrow = sem("yrow")
        yscaled = sem("yscaled")
        h_up = sem("h_up")
        h_sq = sem("h_sq")
        hsum = sem("hsum")
        hmean = sem("hmean")
        hroot = sem("hroot")
        hdiag = sem("hdiag")
        hrow = sem("hrow")
        xf = sem("xf")
        xh = sem("xh")
        xl_v = sem("xl_v")
        xl_p = sem("xl_p")
        gate_done = sem("gate_done")
        up_done = sem("up_done")
        silu = sem("silu")
        prod_done = sem("prod_done")
        act_h = sem("act_h")
        act_l = sem("act_l")
        in_done = sem("in_done")
        in_v = sem("in_v")
        in_a = sem("in_a")
        gates_mm = sem("gates_mm")
        g_a = sem("g_a")
        g_v = sem("g_v")
        gT = sem("gT")
        gT_out = sem("gT_out")
        mrow = sem("mrow")
        msk = sem("msk")
        decs = sem("decs")
        score = sem("score")
        ptd = sem("ptd")
        pv = sem("pv")
        nsq = sem("nsq")
        dens = sem("dens")
        mroot = sem("mroot")
        nscd = sem("nscd")
        nT = sem("nT")
        ym = sem("ym")
        ymh = sem("ymh")
        yml_v = sem("yml_v")
        yml_p = sem("yml_p")
        kz = sem("kz")
        u_done = sem("u_done")
        u_out = sem("u_out")
        upz = sem("upz")
        conv = sem("conv")
        uh = sem("uh")
        ul = sem("ul")
        gb_done = sem("gb_done")
        gb_out = sem("gb_out")
        ga_done = sem("ga_done")
        ga_out = sem("ga_out")
        iu = sem("iu")
        ab = sem("ab")
        rsq = sem("rsq")
        one_a2 = sem("one_a2")
        roots = sem("roots")
        den_step = sem("den_step")
        ry = sem("ry")
        ryh = sem("ryh")
        ryl_v = sem("ryl_v")
        ryl_p = sem("ryl_p")
        lam_a = sem("lam_a")
        lam_v = sem("lam_v")
        oT = sem("oT")
        oc_v = sem("oc_v")
        oc_a = sem("oc_a")

        block = ctx.enter_context(nc.Block())

        def kview(t, c=BC):
            n = KT if c == BC else DKT
            return t[:, 0:n * c].rearrange("p (k c) -> p k c", c=c)

        def rows(w):
            return w.rearrange("(k p) c -> p k c", p=P)

        w_in = rows(a["ml_w_in"][0])
        w_mlout = rows(a["ml_w_out"][0])
        w_lru = rows(a["lru_w_in"][0])
        w_rgout = rows(a["lru_w_out"][0])
        w_ga = rows(a["lru_w_gate_a"][0].rearrange("n c d -> (n c) d"))
        w_gx = rows(a["lru_w_gate_x"][0].rearrange("n c d -> (n c) d"))
        items_before = [0, 8, 17, 25]
        done_before = [0, 4, 5, 9]
        first_block = [N_MLOUT, N_DOWN0, N_RGOUT, N_DOWN1]

        def item_ready(bd, i):
            n, base = first_block[bd], done_before[bd]
            if bd % 2 == 0:
                return [(item_done, base + 1), (w_used, n + 1), (item_done, base + 2), (w_used, n + 2),
                        (item_done, base + 3), (item_done, base + 4), (w_used, n + 3), (w_used, n + 4)][i]
            return (item_done, base + 1) if i == 7 else (w_used, n + 2 * i + 2) if i < 7 else (w_used, n + 16)

        def in_ready(i):
            if i < 2:
                return in_done, i + 1
            if i < 4:
                return w_used, i - 1
            b = (i - 4) // 2
            return (in_done, 3 + b) if i % 2 == 0 else (w_used, N_K + b + 1)

        def u_ready(i):
            if i < 2:
                return u_done, i + 1
            if i < 4:
                return w_used, N_U + i - 1
            b = (i - 4) // 2
            return (u_done, 3 + b) if i % 2 == 0 else (w_used, N_U + 3 + b)

        def gb_ready(g, m):
            return (gb_done, g + 1) if m == 0 else (w_used, N_GB0 + 1 if g == 0 else N_GB1 + g)

        def ga_ready(m, g):
            return (ga_done, (KT - 1) * g + m + 1) if m < KT - 1 else (w_used, N_GA + g + 1)

        def gate_ready(layer, b, j, m):
            nu = (N_UP0, N_UP1)[layer]
            if m == 0:
                return (gate_done, up_done)[b], FP * layer + 1 + j
            return w_used, nu + 2 * j + b + 1
        accs_before = [0, 13, 23, 36]

        def acc_ops(items):
            return sum(it[2] for it in items)

        @block.sync
        def _(sp):
            def load(n, src, c=BC, slot=None, wait=None, landed=None):
                s = n % 2 if slot is None else slot
                if wait is None:
                    wait = n - 1 if n >= 2 else None
                if wait is not None:
                    sp.wait_ge(lo_done, wait)
                sp.dma_start(kview(raw[s], c), src).then_inc(raw_in[s], 16)

            x = a["x"][0].rearrange("(j p) d -> p j d", p=P)
            for j in range(TT):
                sp.dma_start(xin[:, j, :], x[:, j, :]).then_inc(x_in[j], 16)
            load(0, w_in[:, :, 0:BC])

            def vec(ap, row, n):
                sp.dma_start(vrow[row:row + n, :], ap).then_inc(vec_in, 16)

            vec(a["norm_pre_mix"].rearrange("l (k p) -> (l k) p", p=P), V_PREMIX, 16)
            vec(a["norm_post_mix"].rearrange("l (k p) -> (l k) p", p=P), V_POSTMIX, 16)
            vec(a["norm_pre_ffn"].rearrange("l (k p) -> (l k) p", p=P), V_PREFFN, 16)
            vec(a["norm_post_ffn"].rearrange("l (k p) -> (l k) p", p=P), V_POSTFFN, 16)
            vec(a["ml_head_norm"].rearrange("l (k p) -> (l k) p", p=P), V_HEAD, 8)
            vec(a["lru_conv_w"].rearrange("l j (k p) -> (l j k) p", p=P), V_CONVW, 32)
            vec(a["lru_conv_b"].rearrange("l (k p) -> (l k) p", p=P), V_CONVB, 8)
            vec(a["lru_lambda"].rearrange("l (k p) -> (l k) p", p=P), V_LAM, 8)
            vec(a["lru_b_gate_a"].rearrange("l (k p) -> (l k) p", p=P), V_BA, 8)
            sp.dma_start(vrow2[:, :], a["lru_b_gate_x"].rearrange("l (k p) -> (l k) p", p=P)).then_inc(vec_in, 16)
            load(1, w_in[:, :, BC:2 * BC])
            sp.wait_ge(cz, 2)
            gcol = 2 * QK + 2 * VW
            sp.dma_start(gw[:, :, 0:8], w_in[:, :, gcol:gcol + 8]).then_inc(gw_in, 16)
            sp.dma_start(gw[:, :, 32:40], w_in[:, :, gcol + 8:gcol + 16]).then_inc(gw_in, 16)
            sp.dma_start(bif[0:8, 0:1], a["ml_b_if"][0, 0:8].rearrange("(p o) -> p o", o=1)).then_inc(gw_in, 16)
            sp.dma_start(bif[32:40, 0:1], a["ml_b_if"][0, 8:16].rearrange("(p o) -> p o", o=1)).then_inc(gw_in, 16)
            for n in range(2, 12):
                load(n, w_in[:, :, n * BC:(n + 1) * BC])
            for n in range(4):
                load(N_MLOUT + n, w_mlout[:, :, n * BC:(n + 1) * BC])

            def ffn(layer, nu, nd):
                wg, wu = rows(a["ffn_w_gate"][layer]), rows(a["ffn_w_up"][layer])
                wd = rows(a["ffn_w_down"][layer])
                with sp.Fori(0, FP) as j:
                    load(0, wg[:, :, bass.ds(j * BC, BC)], slot=0, wait=nu + 2 * j - 1)
                    load(1, wu[:, :, bass.ds(j * BC, BC)], slot=1, wait=nu + 2 * j)
                with sp.Fori(0, KT) as m:
                    load(0, wd[:, 0:DKT, bass.ds(m * P, P)], c=P, slot=0, wait=nd + 2 * m - 1)
                    load(1, wd[:, DKT:FT, bass.ds(m * P, P)], c=P, slot=1, wait=nd + 2 * m)

            ffn(0, N_UP0, N_DOWN0)
            for n in range(4):
                load(N_U + n, w_lru[:, :, D + n * BC:D + (n + 1) * BC])
            load(N_GB0, w_lru[:, :, 0:BC])
            load(N_GA, w_ga)
            load(N_GX, w_gx)
            for n in range(3):
                load(N_GB1 + n, w_lru[:, :, (n + 1) * BC:(n + 2) * BC])
            for n in range(4):
                load(N_RGOUT + n, w_rgout[:, :, n * BC:(n + 1) * BC])
            ffn(1, N_UP1, N_DOWN1)
            o = out[0].rearrange("(j p) d -> p j d", p=P)
            for j in range(TT):
                sp.wait_ge(oc_v, j + 1)
                sp.wait_ge(oc_a, j + 1)
                sp.dma_start(o[:, j, :], outT[:, j, :]).then_inc(stored, 16)
            sp.wait_ge(stored, 16 * TT)

        @block.scalar
        def _(act):
            def hi(n, c=2048, slot=None, landed=None, used=None):
                s = n % 2 if slot is None else slot
                act.wait_ge(raw_in[s], 16 * (n // 2 + 1) if landed is None else landed)
                if used is None:
                    used = n - 1 if n >= 2 else None
                if used is not None:
                    act.wait_ge(w_used, used)
                act.activation(wh[s][:, 0:c], raw[s][:, 0:c], ACT.Copy).then_inc(hi_done, 1)

            def item(bd, i, bk, m0, nm, t0, nt, acc):
                act.wait_ge(*item_ready(bd, i))
                src = bank[bk][:, 0:nm * nt].rearrange("p (m t) -> p m t", m=nm)
                sq = sqy[:, 0:nm * nt].rearrange("p (m t) -> p m t", m=nm)
                act.activation(y[:, m0, t0:t0 + nt] if nm == 1 else y[:, m0:m0 + nm, t0:t0 + nt],
                               bank[bk][:, 0:nt] if nm == 1 else src, ACT.Copy)
                act.wait_ge(item_acc, acc)
                act.activation(sqy[:, 0:nt] if nm == 1 else sq,
                               bank[bk][:, 0:nt] if nm == 1 else src, ACT.Square).then_inc(item_out, 1)

            def items(bd, which, lst):
                for i in which:
                    item(bd, i, *lst[i],
                         accs_before[bd] + 1 + acc_ops(lst[:i]))

            def squares_h(bd, q):
                if q == 1 or bd:
                    act.wait_ge(hsum, 2 * bd + q + 0)
                for k in range(KT):
                    act.wait_ge(h_up, 16 * bd + 8 * q + k + 1)
                    act.activation(hsq[:, k, :], h[:, k, q * HALF:(q + 1) * HALF],
                                   ACT.Square).then_inc(h_sq, 1)

            def xs_hi(p, q):
                for k in range(KT):
                    act.wait_ge(xf, 16 * p + 8 * q + k + 1)
                    act.activation(xsh[:, k, q * HALF:(q + 1) * HALF], y[:, k, q * HALF:(q + 1) * HALF],
                                   ACT.Copy).then_inc(xh, 1)

            def ffn(layer, nu, nd):
                base = 22 * layer
                for q in range(2):
                    act.wait_ge(*gate_ready(layer, 0, 0, q))
                    if layer or q:
                        act.wait_ge(prod_done, base + q)
                    act.activation(sil[:, :, 0:HALF], bank[2 * q][:, :].rearrange("p (m t) -> p m t", m=2),
                                   ACT.Silu).then_inc(silu, 1)
                with act.Fori(1, FP) as j:
                    hi(0, slot=0, landed=16 * (nu // 2 + 1) + 16 * j, used=nu - 1 + 2 * j)
                    hi(1, slot=1, landed=16 * (nu // 2 + 1) + 16 * j, used=nu + 2 * j)
                    for m in range(2):
                        act.wait_ge(*gate_ready(layer, 0, j, m))
                        act.wait_ge(prod_done, base + 2 * j)
                        act.activation(sil[:, m, :], bank[m][:, :], ACT.Silu).then_inc(silu, 1)
                c = DKT * P
                hi(nd, c)
                hi(nd + 1, c)
                bd = 2 * layer + 1
                with act.Fori(0, 3) as i:
                    for t in range(2):
                        hi(0, c, slot=0, landed=16 * ((nd + 2) // 2 + 1 + t) + 32 * i, used=nd + 1 + 2 * t + 4 * i)
                        hi(1, c, slot=1, landed=16 * ((nd + 2) // 2 + 1 + t) + 32 * i, used=nd + 2 + 2 * t + 4 * i)
                        down_item(bd, i, t)
                hi(nd + 14, c)
                hi(nd + 15, c)
                items(bd, [6], ITEMS_DOWN)

            def down_item(bd, i, t):
                act.wait_ge(w_used, first_block[bd] + 4 * i + 2 * t + 2)
                act.activation(y[:, bass.ds(2 * i + t, 1), :].rearrange("p a t -> p (a t)"), bank[t][:, :], ACT.Copy)
                act.wait_ge(item_acc, accs_before[bd] + 1 + 2 * i + t)
                act.activation(sqy[:, :], bank[t][:, :], ACT.Square).then_inc(item_out, 1)

            def boundary(bd, lst, n):
                a_items = [i for i in range(len(lst)) if lst[i][4] == HALF and lst[i][3] == 0]
                b_items = [i for i in range(len(lst)) if lst[i][4] == HALF and lst[i][3] == HALF]
                items(bd, a_items + b_items[:-1], lst)
                hi(n)
                squares_h(bd, 0)
                items(bd, b_items[-1:], lst)
                hi(n + 1)
                xs_hi(bd + 1, 0)
                squares_h(bd, 1)
                xs_hi(bd + 1, 1)

            for j in range(TT):
                act.wait_ge(x_in[j], 16)
                act.activation(y[:, 2 * j:2 * j + 2, :], xin[:, j, :].rearrange("p (a t) -> p a t", a=2),
                               ACT.Square, accum_out=small[:, 16 + j:17 + j]).then_inc(xsum, 1)
            hi(0)
            for k in range(1, KT, 2):
                act.wait_ge(xT_done, k + 1)
                act.activation(h[:, k, :], bank[k][:, :], ACT.Copy).then_inc(hx_a, 1)
            xs_hi(0, 0)
            hi(1)
            xs_hi(0, 1)
            hi(2)
            act.wait_ge(gates_mm, 1)
            act.wait_ge(g_v, 1)
            act.activation(tg[:, :], SUM[0][0:40, :], ACT.Tanh, bias=bif[0:40, 1:2], scale=1.0 / GATE_CAP).then_inc(g_a, 1)
            act.wait_ge(g_a, 1)
            act.activation(ge[0:8, :], tg[32:40, :], ACT.Exp, scale=-GATE_CAP).then_inc(g_a, 1)
            hi(3)
            act.wait_ge(g_v, 2)
            act.activation(gl_[0:8, :], gy[0:8, :], ACT.Ln).then_inc(g_a, 1)
            act.wait_ge(g_a, 3)
            act.activation(gi[0:8, :], gl_[0:8, :], ACT.Exp, scale=-1.0).then_inc(g_a, 1)
            hi(4)
            act.wait_ge(g_v, 5)
            act.activation(gem[0:8, :], gm[0:8, :], ACT.Exp, scale=-2.0).then_inc(g_a, 1)
            for n in range(5, 10):
                hi(n)
            OFF = [0, 512, 1024, 896]

            def decays(t):
                act.wait_ge(msk, t + 1)
                if t:
                    act.wait_ge(ptd, t)
                for i in range(TT):
                    act.activation(dec[:, OFF[i]:OFF[i] + P], masked[t % 2][:, i, :], ACT.Exp,
                                   bias=ct[:, i, t:t + 1])
                for i in range(TT - 1):
                    last = act.activation(dec[:, OFF[i] + P:OFF[i] + S - P * i],
                                          SUM[0][:, (i + 1) * P:S], ACT.Exp, bias=ct[:, i, t:t + 1])
                last.then_inc(decs, 1)

            def square_nums(t):
                act.wait_ge(pv, t + 1)
                if t >= 2:
                    act.wait_ge(dens, t - 1)
                for j in range(TT):
                    src = ROW[j // 2][:, (j % 2) * (DV + 1):(j % 2) * (DV + 1) + DV]
                    last = act.activation(hsq[:, j, 0:DV], src, ACT.Square, scale=float(DV) ** -0.5,
                                          accum_out=den[:, t % 2, 0, j:j + 1])
                last.then_inc(nsq, 1)

            def out_gate(t):
                act.wait_ge(*in_ready(16 + t))
                act.activation(sigo[:, t, :], SUM[1], ACT.Sigmoid).then_inc(in_a, 1)

            def mix_hi(t):
                act.wait_ge(ym, t + 1)
                act.activation(xsh[:, t, :], y[:, t, :], ACT.Copy).then_inc(ymh, 1)

            act.wait_ge(gT_out, 1)
            for t in range(HEADS):
                decays(t)
                if t >= 1:
                    square_nums(t - 1)
                if t in (2, 4, 6):
                    hi(9 + t // 2)
                out_gate(t)
            square_nums(HEADS - 1)
            for t in range(HEADS):
                mix_hi(t)
                if t == HEADS - 3:
                    hi(13)
            items(0, [0, 1], ITEMS_OUT)
            hi(14)
            items(0, [2, 3], ITEMS_OUT)
            hi(15)
            boundary(0, ITEMS_OUT, N_UP0)
            ffn(0, N_UP0, N_DOWN0)
            boundary(1, ITEMS_DOWN, N_U)
            CW3 = V_CONVW + 3 * KT

            def u_evac(k0, nk, t0, nt, bk, i):
                act.wait_ge(*u_ready(i))
                for m in range(nk):
                    k, src = k0 + m, bank[bk][:, m * nt:(m + 1) * nt]
                    act.activation(upad[:, k, CONV - 1 + t0:CONV - 1 + t0 + nt], src, ACT.Copy)
                    last = act.activation(uc[:, k, t0:t0 + nt], src, ACT.Identity,
                                          scale=vt[:, CW3 + k:CW3 + k + 1],
                                          bias=vt[:, V_CONVB + k:V_CONVB + k + 1])
                last.then_inc(u_out, 1)

            def u_hi(k):
                act.wait_ge(conv, 3 * k + 3)
                act.activation(uch[:, k, :], uc[:, k, :], ACT.Copy).then_inc(uh, 1)

            act.wait_ge(lam_v, 1)
            act.activation(lamc[:, 1, :], lamc[:, 0, :], ACT.Exp, scale=-1.0).then_inc(lam_a, 1)
            act.wait_ge(lam_v, 2)
            act.activation(lamc[:, 3, :], lamc[:, 2, :], ACT.Ln).then_inc(lam_a, 1)
            u_evac(0, 2, 0, HALF, 0, 0)
            u_evac(2, 2, 0, HALF, 1, 1)
            u_evac(0, 2, HALF, HALF, 2, 2)
            hi(N_U + 2)
            u_evac(2, 2, HALF, HALF, 3, 3)
            hi(N_U + 3)
            for k in range(4):
                u_hi(k)
            for k in (4, 5):
                u_evac(k, 1, 0, S, k - 4, k)
            hi(N_GB0)
            for k in (6, 7):
                u_evac(k, 1, 0, S, k - 4, k)
            hi(N_GA)
            for k in range(4, 8):
                u_hi(k)

            def gelu(g, b0):
                for m in range(2):
                    act.wait_ge(*gb_ready(g, m))
                    act.activation(gel[:, 2 * g + m, :], bank[b0 + m][:, :], ACT.Gelu_apprx_tanh).then_inc(gb_out, 1)

            gelu(0, 0)
            hi(N_GX)
            for m in range(KT):
                act.wait_ge(*ga_ready(m, 0))
                act.activation(y[:, m, :], bank[2 + m % 2][:, :], ACT.Sigmoid,
                               bias=vt[:, V_BA + m:V_BA + m + 1]).then_inc(ga_out, 1)
            hi(N_GB1)
            for m in range(KT):
                act.wait_ge(*ga_ready(m, 1))
                if m >= 2:
                    act.wait_ge(iu, m - 1)
                act.activation(sgi[:, m % 2, :], bank[2 + m % 2][:, :], ACT.Sigmoid,
                               bias=vx[:, m:m + 1]).then_inc(ga_out, 1)
            hi(N_GB1 + 1)
            act.wait_ge(lam_v, 3)
            act.wait_ge(w_used, N_GX + 1)
            act.wait_ge(ga_out, 2 * KT)
            for m in range(KT):
                act.activation(la[:, m, :], y[:, m, :], ACT.Exp, scale=lamc[:, 4, m:m + 1])
                act.activation(lt[:, m, :], y[:, m, :], ACT.Tanh, scale=lamc[:, 5, m:m + 1]).then_inc(ab, 1)
            for m in range(0, KT, 4):
                act.wait_ge(one_a2, m + 4)
                act.activation(lt[:, m:m + 4, :], lt[:, m:m + 4, :], ACT.Sqrt).then_inc(roots, 1)
            for g in range(1, 4):
                gelu(g, [None, 0, 2, 0][g])
                if g == 1:
                    hi(N_GB1 + 2)
                if g == 2:
                    hi(N_RGOUT)
            for m in range(KT):
                act.wait_ge(ry, m + 1)
                act.activation(xsh[:, m, :], lt[:, m, :], ACT.Copy).then_inc(ryh, 1)
            hi(N_RGOUT + 1)
            items(2, [0, 1], ITEMS_OUT)
            hi(N_RGOUT + 2)
            items(2, [2, 3], ITEMS_OUT)
            hi(N_RGOUT + 3)
            boundary(2, ITEMS_OUT, N_UP1)
            ffn(1, N_UP1, N_DOWN1)
            items(3, [7, 8], ITEMS_DOWN)
            for j in range(TT):
                act.wait_ge(oT, 2 * j + 2)
                act.activation(outT[:, j, 512:1024], bank[RESULT_BANKS[j][1]][:, :], ACT.Copy).then_inc(oc_a, 1)

        @block.gpsimd
        def _(pool):
            def root(dst, src, n, mean, mean_at, done):
                pool.wait_ge(mean, mean_at)
                pool.tensor_tensor(dst, src, expo[:, 0:n], ALU.pow).then_inc(done, 1)

            def ysq(bd, q):
                root(small[:, 4 + 2 * q:6 + 2 * q], small[:, 2 * q:2 * q + 2], 2, ymean, 2 * bd + q + 1, yroot)

            def hsqr(p, q):
                root(small[:, 12 + 2 * q:14 + 2 * q], small[:, 8 + 2 * q:10 + 2 * q], 2, hmean, 2 * p + q + 1, hroot)

            def residual(bd, q):
                for k in range(KT):
                    pool.wait_ge(yscaled, 16 * bd + 8 * q + k + 1)
                    t = slice(q * HALF, (q + 1) * HALF)
                    pool.tensor_tensor(h[:, k, t], h[:, k, t], y[:, k, t], ALU.add).then_inc(h_up, 1)

            def mix_lo(hi_at, src, done):
                for k in range(1, KT, 2):
                    pool.wait_ge(hi_at, k + 1)
                    pool.tensor_tensor(xsl[:, k, :], src[:, k, :], xsh[:, k, :].bitcast(F32),
                                       ALU.subtract).then_inc(done, 1)

            def xs_lo(p, q):
                for k in range(1, KT, 2):
                    pool.wait_ge(xh, 16 * p + 8 * q + k + 1)
                    t = slice(q * HALF, (q + 1) * HALF)
                    pool.tensor_tensor(xsl[:, k, t], y[:, k, t], xsh[:, k, t].bitcast(F32),
                                       ALU.subtract).then_inc(xl_p, 1)

            def boundary(bd):
                ysq(bd, 0)
                residual(bd, 0)
                hsqr(bd + 1, 0)
                ysq(bd, 1)
                xs_lo(bd + 1, 0)
                residual(bd, 1)
                hsqr(bd + 1, 1)
                xs_lo(bd + 1, 1)

            pool.memset(gw[:, :, :], 0.0).then_inc(cz, 1)
            pool.memset(bif[:, :], 0.0).then_inc(cz, 1)
            pool.memset(ident[:, :], 0.0).then_inc(consts, 1)
            pool.memset(ones[:, :], 1.0).then_inc(consts, 1)
            pool.memset(expo[:, :], -0.5).then_inc(consts, 1)
            pool.memset(mask[:, :], 0.0).then_inc(consts, 1)
            pool.memset(sel[:, :, :], 0.0).then_inc(consts, 1)
            pool.memset(v[:, :, :, DV:DV + 1], 1.0).then_inc(consts, 1)
            pool.wait_ge(consts, 6)
            pool.affine_select(out=ident[:, :], in_=ident[:, :], compare_op=ALU.not_equal, fill=1.0, base=0,
                               pattern=[[-1, P]], channel_multiplier=1).then_inc(consts, 1)
            pool.affine_select(out=mask[:, :], in_=mask[:, :], compare_op=ALU.is_ge, fill=NEG, base=0,
                               pattern=[[1, P]], channel_multiplier=-1).then_inc(consts, 1)
            pool.affine_select(out=sel[:, :, :], in_=sel[:, :, :], compare_op=ALU.not_equal, fill=1.0, base=0,
                               pattern=[[-1, HEADS], [0, P]], channel_multiplier=1).then_inc(consts, 1)
            hsqr(0, 0)
            hsqr(0, 1)
            xs_lo(0, 0)
            xs_lo(0, 1)
            pool.wait_ge(xl_p, 8)
            for e in range(2):
                if e:
                    pool.wait_ge(kz, 1)
                o = DK * (1 - e)
                pool.memset(kT[o:o + DK, e:HEADS:2, :], 0.0).then_inc(kz, 1)
            pool.wait_ge(kz, 2)
            for t in range(HEADS):
                pool.wait_ge(dens, t + 1)
                pool.tensor_tensor(den[:, t % 2, 3, :], den[:, t % 2, 2, :], expo[:, 0:TT],
                                   ALU.pow).then_inc(mroot, 1)
            mix_lo(ymh, y, yml_p)
            boundary(0)
            boundary(1)

            def u_lo(k):
                pool.wait_ge(uh, k + 1)
                pool.tensor_tensor(ucl[:, k, :], uc[:, k, :], uch[:, k, :].bitcast(F32), ALU.subtract).then_inc(ul, 1)

            for k in range(KT):
                u_lo(k)
            mix_lo(ryh, lt, ryl_p)
            boundary(2)
            ysq(3, 0)
            residual(3, 0)
            ysq(3, 1)
            residual(3, 1)

        @block.vector
        def _(dve):
            def lo(n, c=2048, slot=None, count=None):
                s = n % 2 if slot is None else slot
                dve.wait_ge(hi_done, n + 1 if count is None else count)
                dve.tensor_tensor(wl[s][:, 0:c], raw[s][:, 0:c], wh[s][:, 0:c].bitcast(F32),
                                  ALU.subtract).then_inc(lo_done, 1)

            def mix_lo(k, hi_at, src, done):
                dve.wait_ge(hi_at, k + 1)
                dve.tensor_tensor(xsl[:, k, :], src[:, k, :], xsh[:, k, :].bitcast(F32),
                                  ALU.subtract).then_inc(done, 1)

            def mean(dst, src, done):
                dve.tensor_scalar(dst, src, 1.0 / D, EPS, ALU.mult, ALU.add).then_inc(done, 1)

            def to_diag(col, wait, at, done, free, free_at):
                dve.wait_ge(wait, at)
                if free is not None:
                    dve.wait_ge(free, free_at)
                dve.tensor_scalar(diag[:, 0, :], ident[:, :], small[:, col:col + 1], None, ALU.mult)
                dve.tensor_scalar(diag[:, 1, :], ident[:, :], small[:, col + 1:col + 2], None, ALU.mult).then_inc(done, 1)

            def clear_acc(bd):
                if bd:
                    dve.wait_ge(ysum, 2 * bd)
                dve.memset(accy[:, :], 0.0).then_inc(item_acc, 1)

            def accumulate(bd, i, lst):
                _, m0, nm, t0, nt = lst[i]
                dve.wait_ge(item_out, items_before[bd] + i + 1)
                for m in range(nm):
                    dve.wait_ge(item_acc, accs_before[bd] + 1 + acc_ops(lst[:i]) + m)
                    dve.tensor_tensor(accy[:, t0:t0 + nt], accy[:, t0:t0 + nt], sqy[:, m * nt:(m + 1) * nt],
                                      ALU.add).then_inc(item_acc, 1)

            def ymeans(bd, q):
                dve.wait_ge(ysum, 2 * bd + q + 1)
                mean(small[:, 2 * q:2 * q + 2], SUM[q][:, 0:2], ymean)

            def scale_y(bd, q, g):
                dve.wait_ge(yrow, 2 * bd + q + 1)
                t = slice(q * HALF, (q + 1) * HALF)
                for k in range(KT):
                    dve.scalar_tensor_tensor(out=y[:, k, t], in0=y[:, k, t], scalar=vt[:, g + k:g + k + 1],
                                             in1=ROW[q][:, 0:HALF], op0=ALU.mult, op1=ALU.mult).then_inc(yscaled, 1)

            def hmeans(bd, q):
                dve.wait_ge(hsum, 2 * bd + q + 1)
                mean(small[:, 8 + 2 * q:10 + 2 * q], SUM[q][:, 4:6], hmean)

            def xs_build(p, q, g):
                dve.wait_ge(hrow, 2 * p + q + 1)
                t = slice(q * HALF, (q + 1) * HALF)

                def low(k):
                    dve.wait_ge(xh, 16 * p + 8 * q + k + 1)
                    dve.tensor_tensor(xsl[:, k, t], y[:, k, t], xsh[:, k, t].bitcast(F32),
                                      ALU.subtract).then_inc(xl_v, 1)
                for k in range(KT):
                    dve.scalar_tensor_tensor(out=y[:, k, t], in0=h[:, k, t], scalar=vt[:, g + k:g + k + 1],
                                             in1=ROW[q][:, HALF:S], op0=ALU.mult, op1=ALU.mult).then_inc(xf, 1)
                    if k >= 2 and k % 2 == 0:
                        low(k - 2)
                low(6)

            def boundary(bd, lst, n, g_post, g_pre):
                a_items = [i for i in range(len(lst)) if lst[i][4] == HALF and lst[i][3] == 0]
                b_items = [i for i in range(len(lst)) if lst[i][4] == HALF and lst[i][3] == HALF]
                for i in a_items:
                    accumulate(bd, i, lst)
                ymeans(bd, 0)
                to_diag(4, yroot, 2 * bd + 1, ydiag, hrow, 2 * bd + 2)
                for i in b_items[:-1]:
                    accumulate(bd, i, lst)
                scale_y(bd, 0, g_post)
                lo(n)
                accumulate(bd, b_items[-1], lst)
                hmeans(bd, 0)
                to_diag(12, hroot, 2 * bd + 3, hdiag, yrow, 2 * bd + 1)
                ymeans(bd, 1)
                xs_build(bd + 1, 0, g_pre)
                to_diag(6, yroot, 2 * bd + 2, ydiag, hrow, 2 * bd + 3)
                lo(n + 1)
                scale_y(bd, 1, g_post)
                hmeans(bd, 1)
                to_diag(14, hroot, 2 * bd + 4, hdiag, yrow, 2 * bd + 2)
                xs_build(bd + 1, 1, g_pre)

            def ffn(layer, nu, nd):
                base = 22 * layer

                def half(q):
                    t = slice(q * HALF, (q + 1) * HALF)
                    up = bank[2 * q + 1][:, :].rearrange("p (m t) -> p m t", m=2)
                    n = base + q + 1
                    dve.wait_ge(*gate_ready(layer, 1, 0, q))
                    dve.wait_ge(silu, n)
                    if q:
                        dve.wait_ge(act_l, n - 1)
                    dve.tensor_tensor(prod[:, :, 0:HALF], sil[:, :, 0:HALF], up, ALU.mult).then_inc(prod_done, 1)
                    dve.wait_ge(prod_done, n)
                    dve.tensor_copy(acth[:, 0:2, t], prod[:, :, 0:HALF]).then_inc(act_h, 1)
                    dve.wait_ge(act_h, n)
                    dve.tensor_tensor(actl[:, 0:2, t], prod[:, :, 0:HALF], acth[:, 0:2, t].bitcast(F32),
                                      ALU.subtract).then_inc(act_l, 1)

                half(0)
                lo(nu + 2)
                half(1)
                lo(nu + 3)
                with dve.Fori(1, FP) as j:
                    lo(0, slot=0, count=nu + 3 + 2 * j)
                    for m in range(2):
                        n = base + 2 * j + m + 1
                        dve.wait_ge(*gate_ready(layer, 1, j, m))
                        dve.wait_ge(silu, n)
                        dve.wait_ge(act_l, n - 1)
                        dve.tensor_tensor(prod[:, m, :], sil[:, m, :], bank[2 + m][:, :], ALU.mult).then_inc(prod_done, 1)
                        dst_h = acth[:, bass.ds(2 * j + m, 1), :].rearrange("p a t -> p (a t)")
                        dst_l = actl[:, bass.ds(2 * j + m, 1), :].rearrange("p a t -> p (a t)")
                        dve.wait_ge(prod_done, n)
                        dve.tensor_copy(dst_h, prod[:, m, :]).then_inc(act_h, 1)
                        dve.wait_ge(act_h, n)
                        dve.tensor_tensor(dst_l, prod[:, m, :], dst_h.bitcast(F32), ALU.subtract).then_inc(act_l, 1)
                    lo(0, slot=1, count=nu + 4 + 2 * j)
                bd = 2 * layer + 1
                clear_acc(bd)
                c = DKT * P
                with dve.Fori(0, 6) as m:
                    lo(0, c, slot=0, count=nd + 3 + 2 * m)
                    lo(0, c, slot=1, count=nd + 4 + 2 * m)
                    dve.wait_ge(item_out, items_before[bd] + 1 + m)
                    dve.wait_ge(item_acc, accs_before[bd] + 1 + m)
                    dve.tensor_tensor(accy[:, :], accy[:, :], sqy[:, :], ALU.add).then_inc(item_acc, 1)
                lo(nd + 14, c)
                lo(nd + 15, c)
                accumulate(bd, 6, ITEMS_DOWN)

            for k in range(0, KT, 2):
                dve.wait_ge(xT_done, k + 1)
                dve.tensor_copy(h[:, k, :], bank[k][:, :]).then_inc(hx_v, 1)
            for q in range(2):
                dve.wait_ge(xsum, 2 * q + 2)
                mean(small[:, 8 + 2 * q:10 + 2 * q], small[:, 16 + 2 * q:18 + 2 * q], hmean)
            dve.wait_ge(vT_done, 1)
            dve.tensor_copy(vt[:, :], bank[0][:, 0:P])
            dve.tensor_copy(vx[:, :], bank[0][:, P:P + KT]).then_inc(v_ready, 1)
            dve.wait_ge(v_ready, 1)
            lo(0)
            dve.wait_ge(consts, 9)
            dve.wait_ge(hx_a, 4)
            dve.wait_ge(hx_v, 4)
            to_diag(12, hroot, 1, hdiag, None, 0)
            xs_build(0, 0, V_PREMIX)
            lo(1)
            to_diag(14, hroot, 2, hdiag, hrow, 1)
            xs_build(0, 1, V_PREMIX)
            dve.wait_ge(gw_in, 64)
            dve.tensor_scalar(bif[0:40, 1:2], bif[0:40, 0:1], 1.0 / GATE_CAP, None, ALU.mult).then_inc(g_v, 1)

            def q_out(i):
                dve.wait_ge(*in_ready(i))
                q, m0 = i // 2, 2 * (i % 2)
                dve.tensor_scalar(qT[:, m0:m0 + 2, q * HALF:(q + 1) * HALF],
                                  bank[i][:, :].rearrange("p (m t) -> p m t", m=2), float(DK) ** -0.5, None,
                                  ALU.mult).then_inc(in_v, 1)

            for i in range(3):
                q_out(i)
            lo(2)
            q_out(3)
            lo(3)
            G = HEADS
            dve.wait_ge(g_a, 2)
            dve.tensor_scalar(gli[0:G, :], tg[0:G, :], GATE_CAP, None, ALU.mult)
            dve.tensor_scalar(gy[0:G, :], ge[0:G, :], 1.0, None, ALU.add).then_inc(g_v, 1)
            dve.memset(gz[0:G, :], 0.0)
            dve.wait_ge(g_v, 2)
            dve.scalar_tensor_tensor(out=gd[0:G, :], in0=gy[0:G, :], scalar=-1.0, in1=ge[0:G, :],
                                     op0=ALU.add, op1=ALU.subtract).then_inc(g_v, 1)
            dve.wait_ge(g_a, 4)
            dve.wait_ge(g_v, 3)
            dve.tensor_tensor(gd[0:G, :], gd[0:G, :], gi[0:G, :], ALU.mult).then_inc(gT, 1)
            dve.wait_ge(gT, 1)
            dve.tensor_tensor(glf[0:G, :], gd[0:G, :], gl_[0:G, :], ALU.subtract).then_inc(gT, 1)
            dve.wait_ge(gT, 2)
            dve.tensor_tensor_scan(out=gB[0:G, :], data0=glf[0:G, :], data1=gz[0:G, :], initial=0.0,
                                   op0=ALU.add, op1=ALU.add).then_inc(g_v, 1)
            dve.tensor_tensor_scan(out=gm[0:G, :], data0=glf[0:G, :], data1=gli[0:G, :], initial=NEG,
                                   op0=ALU.add, op1=ALU.max).then_inc(g_v, 1)
            dve.wait_ge(g_v, 5)
            dve.tensor_tensor(z[:, :], gB[0:G, :], gm[0:G, :], ALU.subtract)
            dve.tensor_tensor(gc[0:G, :], gli[0:G, :], gB[0:G, :], ALU.subtract).then_inc(g_v, 1)
            dve.wait_ge(kz, 2)
            for i in range(4, 8):
                dve.wait_ge(*in_ready(i))
                for e in range(2):
                    p = slice(DK * e, DK * (e + 1))
                    last = dve.tensor_copy(kT[p, 2 * (i - 4) + e, :], bank[i - 4][p, :])
                last.then_inc(in_v, 1)
                if i % 2:
                    lo(4 + (i - 5) // 2)
            dve.wait_ge(gT, 3)
            dve.tensor_copy(ct[:, :, :], SUM[1][:, 0:32].rearrange("p (j h) -> p j h", j=TT))
            dve.tensor_copy(emt[:, :, :], SUM[1][:, 32:64].rearrange("p (j h) -> p j h", j=TT)).then_inc(gT_out, 1)
            for i in range(8, 16):
                dve.wait_ge(*in_ready(i))
                blk, b = (i - 8) // 2, (i - 8) % 2
                for j in range(2):
                    last = dve.tensor_copy(v[:, 2 * b + j, 2 * blk:2 * blk + 2, 0:DV],
                                           bank[i % 4][:, j * 256:(j + 1) * 256].rearrange("p (h d) -> p h d", h=2))
                last.then_inc(in_v, 1)
                if b:
                    lo(6 + blk)
            OFF = [0, 512, 1024, 896]

            def add_mask(t):
                dve.wait_ge(mrow, t + 1)
                if t >= 2:
                    dve.wait_ge(decs, t - 1)
                dve.tensor_tensor(masked[t % 2][:, :, :], SUM[0][:, :].rearrange("p (j l) -> p j l", j=TT),
                                  mask[:, None, :].to_broadcast([P, TT, P]), ALU.add).then_inc(msk, 1)

            def weigh(t):
                dve.wait_ge(decs, t + 1)
                dve.wait_ge(score, t + 1)
                if t >= 2:
                    dve.wait_ge(pv, t - 1)
                dve.tensor_tensor(pt[t % 2][:, 0:512], dec[:, 0:512], M[0][:, :], ALU.mult)
                dve.tensor_tensor(pt[t % 2][:, 512:1024], dec[:, 512:1024], M[1][:, :], ALU.mult)
                dve.tensor_tensor(pt[t % 2][:, 1024:1280], dec[:, 1024:1280], M[2][:, 0:256],
                                  ALU.mult).then_inc(ptd, 1)

            def denominators(t):
                dve.wait_ge(nsq, t + 1)
                if t >= 2:
                    dve.wait_ge(nscd, t - 1)
                d = den[:, t % 2]
                for b in range(2):
                    src = ROW[b][:, 0:2 * (DV + 1)].rearrange("p (j c) -> p j c", j=2)[:, :, DV]
                    last = dve.tensor_copy(d[:, 1, 2 * b:2 * b + 2], src)
                last.then_inc(den_step, 1)
                dve.wait_ge(den_step, 3 * t + 1)
                dve.tensor_tensor(d[:, 1, :], d[:, 1, :], d[:, 1, :], ALU.mult).then_inc(den_step, 1)
                dve.wait_ge(den_step, 3 * t + 2)
                dve.tensor_tensor(d[:, 1, :], d[:, 1, :], emt[:, :, t], ALU.max).then_inc(den_step, 1)
                dve.wait_ge(den_step, 3 * t + 3)
                dve.scalar_tensor_tensor(out=d[:, 2, :], in0=d[:, 1, :], scalar=EPS, in1=d[:, 0, :],
                                         op0=ALU.mult, op1=ALU.add).then_inc(dens, 1)

            def normalise(t):
                dve.wait_ge(mroot, t + 1)
                if t >= 2:
                    dve.wait_ge(nT, t - 1)
                for j in range(TT):
                    src = ROW[j // 2][:, (j % 2) * (DV + 1):(j % 2) * (DV + 1) + DV]
                    last = dve.tensor_scalar(nsc[t % 2][:, j, :], src, den[:, t % 2, 3, j:j + 1], None, ALU.mult)
                last.then_inc(nscd, 1)

            def gate_out(t):
                dve.wait_ge(nT, t + 1)
                dve.wait_ge(in_a, t + 1)
                dve.scalar_tensor_tensor(out=y[:, t, :], in0=M[3][:, :], scalar=vt[:, V_HEAD + t:V_HEAD + t + 1],
                                         in1=sigo[:, t, :], op0=ALU.mult, op1=ALU.mult).then_inc(ym, 1)

            for t in range(HEADS + 2):
                if t < HEADS:
                    add_mask(t)
                    weigh(t)
                if 1 <= t <= HEADS:
                    denominators(t - 1)
                    normalise(t - 1)
                if t in (2, 4, 6):
                    lo(9 + t // 2)
                if t >= 2:
                    gate_out(t - 2)
            for k in (0, 2, 4):
                mix_lo(k, ymh, y, yml_v)
            mix_lo(6, ymh, y, yml_v)
            lo(13)
            clear_acc(0)
            for i in range(4):
                if i % 2:
                    lo(14 + i // 2)
                accumulate(0, i, ITEMS_OUT)
            boundary(0, ITEMS_OUT, N_UP0, V_POSTMIX, V_PREFFN)
            ffn(0, N_UP0, N_DOWN0)
            boundary(1, ITEMS_DOWN, N_U, V_POSTFFN, V_PREMIX + KT)
            dve.scalar_tensor_tensor(out=lamc[:, 0, :], in0=vt[:, V_LAM:V_LAM + KT], scalar=-1.0,
                                     in1=vt[:, V_LAM:V_LAM + KT], op0=ALU.mult, op1=ALU.max).then_inc(lam_v, 1)
            dve.wait_ge(lam_a, 1)
            dve.tensor_scalar(lamc[:, 2, :], lamc[:, 1, :], 1.0, None, ALU.add).then_inc(lam_v, 1)
            dve.memset(upad[:, :, 0:CONV - 1], 0.0).then_inc(upz, 1)
            dve.wait_ge(upz, 1)

            def convolve(k, ready):
                dve.wait_ge(u_out, ready)
                for j in range(CONV - 1):
                    if j:
                        dve.wait_ge(conv, 3 * k + j)
                    w = V_CONVW + j * KT + k
                    dve.scalar_tensor_tensor(out=uc[:, k, :], in0=upad[:, k, j:j + S], scalar=vt[:, w:w + 1],
                                             in1=uc[:, k, :], op0=ALU.mult, op1=ALU.add).then_inc(conv, 1)

            for k in range(KT):
                if k == 1:
                    lo(N_U + 2)
                if k == 3:
                    lo(N_U + 3)
                if k == 6:
                    lo(N_GB0)
                convolve(k, 3 if k < 2 else 4 if k < 4 else k + 1)
            lo(N_GA)
            dve.wait_ge(lam_a, 2)
            dve.reciprocal(lamc[:, 4, :], lamc[:, 2, :])
            dve.scalar_tensor_tensor(out=lamc[:, 5, :], in0=lamc[:, 2, :], scalar=-1.0, in1=lamc[:, 1, :],
                                     op0=ALU.add, op1=ALU.subtract).then_inc(upz, 1)
            dve.wait_ge(upz, 2)
            dve.tensor_tensor(lamc[:, 4, :], lamc[:, 4, :], lamc[:, 5, :], ALU.mult).then_inc(upz, 1)
            dve.wait_ge(upz, 3)
            dve.tensor_tensor(lamc[:, 3, :], lamc[:, 4, :], lamc[:, 3, :], ALU.subtract).then_inc(upz, 1)
            dve.wait_ge(upz, 4)
            dve.scalar_tensor_tensor(out=lamc[:, 2, :], in0=vt[:, V_LAM:V_LAM + KT], scalar=0.0, in1=lamc[:, 3, :],
                                     op0=ALU.min, op1=ALU.add).then_inc(upz, 1)
            dve.wait_ge(upz, 5)
            dve.tensor_scalar(lamc[:, 4, :], lamc[:, 2, :], LRU_C, None, ALU.mult)
            dve.tensor_scalar(lamc[:, 5, :], lamc[:, 2, :], -LRU_C, None, ALU.mult).then_inc(lam_v, 1)
            lo(N_GX)
            for m in range(KT):
                if m == 2:
                    lo(N_GB1)
                dve.wait_ge(ga_out, KT + m + 1)
                dve.wait_ge(ul, m + 1)
                dve.tensor_tensor(uc[:, m, :], uc[:, m, :], sgi[:, m % 2, :], ALU.mult).then_inc(iu, 1)
            lo(N_GB1 + 1)
            for m in range(KT):
                dve.wait_ge(ab, m + 1)
                dve.tensor_tensor(y[:, m, :], la[:, m, :], la[:, m, :], ALU.mult).then_inc(rsq, 1)
                dve.wait_ge(rsq, m + 1)
                dve.scalar_tensor_tensor(out=lt[:, m, :], in0=y[:, m, :], scalar=1.0, in1=lt[:, m, :],
                                         op0=ALU.add, op1=ALU.mult).then_inc(one_a2, 1)
            for m in range(KT):
                dve.wait_ge(roots, m // 4 + 1)
                dve.wait_ge(iu, m + 1)
                dve.tensor_tensor(uc[:, m, :], lt[:, m, :], uc[:, m, :], ALU.mult).then_inc(rsq, 1)
                dve.wait_ge(rsq, KT + 2 * m + 1)
                dve.tensor_tensor_scan(out=y[:, m, :], data0=la[:, m, :], data1=uc[:, m, :], initial=0.0,
                                       op0=ALU.mult, op1=ALU.add).then_inc(rsq, 1)
                dve.wait_ge(rsq, KT + 2 * m + 2)
                dve.wait_ge(gb_out, m + 1)
                dve.tensor_tensor(lt[:, m, :], y[:, m, :], gel[:, m, :], ALU.mult).then_inc(ry, 1)
                if m == 3:
                    lo(N_GB1 + 2)
                if m == 5:
                    lo(N_RGOUT)
            for k in range(0, KT, 2):
                mix_lo(k, ryh, lt, ryl_v)
            lo(N_RGOUT + 1)
            clear_acc(2)
            for i in range(4):
                if i % 2:
                    lo(N_RGOUT + 2 + i // 2)
                accumulate(2, i, ITEMS_OUT)
            boundary(2, ITEMS_OUT, N_UP1, V_POSTMIX + KT, V_PREFFN + KT)
            ffn(1, N_UP1, N_DOWN1)
            accumulate(3, 7, ITEMS_DOWN)
            ymeans(3, 0)
            to_diag(4, yroot, 7, ydiag, hrow, 8)
            scale_y(3, 0, V_POSTFFN + KT)
            accumulate(3, 8, ITEMS_DOWN)
            ymeans(3, 1)
            to_diag(6, yroot, 8, ydiag, yrow, 7)

            def result(j):
                dve.wait_ge(oT, 2 * j + 1)
                dve.tensor_copy(outT[:, j, 0:512], bank[RESULT_BANKS[j][0]][:, :]).then_inc(oc_v, 1)

            scale_y(3, 1, V_POSTFFN + KT)
            for j in range(TT):
                result(j)

        @block.tensor
        def _(pe):
            def products(dst, sh, sl, mh, ml, first, last):
                pe.matmul(dst, sh, mh, start=first, stop=False)
                pe.matmul(dst, sh, ml, start=False, stop=False)
                return pe.matmul(dst, sl, mh, start=False, stop=last)

            def split_block(n, mm, dst, t0, nt, ready=None):
                s = n % 2
                for k in range(KT):
                    if ready is not None:
                        ready(k)
                    c = slice(mm * P, (mm + 1) * P)
                    last = products(dst, kview(wh[s])[:, k, c], kview(wl[s])[:, k, c],
                                    xsh[:, k, t0:t0 + nt], xsl[:, k, t0:t0 + nt], k == 0, k == KT - 1)
                return last

            def full_block(n, banks, done, waits=None, ready=None):
                pe.wait_ge(lo_done, n + 1)
                for mm in range(2):
                    if waits is not None:
                        waits(mm)
                    last = split_block(n, mm, banks[mm], 0, S, ready if mm == 0 else None)
                    last.then_inc(w_used if mm else done, 1)

            def sum_y(bd, q, accs):
                pe.wait_ge(item_acc, accs)
                for j in range(2):
                    t = q * HALF + j * P
                    last = pe.matmul(SUM[q][:, j:j + 1], accy[:, t:t + P], ones[:, 0:1], start=(j == 0),
                                     stop=(j == 1), skip_group_check=True)
                last.then_inc(ysum, 1)

            def row_y(bd, q):
                pe.wait_ge(ydiag, 2 * bd + q + 1)
                pe.matmul(ROW[q][:, 0:HALF], ones[:, :], diag[:, :, :].rearrange("p a t -> p (a t)"),
                          start=True, stop=True).then_inc(yrow, 1)

            def sum_h(bd, q):
                for k in range(KT):
                    pe.wait_ge(h_sq, 16 * bd + 8 * q + k + 1)
                    for j in range(2):
                        last = pe.matmul(SUM[q][:, 4 + j:5 + j], hsq[:, k, j * P:(j + 1) * P], ones[:, 0:1],
                                         start=(k == 0 and j == 0), stop=(k == KT - 1), skip_group_check=True)
                last.then_inc(hsum, 1)

            def row_h(p, q):
                pe.wait_ge(hdiag, 2 * p + q + 1)
                pe.matmul(ROW[q][:, HALF:S], ones[:, :], diag[:, :, :].rearrange("p a t -> p (a t)"),
                          start=True, stop=True).then_inc(hrow, 1)

            def mix_ready(even, odd):
                return lambda k: pe.wait_ge(odd if k % 2 else even, k // 2 + 1)

            def xs_ready(p, q):
                def ready(k):
                    if k % 2 == 0:
                        pe.wait_ge(xl_v, 8 * p + 4 * q + k // 2 + 1)
                    else:
                        pe.wait_ge(xl_p, 8 * p + 4 * q + k // 2 + 1)
                return ready

            def first_two(n, p, done, bd=None):
                dn = done if isinstance(done, tuple) else (done, done)
                for b in range(2):
                    pe.wait_ge(lo_done, n + b + 1)
                    for mm in range(2):
                        last = split_block(n + b, mm, M[b][:, mm * HALF:(mm + 1) * HALF], 0, HALF,
                                           xs_ready(p, 0) if b == 0 and mm == 0 else None)
                        if bd is not None and b == 0 and mm == 0:
                            row_y(bd, 1)
                    last.then_inc(dn[b], 1)
                if bd is not None:
                    sum_h(bd, 1)
                    row_h(p, 1)
                for b in range(2):
                    for mm in range(2):
                        last = split_block(n + b, mm, M[2 + b][:, mm * HALF:(mm + 1) * HALF], HALF, HALF,
                                           xs_ready(p, 1) if b == 0 and mm == 0 else None)
                    last.then_inc(w_used, 1)

            accs_after = {0: (ITEMS_OUT, 6, 8), 1: (ITEMS_DOWN, 8, 9), 2: (ITEMS_OUT, 6, 8), 3: (ITEMS_DOWN, 8, 9)}

            def sum_y_b(bd):
                lst, _, nb = accs_after[bd]
                sum_y(bd, 1, accs_before[bd] + 1 + acc_ops(lst[:nb]))

            def sum_y_a(bd):
                lst, na, _ = accs_after[bd]
                sum_y(bd, 0, accs_before[bd] + 1 + acc_ops(lst[:na]))

            def out_proj(bd, n, ready):
                base = items_before[bd]
                full_block(n, [M[0], M[1]], item_done, ready=ready)
                full_block(n + 1, [M[2], M[3]], item_done)
                for b in range(2):
                    pe.wait_ge(lo_done, n + 3 + b)
                    pe.wait_ge(item_out, base + b + 1)
                    for mm in range(2):
                        last = split_block(n + 2 + b, mm, M[b][:, mm * HALF:(mm + 1) * HALF], 0, HALF)
                    last.then_inc(item_done, 1)
                for b in range(2):
                    pe.wait_ge(item_out, base + b + 3)
                    for mm in range(2):
                        last = split_block(n + 2 + b, mm, M[2 + b][:, mm * HALF:(mm + 1) * HALF], HALF, HALF)
                        if b == 0 and mm == 0:
                            sum_y_a(bd)
                    last.then_inc(w_used, 1)
                    if b == 0:
                        row_y(bd, 0)
                sum_h(bd, 0)
                sum_y_b(bd)
                row_h(bd + 1, 0)

            def down_part(s, part, dst, t0, nt):
                for k in range(DKT):
                    kk = part * DKT + k
                    last = products(dst, kview(wh[s], P)[:, k, :], kview(wl[s], P)[:, k, :],
                                    acth[:, kk, t0:t0 + nt], actl[:, kk, t0:t0 + nt],
                                    kk == 0, kk == FT - 1)
                return last

            def ffn(layer, nu, nd):
                base = 22 * layer
                bd = 2 * layer + 1
                first_two(nu, bd, (gate_done, up_done), bd - 1)
                with pe.Fori(1, FP) as j:
                    for b, done in ((0, gate_done), (1, up_done)):
                        pe.wait_ge(lo_done, nu + 1 + b + 2 * j)
                        for mm in range(2):
                            if b == 0:
                                pe.wait_ge(silu, base + 2 * j - 1 + mm)
                                if mm:
                                    pe.wait_ge(prod_done, base + 2 * j - 1)
                            else:
                                pe.wait_ge(prod_done, base + 2 * j - 1 + mm)
                            for k in range(KT):
                                c = slice(mm * P, (mm + 1) * P)
                                last = products(M[2 * b + mm][:, :], kview(wh[b])[:, k, c], kview(wl[b])[:, k, c],
                                                xsh[:, k, :], xsl[:, k, :], k == 0, k == KT - 1)
                            last.then_inc(w_used if mm else done, 1)
                pe.wait_ge(silu, base + 22)
                pe.wait_ge(act_l, base + 20)
                it = items_before[bd]
                with pe.Fori(0, 3) as i:
                    for t in range(2):
                        pe.wait_ge(item_out, it - 1 + t + 2 * i)
                        for part in range(2):
                            pe.wait_ge(lo_done, nd + 1 + part + 2 * t + 4 * i)
                            if part:
                                pe.wait_ge(act_l, base + 22)
                            down_part(part, part, M[t][:, :], 0, S).then_inc(w_used, 1)
                pe.wait_ge(item_out, it + 5)
                for part in range(2):
                    pe.wait_ge(lo_done, nd + 13 + part)
                    down_part(part, part, M[0][:, :], 0, S).then_inc(w_used, 1)
                pe.wait_ge(item_out, it + 6)
                for part in range(2):
                    pe.wait_ge(lo_done, nd + 15 + part)
                    last = down_part(part, part, M[1][:, 0:HALF], 0, HALF)
                last.then_inc(item_done, 1)
                pe.wait_ge(prod_done, base + 22)
                down_part(0, 0, M[2][:, 0:HALF], HALF, HALF).then_inc(w_used, 1)
                sum_y_a(bd)
                down_part(1, 1, M[2][:, 0:HALF], HALF, HALF).then_inc(w_used, 1)
                row_y(bd, 0)
                if layer == 0:
                    sum_h(bd, 0)
                    sum_y_b(bd)
                    row_h(bd + 1, 0)

            pe.wait_ge(consts, 9)
            for j in range(TT):
                pe.wait_ge(x_in[j], 16)
                for k in range(KT):
                    last = pe.transpose(bank[k][:, j * P:(j + 1) * P], xin[:, j, k * P:(k + 1) * P], ident[:, :])
                    if j == TT - 1:
                        last.then_inc(xT_done, 1)
            pe.wait_ge(vec_in, 160)
            pe.wait_ge(hx_v, 1)
            pe.transpose(bank[0][:, 0:P], vrow[:, :], ident[:, :])
            pe.transpose(bank[0][:, P:P + KT], vrow2[:, :], ident[0:KT, 0:KT]).then_inc(vT_done, 1)
            pe.wait_ge(hx_v, 4)
            row_h(0, 0)
            pe.wait_ge(hx_a, 4)
            row_h(0, 1)
            pe.wait_ge(v_ready, 1)
            first_two(N_Q, 0, in_done)
            pe.wait_ge(gw_in, 64)
            for k in range(KT):
                last = pe.matmul(SUM[0][0:40, :], gw[:, k, :], y[:, k, :], start=(k == 0), stop=(k == KT - 1))
            last.then_inc(gates_mm, 1)
            for b in range(2):
                full_block(N_K + b, [M[2 * b], M[2 * b + 1]], in_done,
                           waits=lambda mm, b=b: pe.wait_ge(in_v, 2 * b + mm + 1))
            pe.wait_ge(g_v, 6)
            pe.wait_ge(g_a, 5)
            for j in range(TT):
                pe.transpose(SUM[1][:, 8 * j:8 * j + 8], gc[0:8, j * P:(j + 1) * P], ident[0:8, 0:8])
            for j in range(TT):
                last = pe.transpose(SUM[1][:, 32 + 8 * j:40 + 8 * j], gem[0:8, j * P:(j + 1) * P], ident[0:8, 0:8])
            last.then_inc(gT, 1)
            for b in range(4):
                n = N_V + b
                pe.wait_ge(lo_done, n + 1)
                for bb in range(2):
                    i = 8 + 2 * b + bb
                    pe.wait_ge(in_v, i - 3)
                    for j in range(2):
                        for k in range(KT):
                            t = slice((2 * bb + j) * P, (2 * bb + j + 1) * P)
                            last = products(M[i % 4][:, j * 256:(j + 1) * 256], xsh[:, k, t], xsl[:, k, t],
                                            kview(wh[n % 2])[:, k, :], kview(wl[n % 2])[:, k, :],
                                            k == 0, k == KT - 1)
                    last.then_inc(w_used if bb else in_done, 1)
            OFF = [0, 512, 1024, 896]

            def scores(t):
                if t:
                    pe.wait_ge(decs, t)
                pe.matmul(SUM[0][:, :], sel[:, t, :], z[:, :], start=True, stop=True).then_inc(mrow, 1)
                if t:
                    pe.wait_ge(ptd, t)
                for i in (0, 1, 2, 3):
                    dst = [M[0][:, :], M[1][:, 0:384], M[2][:, 0:256], M[1][:, 384:512]][i]
                    last = pe.matmul(dst, kT[:, t, i * P:(i + 1) * P], qT[:, t // 2, i * P:S],
                                     start=True, stop=True)
                last.then_inc(score, 1)

            def outputs(t):
                pe.wait_ge(ptd, t + 1)
                if t:
                    pe.wait_ge(nscd, t)
                for j in range(TT):
                    for i in range(j + 1):
                        o = OFF[i] + (j - i) * P
                        last = pe.matmul(ROW[j // 2][:, (j % 2) * (DV + 1):(j % 2 + 1) * (DV + 1)],
                                         pt[t % 2][:, o:o + P], v[:, i, t, :], start=(i == 0), stop=(i == j))
                last.then_inc(pv, 1)

            def turn(t):
                pe.wait_ge(nscd, t + 1)
                if t:
                    pe.wait_ge(ym, t)
                for j in range(TT):
                    last = pe.transpose(M[3][:, j * P:(j + 1) * P], nsc[t % 2][:, j, :], ident[:, :])
                last.then_inc(nT, 1)

            def out_gate(t):
                if t % 2 == 0:
                    pe.wait_ge(lo_done, N_O + t // 2 + 1)
                if t:
                    pe.wait_ge(in_a, t)
                split_block(N_O + t // 2, t % 2, SUM[1], 0, S).then_inc(w_used if t % 2 else in_done, 1)

            pe.wait_ge(gT_out, 1)
            pe.wait_ge(in_v, 16)
            for t in range(HEADS + 2):
                if t < HEADS:
                    scores(t)
                if 1 <= t <= HEADS:
                    outputs(t - 1)
                if t < HEADS:
                    out_gate(t)
                if t >= 2:
                    turn(t - 2)
            out_proj(0, N_MLOUT, mix_ready(yml_v, yml_p))
            ffn(0, N_UP0, N_DOWN0)
            first_two(N_U, 2, u_done, 1)
            for b in range(2):
                full_block(N_U + 2 + b, [M[2 * b], M[2 * b + 1]], u_done,
                           waits=lambda mm, b=b: pe.wait_ge(u_out, 2 * b + mm + 1))
            full_block(N_GB0, [M[0], M[1]], gb_done, waits=lambda mm: pe.wait_ge(u_out, 5 + mm))
            pe.wait_ge(u_out, 8)
            for g, n in ((0, N_GA), (1, N_GX)):
                pe.wait_ge(lo_done, n + 1)
                for m in range(KT):
                    if g == 0:
                        pe.wait_ge(ul, 2 * (m // 2) + 2)
                    if g or m >= 2:
                        pe.wait_ge(ga_out, KT * g + m - 1)
                    for k in range(2):
                        kk, c = 2 * (m // 2) + k, slice((m % 2) * P, (m % 2 + 1) * P)
                        last = products(bank[2 + m % 2], kview(wh[n % 2])[:, kk, c],
                                        kview(wl[n % 2])[:, kk, c], uch[:, kk, :], ucl[:, kk, :], k == 0, k == 1)
                    last.then_inc(w_used if m == KT - 1 else ga_done, 1)
            for b in range(3):
                def bank_read(mm, b=b):
                    if b == 1:
                        pe.wait_ge(ga_out, 16)
                    else:
                        pe.wait_ge(gb_out, (1 if b == 0 else 3) + mm)
                full_block(N_GB1 + b, [M[0], M[1]] if b != 1 else [M[2], M[3]], gb_done, waits=bank_read)
            pe.wait_ge(gb_out, 8)
            out_proj(2, N_RGOUT, mix_ready(ryl_v, ryl_p))
            ffn(1, N_UP1, N_DOWN1)
            sum_y_b(3)
            for q in range(2):
                if q == 1:
                    row_y(3, 1)
                pe.wait_ge(h_up, 48 + 8 * q + 8)
                for jj in range(2):
                    j = 2 * q + jj
                    for b in range(2):
                        dst = RESULT_BANKS[j][b]
                        if j == 3:
                            pe.wait_ge(oc_v if b == 0 else oc_a, 1)
                        if j == 2:
                            pe.wait_ge(item_out, items_before[3] + 9)
                        for k in range(4):
                            last = pe.transpose(bank[dst][:, k * P:(k + 1) * P],
                                                h[:, 4 * b + k, j * P:(j + 1) * P], ident[:, :])
                        last.then_inc(oT, 1)


NAMES = ["x", "ml_w_in", "ml_b_if", "ml_head_norm", "ml_w_out", "lru_w_in", "lru_conv_w", "lru_conv_b",
         "lru_w_gate_a", "lru_b_gate_a", "lru_w_gate_x", "lru_b_gate_x", "lru_lambda", "lru_w_out",
         "norm_pre_mix", "norm_post_mix", "norm_pre_ffn", "norm_post_ffn",
         "ffn_w_gate", "ffn_w_up", "ffn_w_down"]


def kernel(**inputs):
    import numpy as _np
    import concourse.bacc as _bacc
    from concourse.bass_utils import run_bass_kernel_spmd as _run

    nc = _bacc.Bacc("TRN2", target_bir_lowering=False, num_devices=1, dynamic_dma_scratch_size=1024)
    arrays, aps = {}, {}
    for name in NAMES:
        arr = _np.ascontiguousarray(inputs[name])
        arrays[f"in_{name}"] = arr
        aps[name] = nc.dram_tensor(f"in_{name}", arr.shape, F32, kind="ExternalInput").ap()
    out = nc.dram_tensor("out_0", (1, S, D), F32, kind="ExternalOutput").ap()
    build(nc, aps, out)
    r = _run(nc, [arrays], core_ids=[0])
    return r.results[0]["out_0"]
```

```python
from contextlib import ExitStack

import numpy as np
import concourse.bass as bass
import concourse.mybir as mybir

F32 = mybir.dt.float32
F32R = mybir.dt.float32r
ALU = mybir.AluOpType
ACT = mybir.ActivationFunctionType

P = 128
D = 1024
S = 512
KT = D // P
TT = S // P
HALF = S // 2
HEADS = 8
DK = 64
DV = 128
QK = HEADS * DK
VW = HEADS * DV
GATE_CAP = 15.0
LRU_C = 8.0
CONV = 4
FF = 2816
FT = FF // P
EPS = 1e-6
NEG = -1e30
BC = 256
FP = FF // BC
DKT = FT // 2

N_Q, N_K, N_V, N_O = 0, 2, 4, 8
N_MLOUT = 12
N_UP0 = 16
N_DOWN0 = N_UP0 + 2 * FP
N_U = N_DOWN0 + 2 * KT
N_GB0 = N_U + 4
N_GA, N_GX = N_GB0 + 1, N_GB0 + 2
N_GB1 = N_GX + 1
N_RGOUT = N_GB1 + 3
N_UP1 = N_RGOUT + 4
N_DOWN1 = N_UP1 + 2 * FP

VECTORS = [("norm_pre_mix", 2), ("norm_post_mix", 2), ("norm_pre_ffn", 2), ("norm_post_ffn", 2), ("ml_head_norm", 1),
           ("lru_conv_w", CONV), ("lru_conv_b", 1), ("lru_lambda", 1), ("lru_b_gate_a", 1), ("lru_b_gate_x", 1)]
V_PREMIX, V_POSTMIX, V_PREFFN, V_POSTFFN, V_HEAD, V_CONVW, V_CONVB, V_LAM, V_BA, V_BX, V_END = (
    KT * sum(n for _, n in VECTORS[:i]) for i in range(len(VECTORS) + 1))

LO_DVE, LO_POOL = (2, 4, 6, 7), (0, 1, 3, 5)

ITEMS_OUT = [(0, 0, 1, 0, S), (1, 1, 1, 0, S), (2, 2, 1, 0, S), (3, 3, 1, 0, S),
             (0, 4, 2, 0, HALF), (1, 6, 2, 0, HALF), (2, 4, 2, HALF, HALF), (3, 6, 2, HALF, HALF)]
ITEMS_DOWN = [(m % 2, m, 1, 0, S) for m in range(7)] + [(1, 7, 1, 0, HALF), (2, 7, 1, HALF, HALF)]


def build(nc, a, out):
    ctx = ExitStack()
    with ctx:
        free = [-(-nc.sbuf_base // 64) * 64]

        def sb(name, shape, dt=F32):
            size = int(np.prod(shape[1:])) * 4
            t = nc.alloc_sbuf_tensor_at(name, shape, dt, offset=free[0])
            free[0] += -(-size // 32) * 32
            return t

        vt = sb("vt", [P, V_END])
        ident = sb("ident", [P, P])
        ones = sb("ones", [P, P])
        small = sb("small", [P, 32])
        expo = sb("expo", [P, 8])
        bif = sb("bif", [P, 2])
        h = sb("h", [P, KT, S])
        xs_at = free[0]
        xsh = sb("xsh", [P, KT, S], F32R)
        xsl = sb("xsl", [P, KT, S], F32R)
        y = sb("y", [P, KT, S])
        raw = [sb(f"raw{s}", [P, 2048]) for s in range(2)]
        wh = [sb(f"wh{s}", [P, 2048], F32R) for s in range(2)]
        wl = [sb(f"wl{s}", [P, 2048], F32R) for s in range(2)]
        sqy = sb("sqy", [P, S])
        hrow_s = sqy
        accy = sb("accy", [P, S])
        hsq = sb("hsq", [P, KT, HALF])
        diag = sb("diag", [P, 2, P])
        sil = sb("sil", [P, 2, S])
        sil_end = free[0]
        prod = sb("prod", [P, 2, S])
        free[0] = sil_end - 4 * 2 * S
        hsq_b = sb("hsq_b", [P, KT, HALF])
        region = free[0]
        acth = sb("acth", [P, FT, S], F32R)
        actl = sb("actl", [P, FT, S], F32R)
        assert free[0] <= nc.sbuf_usable_end, (free[0], nc.sbuf_usable_end)
        end = free[0]
        free[0] = region
        qT = sb("qT", [P, QK // P, S])
        at_k = free[0]
        kT = sb("kT", [P, HEADS, S])
        v = sb("v", [P, TT, HEADS, DV + 1])
        at_sigo = free[0]
        sigo = sb("sigo", [P, KT, S])
        z = sb("z", [HEADS, S])
        ct = sb("ct", [P, TT, HEADS])
        emt = sb("emt", [P, TT, HEADS])
        mask = sb("mask", [P, P])
        sel = sb("sel", [HEADS, HEADS, P])
        early = free[0]
        masked = [sb(f"masked{i}", [P, TT, P]) for i in range(2)]
        dec = sb("dec", [P, 1280])
        pt = [sb(f"pt{i}", [P, 1280]) for i in range(2)]
        nsc = [sb(f"nsc{i}", [P, TT, DV]) for i in range(2)]
        den = sb("den", [P, 2, 4, TT])
        assert free[0] <= end, (free[0], end)
        free[0] = early
        xin = sb("xin", [P, TT, D])
        gw = sb("gw", [P, KT, 40])
        assert free[0] <= end
        free[0] = early
        ge, gy, gl_, gd, gi, gli, glf, gB, gm, gc, gem, gz = (
            sb(f"g{i}", [40, S]) for i in range(12))
        tg = sil[0:40, 0, :]
        assert free[0] <= end
        free[0] = at_k
        mlh = sb("mlh", [P, KT, S], F32R)
        free[0] = at_sigo
        mll = sb("mll", [P, KT, S], F32R)
        free[0] = region
        upad = sb("upad", [P, KT, CONV - 1 + S + 1])
        at_uc = free[0]
        uc = sb("uc", [P, KT, S])
        at_uch = free[0]
        uch = sb("uch", [P, KT, S], F32R)
        ucl = sb("ucl", [P, KT, S], F32R)
        gel = sb("gel", [P, KT, S])
        sgi = upad[:, :, 0:S]
        lamc = sb("lamc", [P, 6, KT])
        assert free[0] <= end, (free[0], end)
        free[0] = at_uch
        la = sb("la", [P, KT, S])
        lt = sb("lt", [P, KT, S])
        free[0] = at_uc
        rgh = sb("rgh", [P, KT, S], F32R)
        free[0] = at_uch
        rgl = sb("rgl", [P, KT, S], F32R)
        free[0] = xs_at
        outT = sb("outT", [P, TT, D])
        yg = sb("yg", [P, TT, D])
        hT = [y[:, 2 * j:2 * j + 2, :].rearrange("p a t -> p (a t)") for j in range(TT)]
        gdiag = hsq[:, 0:4, :].rearrange("p a t -> p (a t)")
        grow = hsq[:, 4:8, :].rearrange("p a t -> p (a t)")

        bank = [ctx.enter_context(nc.psum_tensor(f"bank{i}", [P, 512], F32))[:, :] for i in range(8)]
        M = bank[:4]
        SUM = bank[4:6]
        X_BANKS = [[bank[b] for b in bs] for bs in ((0, 1, 2, 3), (4, 5, 2, 3))]
        ROW = bank[6:8]

        def sem(name):
            return ctx.enter_context(nc.semaphore(name))

        x_in = [sem(f"x_in{j}") for j in range(TT)]
        vec_in = sem("vec_in")
        gate_w_in = sem("gate_w_in")
        stored = sem("stored")
        raw_in = [sem("raw_in0"), sem("raw_in1")]
        hi_done = sem("hi_done")
        lo_done = sem("lo_done")
        w_used = sem("w_used")
        consts = sem("consts")
        zeroed = sem("zeroed")
        x_turned = sem("x_turned")
        x_out_v = sem("x_out_v")
        x_out_a = sem("x_out_a")
        xsum = sem("xsum")
        item_done = sem("item_done")
        item_out = sem("item_out")
        item_acc = sem("item_acc")
        ysum = sem("ysum")
        ymean = sem("ymean")
        yroot = sem("yroot")
        ydiag = sem("ydiag")
        yrow = sem("yrow")
        yscaled = sem("yscaled")
        h_up = sem("h_up")
        h_sq = sem("h_sq")
        h_acc = sem("h_acc")
        hsum = sem("hsum")
        hmean = sem("hmean")
        hroot = sem("hroot")
        hdiag = sem("hdiag")
        hrow = sem("hrow")
        x_scaled = sem("x_scaled")
        x_hi = sem("x_hi")
        x0_lo_v = sem("x0_lo_v")
        x_lo = sem("x_lo")
        row_in = sem("row_in")
        gate_in = sem("gate_in")
        up_in = sem("up_in")
        x0_lo_p = sem("x0_lo_p")
        gate_done = sem("gate_done")
        up_done = sem("up_done")
        silu = sem("silu")
        prod_done = sem("prod_done")
        act_h = sem("act_h")
        act_l = sem("act_l")
        proj_done = sem("proj_done")
        proj_out = sem("proj_out")
        ogate_out = sem("ogate_out")
        gates_mm = sem("gates_mm")
        gates_act = sem("gates_act")
        gates_dve = sem("gates_dve")
        gates_turned = sem("gates_turned")
        gates_kept = sem("gates_kept")
        row_done = sem("row_done")
        mask_added = sem("mask_added")
        decay_done = sem("decay_done")
        score = sem("score")
        weighed = sem("weighed")
        numer_done = sem("numer_done")
        numer_sq = sem("numer_sq")
        denom_done = sem("denom_done")
        denom_root = sem("denom_root")
        normalised = sem("normalised")
        turned = sem("turned")
        mixed = sem("mixed")
        mixed_hi = sem("mixed_hi")
        mixed_lo_v = sem("mixed_lo_v")
        mixed_lo_p = sem("mixed_lo_p")
        k_zeroed = sem("k_zeroed")
        u_done = sem("u_done")
        u_out = sem("u_out")
        uc_out = sem("uc_out")
        branch_in = sem("branch_in")
        pad_zeroed = sem("pad_zeroed")
        conv = sem("conv")
        u_rounded = sem("u_rounded")
        u_low = sem("u_low")
        branch_done = sem("branch_done")
        branch_out = sem("branch_out")
        rgate_done = sem("rgate_done")
        rgate_out = sem("rgate_out")
        gated_u = sem("gated_u")
        a_done = sem("a_done")
        a2_done = sem("a2_done")
        one_a2 = sem("one_a2")
        roots = sem("roots")
        scan_in = sem("scan_in")
        scanned = sem("scanned")
        den_step = sem("den_step")
        rg_out = sem("rg_out")
        rg_out_hi = sem("rg_out_hi")
        rg_out_lo_v = sem("rg_out_lo_v")
        rg_out_lo_p = sem("rg_out_lo_p")
        lam_a = sem("lam_a")
        lam_v = sem("lam_v")
        hT_done = sem("hT_done")
        hT_out = sem("hT_out")
        gdiag_done = sem("gdiag_done")
        tile_done = sem("tile_done")
        tile_sq = sem("tile_sq")
        tile_g = sem("tile_g")
        tile_mean = sem("tile_mean")
        tile_root = sem("tile_root")
        result = sem("result")

        block = ctx.enter_context(nc.Block())

        def kview(t, c=BC):
            n = {BC: KT, P: DKT, D: 2}[c]
            return t[:, 0:n * c].rearrange("p (k c) -> p k c", c=c)

        def rows(w):
            return w.rearrange("(k p) c -> p k c", p=P)

        w_in = rows(a["ml_w_in"][0])
        w_mlout = rows(a["ml_w_out"][0])
        w_lru = rows(a["lru_w_in"][0])
        w_rgout = rows(a["lru_w_out"][0])
        w_ga = rows(a["lru_w_gate_a"][0].rearrange("n c d -> (n c) d"))
        w_gx = rows(a["lru_w_gate_x"][0].rearrange("n c d -> (n c) d"))
        items_before = [0, 8, 17]
        done_before = [0, 4, 5]
        first_block = [N_MLOUT, N_DOWN0, N_RGOUT]

        def item_ready(bd, i):
            n, base = first_block[bd], done_before[bd]
            if bd % 2 == 0:
                return [(item_done, base + 1), (w_used, n + 1), (item_done, base + 2), (w_used, n + 2),
                        (item_done, base + 3), (item_done, base + 4), (w_used, n + 3), (w_used, n + 4)][i]
            return (item_done, base + 1) if i == 7 else (w_used, n + 2 * i + 2) if i < 7 else (w_used, n + 16)

        def in_ready(i):
            if i < 2:
                return proj_done, i + 1
            if i < 4:
                return w_used, i - 1
            b = (i - 4) // 2
            return (proj_done, 3 + b) if i % 2 == 0 else (w_used, N_K + b + 1)

        def u_ready(i):
            if i < 2:
                return u_done, i + 1
            if i < 4:
                return w_used, N_U + i - 1
            b = (i - 4) // 2
            return (u_done, 3 + b) if i % 2 == 0 else (w_used, N_U + 3 + b)

        def gb_ready(g, m):
            return (branch_done, g + 1) if m == 0 else (w_used, N_GB0 + 1 if g == 0 else N_GB1 + g)

        def gate_index(m, g):
            return KT * (m // 4) + 4 * g + m % 4

        def ga_ready(m, g):
            i = gate_index(m, g)
            return (rgate_done, i + (i < 12)) if m < KT - 1 else (w_used, N_GA + g + 1)

        def gate_bank(m, g):
            return bank[(2 + gate_index(m, g)) % 8]

        def gate_ready(layer, b, j, m):
            nu = (N_UP0, N_UP1)[layer]
            if m == 0:
                return (gate_done, up_done)[b], FP * layer + 1 + j
            return w_used, nu + 2 * j + b + 1
        accs_before = [0, 13, 23]

        def acc_ops(items):
            return sum(it[2] for it in items)

        @block.sync
        def _(sp):
            def load(n, src, c=BC, slot=None, wait=None):
                s = n % 2 if slot is None else slot
                if wait is None:
                    wait = n - 1 if n >= 2 else None
                if wait is not None:
                    sp.wait_ge(lo_done, wait)
                sp.dma_start(kview(raw[s], c), src).then_inc(raw_in[s], 16)

            x = a["x"][0].rearrange("(j p) d -> p j d", p=P)
            for j in range(TT // 2):
                sp.dma_start(xin[:, j, :], x[:, j, :]).then_inc(x_in[j], 16)
            sp.dma_start(vt[:, :], a["vectors"]).then_inc(vec_in, 16)
            load(0, w_in[:, :, 0:BC])
            for j in range(TT // 2, TT):
                sp.dma_start(xin[:, j, :], x[:, j, :]).then_inc(x_in[j], 16)
            load(1, w_in[:, :, BC:2 * BC])
            sp.wait_ge(zeroed, 2)
            gcol = 2 * QK + 2 * VW
            sp.dma_start(gw[:, :, 0:8], w_in[:, :, gcol:gcol + 8]).then_inc(gate_w_in, 16)
            sp.dma_start(gw[:, :, 32:40], w_in[:, :, gcol + 8:gcol + 16]).then_inc(gate_w_in, 16)
            sp.dma_start(bif[0:8, 0:1], a["ml_b_if"][0, 0:8].rearrange("(p o) -> p o", o=1)).then_inc(gate_w_in, 16)
            sp.dma_start(bif[32:40, 0:1], a["ml_b_if"][0, 8:16].rearrange("(p o) -> p o", o=1)).then_inc(gate_w_in, 16)
            for n in range(2, 12):
                load(n, w_in[:, :, n * BC:(n + 1) * BC])
            for n in range(4):
                load(N_MLOUT + n, w_mlout[:, :, n * BC:(n + 1) * BC])

            def ffn(layer, nu, nd):
                wg, wu = rows(a["ffn_w_gate"][layer]), rows(a["ffn_w_up"][layer])
                wd = rows(a["ffn_w_down"][layer])
                with sp.Fori(0, FP) as j:
                    load(0, wg[:, :, bass.ds(j * BC, BC)], slot=0, wait=nu + 2 * j - 1)
                    load(1, wu[:, :, bass.ds(j * BC, BC)], slot=1, wait=nu + 2 * j)
                if layer == 1:
                    def rows_of(b):
                        return wd[:, bass.ds(2 * b, 2), :]
                    with sp.Fori(0, FP // 2) as i:
                        load(0, rows_of(2 * i), c=D, slot=0, wait=nd + 2 * i - 1)
                        load(1, rows_of(2 * i + 1), c=D, slot=1, wait=nd + 2 * i)
                    load(nd + FP - 1, wd[:, FT - 2:FT, :], c=D)
                    return
                with sp.Fori(0, KT) as m:
                    load(0, wd[:, 0:DKT, bass.ds(m * P, P)], c=P, slot=0, wait=nd + 2 * m - 1)
                    load(1, wd[:, DKT:FT, bass.ds(m * P, P)], c=P, slot=1, wait=nd + 2 * m)

            ffn(0, N_UP0, N_DOWN0)
            for n in range(4):
                load(N_U + n, w_lru[:, :, D + n * BC:D + (n + 1) * BC])
            load(N_GB0, w_lru[:, :, 0:BC])
            load(N_GA, w_ga)
            load(N_GX, w_gx)
            for n in range(3):
                load(N_GB1 + n, w_lru[:, :, (n + 1) * BC:(n + 2) * BC])
            for n in range(4):
                load(N_RGOUT + n, w_rgout[:, :, n * BC:(n + 1) * BC])
            ffn(1, N_UP1, N_DOWN1)
            o = out[0].rearrange("(j p) d -> p j d", p=P)
            for i in range(2 * TT):
                j, c = i // 2, slice(S * (i % 2), S * (i % 2 + 1))
                sp.wait_ge(result, i + 1)
                sp.dma_start(o[:, j, c], outT[:, j, c]).then_inc(stored, 16)
            sp.wait_ge(stored, 16 * 2 * TT)

        @block.scalar
        def _(act):
            def hi(n, c=2048, slot=None, landed=None, used=None):
                s = n % 2 if slot is None else slot
                act.wait_ge(raw_in[s], 16 * (n // 2 + 1) if landed is None else landed)
                if used is None:
                    used = n - 1 if n >= 2 else None
                if used is not None:
                    act.wait_ge(w_used, used)
                act.activation(wh[s][:, 0:c], raw[s][:, 0:c], ACT.Copy).then_inc(hi_done, 1)

            def item(bd, i, bk, m0, nm, t0, nt, acc):
                act.wait_ge(*item_ready(bd, i))
                src = bank[bk][:, 0:nm * nt].rearrange("p (m t) -> p m t", m=nm)
                sq = sqy[:, 0:nm * nt].rearrange("p (m t) -> p m t", m=nm)
                act.activation(y[:, m0, t0:t0 + nt] if nm == 1 else y[:, m0:m0 + nm, t0:t0 + nt],
                               bank[bk][:, 0:nt] if nm == 1 else src, ACT.Copy)
                act.wait_ge(item_acc, acc)
                act.activation(sqy[:, 0:nt] if nm == 1 else sq,
                               bank[bk][:, 0:nt] if nm == 1 else src, ACT.Square).then_inc(item_out, 1)

            def items(bd, which, lst):
                for i in which:
                    item(bd, i, *lst[i], accs_before[bd] + 1 + acc_ops(lst[:i]))

            def input_hi(bd, q, g):
                for k in range(KT):
                    act.wait_ge(h_up, 16 * bd + 8 * q + k + 1)
                    act.activation(xsh[:, k, q * HALF:(q + 1) * HALF], h[:, k, q * HALF:(q + 1) * HALF],
                                   ACT.Copy, scale=vt[:, g + k:g + k + 1]).then_inc(x_hi, 1)

            def squares_h(bd, q):
                t = slice(q * HALF, (q + 1) * HALF)
                act.wait_ge(h_up, 16 * bd + 8 * q + 8)
                if bd:
                    act.wait_ge(h_acc, 3 * (2 * bd + q) - 3)
                for k in range(0, KT, 4):
                    act.activation((hsq, hsq_b)[q][:, k:k + 4, :], h[:, k:k + 4, t], ACT.Square).then_inc(h_sq, 1)

            def xs_hi(p, q):
                for k in range(KT):
                    act.wait_ge(x_scaled, 16 * p + 8 * q + k + 1)
                    act.activation(xsh[:, k, q * HALF:(q + 1) * HALF], y[:, k, q * HALF:(q + 1) * HALF],
                                   ACT.Copy).then_inc(x_hi, 1)

            def ffn(layer, nu, nd):
                base = 22 * layer
                for q in range(2):
                    t = slice(q * HALF, (q + 1) * HALF)
                    if q == 0:
                        hi(nu + 2)
                    act.wait_ge(gate_in, base + q + 1)
                    act.activation(sil[:, :, t], sil[:, :, t], ACT.Silu).then_inc(silu, 1)
                    if q == 1:
                        hi(nu + 3)
                    elif layer == 1:
                        for i in range(2 * TT + 2):
                            act.wait_ge(hT_done, i + 1)
                            dst = hT[i // 2] if i < 2 * TT else grow
                            act.activation(dst[:, S * (i % 2):S * (i % 2 + 1)], bank[4 + i % 4],
                                           ACT.Copy).then_inc(hT_out, 1)
                with act.Fori(1, FP) as j:
                    for m in range(2):
                        act.wait_ge(gate_in, base + 2 * j + m + 1)
                        act.activation(sil[:, m, :], sil[:, m, :], ACT.Silu).then_inc(silu, 1)
                    hi(0, slot=0, landed=16 * (nu // 2 + 2) + 16 * j, used=nu + 1 + 2 * j)
                    hi(1, slot=1, landed=16 * (nu // 2 + 2) + 16 * j, used=nu + 2 + 2 * j)
                if layer == 1:
                    with act.Fori(0, (FP - 3) // 2) as i:
                        hi(0, slot=0, landed=16 * (nd // 2 + 2) + 16 * i, used=nd + 1 + 2 * i)
                        hi(1, slot=1, landed=16 * (nd // 2 + 2) + 16 * i, used=nd + 2 + 2 * i)
                    hi(nd + FP - 1)
                    return
                c = DKT * P
                bd = 2 * layer + 1
                with act.Fori(0, 3) as i:
                    for t in range(2):
                        hi(0, c, slot=0, landed=16 * ((nd + 2) // 2 + 1 + t) + 32 * i, used=nd + 1 + 2 * t + 4 * i)
                        hi(1, c, slot=1, landed=16 * ((nd + 2) // 2 + 1 + t) + 32 * i, used=nd + 2 + 2 * t + 4 * i)
                        down_item(bd, i, t)
                hi(nd + 14, c)
                hi(nd + 15, c)
                items(bd, [6], ITEMS_DOWN)

            def down_item(bd, i, t):
                act.wait_ge(w_used, first_block[bd] + 4 * i + 2 * t + 2)
                act.activation(y[:, bass.ds(2 * i + t, 1), :].rearrange("p a t -> p (a t)"), bank[t][:, :], ACT.Copy)
                act.wait_ge(item_acc, accs_before[bd] + 1 + 2 * i + t)
                act.activation(sqy[:, :], bank[t][:, :], ACT.Square).then_inc(item_out, 1)

            def boundary(bd, lst, n, g):
                a_items = [i for i in range(len(lst)) if lst[i][4] == HALF and lst[i][3] == 0]
                b_items = [i for i in range(len(lst)) if lst[i][4] == HALF and lst[i][3] == HALF]
                items(bd, a_items, lst)
                hi(n)
                input_hi(bd, 0, g)
                hi(n + 1)
                items(bd, b_items, lst)
                squares_h(bd, 0)
                input_hi(bd, 1, g)
                squares_h(bd, 1)

            def squares_x(q):
                for j in (2 * q, 2 * q + 1):
                    act.wait_ge(x_in[j], 16)
                    dump = y[:, 2 * j:2 * j + 2, :].rearrange("p a t -> p (a t)") if q == 0 else (
                        hsq[:, 4 * (j - 2):4 * (j - 1), :].rearrange("p a t -> p (a t)"))
                    act.activation(dump, xin[:, j, :], ACT.Square,
                                   accum_out=small[:, 16 + j:17 + j]).then_inc(xsum, 1)

            def copy_x(q):
                for b in (1, 3):
                    act.wait_ge(x_turned, 4 * q + b + 1)
                    act.activation(h[:, 2 * b:2 * b + 2, q * HALF:(q + 1) * HALF],
                                   X_BANKS[q][b].rearrange("p (m t) -> p m t", m=2), ACT.Copy).then_inc(x_out_a, 1)

            squares_x(0)
            act.wait_ge(vec_in, 16)
            copy_x(0)
            hi(0)
            xs_hi(0, 0)
            hi(1)
            squares_x(1)
            copy_x(1)
            xs_hi(0, 1)
            hi(2)
            act.wait_ge(gates_mm, 1)
            act.wait_ge(gates_dve, 1)
            act.activation(tg[:, :], SUM[0][0:40, :], ACT.Tanh, bias=bif[0:40, 1:2], scale=1.0 / GATE_CAP).then_inc(gates_act, 1)
            act.wait_ge(gates_act, 1)
            act.activation(ge[0:8, :], tg[32:40, :], ACT.Exp, scale=-GATE_CAP).then_inc(gates_act, 1)
            hi(3)
            act.wait_ge(gates_dve, 2)
            act.activation(gl_[0:8, :], gy[0:8, :], ACT.Ln).then_inc(gates_act, 1)
            act.wait_ge(gates_act, 3)
            act.activation(gi[0:8, :], gl_[0:8, :], ACT.Exp, scale=-1.0).then_inc(gates_act, 1)
            hi(4)
            act.wait_ge(gates_dve, 5)
            act.activation(gem[0:8, :], gm[0:8, :], ACT.Exp, scale=-2.0).then_inc(gates_act, 1)
            for n in range(5, 10):
                hi(n)
            OFF = [0, 512, 1024, 896]

            def decays(t):
                act.wait_ge(mask_added, t + 1)
                if t:
                    act.wait_ge(weighed, t)
                for i in range(TT):
                    act.activation(dec[:, OFF[i]:OFF[i] + P], masked[t % 2][:, i, :], ACT.Exp,
                                   bias=ct[:, i, t:t + 1])
                for i in range(TT - 1):
                    last = act.activation(dec[:, OFF[i] + P:OFF[i] + S - P * i],
                                          SUM[0][:, (i + 1) * P:S], ACT.Exp, bias=ct[:, i, t:t + 1])
                last.then_inc(decay_done, 1)

            def square_nums(t):
                act.wait_ge(numer_done, t + 1)
                if t >= 2:
                    act.wait_ge(denom_done, t - 1)
                for j in range(TT):
                    src = ROW[j // 2][:, (j % 2) * (DV + 1):(j % 2) * (DV + 1) + DV]
                    last = act.activation(hsq[:, j, 0:DV], src, ACT.Square, scale=float(DV) ** -0.5,
                                          accum_out=den[:, t % 2, 0, j:j + 1])
                last.then_inc(numer_sq, 1)

            def out_gate(t):
                act.wait_ge(*in_ready(16 + t))
                act.activation(sigo[:, t, :], SUM[1], ACT.Sigmoid).then_inc(ogate_out, 1)

            def mix_hi(t0, t1):
                act.wait_ge(score, HEADS)
                for t in range(t0, t1):
                    act.wait_ge(mixed, t + 1)
                    act.activation(mlh[:, t, :], y[:, t, :], ACT.Copy).then_inc(mixed_hi, 1)

            act.wait_ge(gates_kept, 1)
            for t in range(HEADS):
                decays(t)
                if t >= 1:
                    square_nums(t - 1)
                if t in (2, 4, 6):
                    hi(9 + t // 2)
                if t < HEADS - 1:
                    out_gate(t)
            mix_hi(0, 4)
            square_nums(HEADS - 1)
            out_gate(HEADS - 1)
            mix_hi(4, 8)
            hi(13)
            items(0, [0, 1], ITEMS_OUT)
            hi(14)
            items(0, [2, 3], ITEMS_OUT)
            hi(15)
            boundary(0, ITEMS_OUT, N_UP0, V_PREFFN)
            ffn(0, N_UP0, N_DOWN0)
            boundary(1, ITEMS_DOWN, N_U, V_PREMIX + KT)
            CW3 = V_CONVW + 3 * KT

            def last_tap(k0, nk, t0, nt, i):
                act.wait_ge(u_out, i + 1)
                for m in range(nk):
                    k = k0 + m
                    last = act.activation(uc[:, k, t0:t0 + nt], upad[:, k, CONV - 1 + t0:CONV - 1 + t0 + nt],
                                          ACT.Identity, scale=vt[:, CW3 + k:CW3 + k + 1],
                                          bias=vt[:, V_CONVB + k:V_CONVB + k + 1])
                last.then_inc(uc_out, 1)

            def u_hi(k):
                act.wait_ge(conv, 3 * k + 3)
                act.activation(uch[:, k, :], uc[:, k, :], ACT.Copy).then_inc(u_rounded, 1)

            hi(N_U + 2)
            last_tap(0, 2, 0, HALF, 0)
            last_tap(2, 2, 0, HALF, 1)
            hi(N_U + 3)
            last_tap(0, 2, HALF, HALF, 2)
            last_tap(2, 2, HALF, HALF, 3)
            act.wait_ge(lam_v, 1)
            act.activation(lamc[:, 1, :], lamc[:, 0, :], ACT.Exp, scale=-1.0).then_inc(lam_a, 1)
            act.wait_ge(lam_v, 2)
            act.activation(lamc[:, 3, :], lamc[:, 2, :], ACT.Ln).then_inc(lam_a, 1)
            u_hi(0)
            hi(N_GB0)
            u_hi(1)
            for k in (4, 5):
                last_tap(k, 1, 0, S, k)
            for k in (2, 3):
                u_hi(k)
            hi(N_GA)
            for k in (6, 7):
                last_tap(k, 1, 0, S, k)
            for k in range(4, 8):
                if k == 6:
                    hi(N_GX)
                u_hi(k)

            def gelu(g):
                for m in range(2):
                    act.wait_ge(branch_in, 2 * g + m + 1)
                    act.activation(gel[:, 2 * g + m, :], gel[:, 2 * g + m, :], ACT.Gelu_apprx_tanh).then_inc(branch_out, 1)

            def gates(b):
                for m in range(4 * b, 4 * b + 4):
                    act.wait_ge(*ga_ready(m, 0))
                    act.activation(y[:, m, :], gate_bank(m, 0)[:, :], ACT.Sigmoid,
                                   bias=vt[:, V_BA + m:V_BA + m + 1]).then_inc(rgate_out, 1)
                for m in range(4 * b, 4 * b + 4):
                    act.wait_ge(*ga_ready(m, 1))
                    act.activation(sgi[:, m, :], gate_bank(m, 1)[:, :], ACT.Sigmoid,
                                   bias=vt[:, V_BX + m:V_BX + m + 1]).then_inc(rgate_out, 1)

            def decay(b):
                act.wait_ge(rgate_out, KT * b + 4)
                for m in range(4 * b, 4 * b + 4):
                    act.activation(la[:, m, :], y[:, m, :], ACT.Exp, scale=lamc[:, 4, m:m + 1])
                    act.activation(lt[:, m, :], y[:, m, :], ACT.Tanh, scale=lamc[:, 5, m:m + 1]).then_inc(a_done, 1)

            def sqrts(b):
                act.wait_ge(one_a2, 4 * b + 4)
                act.activation(lt[:, 4 * b:4 * b + 4, :], lt[:, 4 * b:4 * b + 4, :], ACT.Sqrt).then_inc(roots, 1)

            def out_hi(lo_tile, hi_tile):
                for m in range(lo_tile, hi_tile):
                    act.wait_ge(rg_out, m + 1)
                    act.activation(rgh[:, m, :], lt[:, m, :], ACT.Copy).then_inc(rg_out_hi, 1)

            gates(0)
            hi(N_GB1)
            gates(1)
            hi(N_GB1 + 1)
            act.wait_ge(lam_v, 3)
            decay(0)
            decay(1)
            sqrts(0)
            hi(N_GB1 + 2)
            sqrts(1)
            hi(N_RGOUT)
            for g in range(3):
                gelu(g)
            out_hi(0, 6)
            gelu(3)
            out_hi(6, 8)
            hi(N_RGOUT + 1)
            items(2, [0, 1], ITEMS_OUT)
            hi(N_RGOUT + 2)
            items(2, [2, 3], ITEMS_OUT)
            hi(N_RGOUT + 3)
            boundary(2, ITEMS_OUT, N_UP1, V_PREFFN + KT)
            ffn(1, N_UP1, N_DOWN1)
            squares = [raw[1][:, S * i:S * (i + 1)] for i in range(4)] + [sil[:, i, :] for i in range(2)] + [
                prod[:, i, :] for i in range(2)]
            for i in range(2 * TT):
                act.wait_ge(tile_done, i + 1)
                act.activation(squares[i], bank[i], ACT.Square, scale=float(D) ** -0.5,
                               accum_out=small[:, 16 + i:17 + i]).then_inc(tile_sq, 1)

        @block.gpsimd
        def _(pool):
            def root(dst, src, n, mean, mean_at, done):
                pool.wait_ge(mean, mean_at)
                pool.tensor_tensor(dst, src, expo[:, 0:n], ALU.pow).then_inc(done, 1)

            def ysq(bd, q):
                root(small[:, 4 + 2 * q:6 + 2 * q], small[:, 2 * q:2 * q + 2], 2, ymean, 2 * bd + q + 1, yroot)

            def hsqr(p, q):
                root(small[:, 12 + 2 * q:14 + 2 * q], small[:, 8 + 2 * q:10 + 2 * q], 2, hmean, 2 * p + q + 1, hroot)

            def residual(bd, q):
                for k in range(KT):
                    pool.wait_ge(yscaled, 16 * bd + 8 * q + k + 1)
                    t = slice(q * HALF, (q + 1) * HALF)
                    pool.tensor_tensor(h[:, k, t], h[:, k, t], y[:, k, t], ALU.add).then_inc(h_up, 1)

            def mix_lo(hi_at, src, h_part, l_part, done):
                for k in LO_POOL:
                    pool.wait_ge(hi_at, k + 1)
                    pool.tensor_tensor(l_part[:, k, :], src[:, k, :], h_part[:, k, :].bitcast(F32),
                                       ALU.subtract).then_inc(done, 1)

            def xs_lo(p, q):
                for k in range(1, KT, 2):
                    pool.wait_ge(x_hi, 16 * p + 8 * q + k + 1)
                    t = slice(q * HALF, (q + 1) * HALF)
                    pool.tensor_tensor(xsl[:, k, t], y[:, k, t], xsh[:, k, t].bitcast(F32),
                                       ALU.subtract).then_inc(x0_lo_p, 1)

            def boundary(bd):
                ysq(bd, 0)
                residual(bd, 0)
                ysq(bd, 1)
                residual(bd, 1)
                hsqr(bd + 1, 0)
                hsqr(bd + 1, 1)

            pool.memset(gw[:, :, :], 0.0).then_inc(zeroed, 1)
            pool.memset(bif[:, :], 0.0).then_inc(zeroed, 1)
            pool.memset(ident[:, :], 0.0).then_inc(consts, 1)
            pool.memset(ones[:, :], 1.0).then_inc(consts, 1)
            pool.memset(expo[:, :], -0.5).then_inc(consts, 1)
            pool.memset(mask[:, :], 0.0).then_inc(consts, 1)
            pool.memset(sel[:, :, :], 0.0).then_inc(consts, 1)
            pool.memset(v[:, :, :, DV:DV + 1], 1.0).then_inc(consts, 1)
            pool.wait_ge(consts, 6)
            pool.affine_select(out=ident[:, :], in_=ident[:, :], compare_op=ALU.not_equal, fill=1.0, base=0,
                               pattern=[[-1, P]], channel_multiplier=1).then_inc(consts, 1)
            pool.affine_select(out=mask[:, :], in_=mask[:, :], compare_op=ALU.is_ge, fill=NEG, base=0,
                               pattern=[[1, P]], channel_multiplier=-1).then_inc(consts, 1)
            pool.affine_select(out=sel[:, :, :], in_=sel[:, :, :], compare_op=ALU.not_equal, fill=1.0, base=0,
                               pattern=[[-1, HEADS], [0, P]], channel_multiplier=1).then_inc(consts, 1)
            hsqr(0, 0)
            xs_lo(0, 0)
            hsqr(0, 1)
            xs_lo(0, 1)
            pool.wait_ge(x0_lo_p, 8)
            for e in range(2):
                if e:
                    pool.wait_ge(k_zeroed, 1)
                o = DK * (1 - e)
                pool.memset(kT[o:o + DK, e:HEADS:2, :], 0.0).then_inc(k_zeroed, 1)
            pool.wait_ge(k_zeroed, 2)
            for t in range(HEADS):
                pool.wait_ge(denom_done, t + 1)
                pool.tensor_tensor(den[:, t % 2, 3, :], den[:, t % 2, 2, :], expo[:, 0:TT],
                                   ALU.pow).then_inc(denom_root, 1)
            mix_lo(mixed_hi, y, mlh, mll, mixed_lo_p)
            boundary(0)
            boundary(1)

            def u_lo(k):
                pool.wait_ge(u_rounded, k + 1)
                pool.tensor_tensor(ucl[:, k, :], uc[:, k, :], uch[:, k, :].bitcast(F32), ALU.subtract).then_inc(u_low, 1)

            for k in range(KT):
                u_lo(k)
            for m in range(KT):
                pool.wait_ge(rgate_out, gate_index(m, 1) + 1)
                pool.wait_ge(u_low, m + 1)
                pool.tensor_tensor(uc[:, m, :], uc[:, m, :], sgi[:, m, :], ALU.mult).then_inc(gated_u, 1)
            for m in range(KT):
                pool.wait_ge(roots, m // 4 + 1)
                pool.wait_ge(gated_u, m + 1)
                pool.tensor_tensor(uc[:, m, :], lt[:, m, :], uc[:, m, :], ALU.mult).then_inc(scan_in, 1)
            mix_lo(rg_out_hi, lt, rgh, rgl, rg_out_lo_p)
            boundary(2)
            for j in range(TT):
                root(small[:, 28 + j:29 + j], small[:, 24 + j:25 + j], 1, tile_mean, j + 1, tile_root)

        @block.vector
        def _(dve):
            def lo(n, c=2048, slot=None, count=None):
                s = n % 2 if slot is None else slot
                dve.wait_ge(hi_done, n + 1 if count is None else count)
                dve.tensor_tensor(wl[s][:, 0:c], raw[s][:, 0:c], wh[s][:, 0:c].bitcast(F32),
                                  ALU.subtract).then_inc(lo_done, 1)

            def mix_lo(k, hi_at, src, h_part, l_part, done):
                dve.wait_ge(hi_at, k + 1)
                dve.tensor_tensor(l_part[:, k, :], src[:, k, :], h_part[:, k, :].bitcast(F32),
                                  ALU.subtract).then_inc(done, 1)

            def mean(dst, src, done):
                dve.tensor_scalar(dst, src, 1.0 / D, EPS, ALU.mult, ALU.add).then_inc(done, 1)

            def to_diag(col, wait, at, done, free, free_at):
                dve.wait_ge(wait, at)
                if free is not None:
                    dve.wait_ge(free, free_at)
                dve.tensor_scalar(diag[:, 0, :], ident[:, :], small[:, col:col + 1], None, ALU.mult)
                dve.tensor_scalar(diag[:, 1, :], ident[:, :], small[:, col + 1:col + 2], None, ALU.mult).then_inc(done, 1)

            def clear_acc(bd):
                if bd:
                    dve.wait_ge(hsum, 2 * bd)
                dve.memset(accy[:, :], 0.0).then_inc(item_acc, 1)

            def accumulate(bd, i, lst):
                _, m0, nm, t0, nt = lst[i]
                dve.wait_ge(item_out, items_before[bd] + i + 1)
                for m in range(nm):
                    dve.wait_ge(item_acc, accs_before[bd] + 1 + acc_ops(lst[:i]) + m)
                    dve.tensor_tensor(accy[:, t0:t0 + nt], accy[:, t0:t0 + nt], sqy[:, m * nt:(m + 1) * nt],
                                      ALU.add).then_inc(item_acc, 1)

            def ymeans(bd, q):
                dve.wait_ge(ysum, 2 * bd + q + 1)
                mean(small[:, 2 * q:2 * q + 2], SUM[q][:, 0:2], ymean)

            def scale_y(bd, q, g):
                dve.wait_ge(yrow, 2 * bd + q + 1)
                t = slice(q * HALF, (q + 1) * HALF)
                for k in range(KT):
                    dve.scalar_tensor_tensor(out=y[:, k, t], in0=y[:, k, t], scalar=vt[:, g + k:g + k + 1],
                                             in1=ROW[q][:, 0:HALF], op0=ALU.mult, op1=ALU.mult).then_inc(yscaled, 1)

            def hmeans(bd, q):
                dve.wait_ge(hsum, 2 * bd + q + 1)
                mean(small[:, 8 + 2 * q:10 + 2 * q], SUM[q][:, 4:6], hmean)

            def xs_build(p, q, g, n=None):
                dve.wait_ge(hrow, 2 * p + q + 1)
                t = slice(q * HALF, (q + 1) * HALF)

                def low(k):
                    dve.wait_ge(x_hi, 16 * p + 8 * q + k + 1)
                    dve.tensor_tensor(xsl[:, k, t], y[:, k, t], xsh[:, k, t].bitcast(F32),
                                      ALU.subtract).then_inc(x0_lo_v, 1)
                for k in range(KT):
                    dve.scalar_tensor_tensor(out=y[:, k, t], in0=h[:, k, t], scalar=vt[:, g + k:g + k + 1],
                                             in1=ROW[q][:, HALF:S], op0=ALU.mult, op1=ALU.mult).then_inc(x_scaled, 1)
                    if k == 2 and n is not None:
                        lo(n)
                    if k >= 2 and k % 2 == 0:
                        low(k - 2)
                low(6)

            def next_input(bd, q, g_post, g_pre, lag, n=None):
                dve.wait_ge(yrow, 2 * bd + q + 1)
                t = slice(q * HALF, (q + 1) * HALF)
                for k in range(KT + lag):
                    if k < KT:
                        dve.scalar_tensor_tensor(out=y[:, k, t], in0=y[:, k, t], scalar=vt[:, g_post + k:g_post + k + 1],
                                                 in1=ROW[q][:, 0:HALF], op0=ALU.mult, op1=ALU.mult).then_inc(yscaled, 1)
                    if k == lag - 1 and n is not None:
                        lo(n)
                    if k >= lag:
                        i = k - lag
                        dve.wait_ge(x_hi, 16 * (bd + 1) + 8 * q + i + 1)
                        dve.scalar_tensor_tensor(out=xsl[:, i, t], in0=h[:, i, t], scalar=vt[:, g_pre + i:g_pre + i + 1],
                                                 in1=xsh[:, i, t].bitcast(F32), op0=ALU.mult,
                                                 op1=ALU.subtract).then_inc(x_lo, 1)

            def add_up(bd, q):
                at = 3 * (2 * bd + q)
                sq = (hsq, hsq_b)[q]
                dve.wait_ge(h_sq, 4 * bd + 2 * q + 2)
                dve.tensor_tensor(sq[:, 0:4, :], sq[:, 0:4, :], sq[:, 4:8, :], ALU.add).then_inc(h_acc, 1)
                dve.wait_ge(h_acc, at + 1)
                dve.tensor_tensor(sq[:, 0:2, :], sq[:, 0:2, :], sq[:, 2:4, :], ALU.add).then_inc(h_acc, 1)
                dve.wait_ge(h_acc, at + 2)
                dve.tensor_tensor(accy[:, q * HALF:(q + 1) * HALF], sq[:, 0, :], sq[:, 1, :],
                                  ALU.add).then_inc(h_acc, 1)

            def row_copy(bd, q):
                dve.wait_ge(hrow, 2 * bd + q + 3)
                dve.tensor_copy(hrow_s[:, q * HALF:(q + 1) * HALF], ROW[q][:, HALF:S]).then_inc(row_in, 1)

            def boundary(bd, lst, n, g_post, g_pre):
                a_items = [i for i in range(len(lst)) if lst[i][4] == HALF and lst[i][3] == 0]
                b_items = [i for i in range(len(lst)) if lst[i][4] == HALF and lst[i][3] == HALF]
                for i in a_items:
                    accumulate(bd, i, lst)
                ymeans(bd, 0)
                to_diag(4, yroot, 2 * bd + 1, ydiag, hrow, 2 * bd + 2)
                next_input(bd, 0, g_post, g_pre, KT, n)
                lo(n + 1)
                for i in b_items:
                    accumulate(bd, i, lst)
                ymeans(bd, 1)
                to_diag(6, yroot, 2 * bd + 2, ydiag, yrow, 2 * bd + 1)
                next_input(bd, 1, g_post, g_pre, 3)
                add_up(bd, 0)
                hmeans(bd, 0)
                add_up(bd, 1)
                to_diag(12, hroot, 2 * bd + 3, hdiag, yrow, 2 * bd + 2)
                row_copy(bd, 0)
                hmeans(bd, 1)
                lo(n + 2)
                to_diag(14, hroot, 2 * bd + 4, hdiag, hrow, 2 * bd + 3)

            def ffn(layer, nu, nd):
                base = 22 * layer

                row = 4 * layer

                def rounded(dst_h, dst_l, src, n):
                    dve.wait_ge(prod_done, n)
                    dve.tensor_copy(dst_h, src).then_inc(act_h, 1)
                    dve.wait_ge(act_h, n)
                    dve.tensor_tensor(dst_l, src, dst_h.bitcast(F32), ALU.subtract).then_inc(act_l, 1)

                def scaled(q):
                    t = slice(q * HALF, (q + 1) * HALF)
                    gate, up = (bank[2 * q + i][:, :].rearrange("p (m t) -> p m t", m=2) for i in range(2))
                    r = hrow_s[:, None, t].to_broadcast([P, 2, HALF])
                    dve.wait_ge(*gate_ready(layer, 0, 0, q))
                    dve.wait_ge(row_in, row + q + 1)
                    if layer:
                        dve.wait_ge(act_l, base)
                    dve.tensor_tensor(sil[:, :, t], gate, r, ALU.mult).then_inc(gate_in, 1)
                    dve.wait_ge(*gate_ready(layer, 1, 0, q))
                    dve.tensor_tensor(prod[:, :, t], up, r, ALU.mult).then_inc(up_in, 1)

                def half(q):
                    t = slice(q * HALF, (q + 1) * HALF)
                    n = base + q + 1
                    dve.wait_ge(up_in, n)
                    dve.wait_ge(silu, n)
                    dve.tensor_tensor(prod[:, :, t], sil[:, :, t], prod[:, :, t], ALU.mult).then_inc(prod_done, 1)
                    rounded(acth[:, 0:2, t], actl[:, 0:2, t], prod[:, :, t], n)

                scaled(0)
                row_copy(2 * layer, 1)
                if layer == 1:
                    dve.wait_ge(h_acc, 18)
                    dve.tensor_tensor(gdiag.rearrange("p (k t) -> p k t", k=KT), ident[:, None, :].to_broadcast([P, KT, P]),
                                      vt[:, V_POSTFFN + KT:V_POSTFFN + 2 * KT, None].to_broadcast([P, KT, P]),
                                      ALU.mult).then_inc(gdiag_done, 1)
                scaled(1)
                half(0)
                half(1)
                lo(nu + 3)
                with dve.Fori(1, FP) as j:
                    for m in range(2):
                        dve.wait_ge(*gate_ready(layer, 0, j, m))
                        dve.wait_ge(act_l, base + 2 * j)
                        dve.tensor_tensor(sil[:, m, :], bank[m][:, :], hrow_s[:, :], ALU.mult).then_inc(gate_in, 1)
                    lo(0, slot=0, count=nu + 3 + 2 * j)
                    for m in range(2):
                        n = base + 2 * j + m + 1
                        dve.wait_ge(*gate_ready(layer, 1, j, m))
                        dve.tensor_tensor(prod[:, m, :], bank[2 + m][:, :], hrow_s[:, :], ALU.mult).then_inc(up_in, 1)
                        dve.wait_ge(up_in, n)
                        dve.wait_ge(silu, n)
                        dve.tensor_tensor(prod[:, m, :], sil[:, m, :], prod[:, m, :], ALU.mult).then_inc(prod_done, 1)
                        rounded(acth[:, bass.ds(2 * j + m, 1), :].rearrange("p a t -> p (a t)"),
                                actl[:, bass.ds(2 * j + m, 1), :].rearrange("p a t -> p (a t)"), prod[:, m, :], n)
                    lo(0, slot=1, count=nu + 4 + 2 * j)
                if layer == 1:
                    with dve.Fori(0, (FP - 3) // 2) as i:
                        lo(0, slot=0, count=nd + 3 + 2 * i)
                        lo(0, slot=1, count=nd + 4 + 2 * i)
                    lo(nd + FP - 1)
                    return
                bd = 2 * layer + 1
                clear_acc(bd)
                c = DKT * P
                with dve.Fori(0, 6) as m:
                    lo(0, c, slot=0, count=nd + 3 + 2 * m)
                    lo(0, c, slot=1, count=nd + 4 + 2 * m)
                    dve.wait_ge(item_out, items_before[bd] + 1 + m)
                    dve.wait_ge(item_acc, accs_before[bd] + 1 + m)
                    dve.tensor_tensor(accy[:, :], accy[:, :], sqy[:, :], ALU.add).then_inc(item_acc, 1)
                lo(nd + 14, c)
                lo(nd + 15, c)
                accumulate(bd, 6, ITEMS_DOWN)

            def copy_x(q):
                for b in (0, 2):
                    dve.wait_ge(x_turned, 4 * q + b + 1)
                    dve.tensor_copy(h[:, 2 * b:2 * b + 2, q * HALF:(q + 1) * HALF],
                                    X_BANKS[q][b].rearrange("p (m t) -> p m t", m=2)).then_inc(x_out_v, 1)

            def mean_x(q):
                dve.wait_ge(xsum, 2 * q + 2)
                mean(small[:, 8 + 2 * q:10 + 2 * q], small[:, 16 + 2 * q:18 + 2 * q], hmean)

            mean_x(0)
            dve.wait_ge(consts, 9)
            to_diag(12, hroot, 1, hdiag, None, 0)
            copy_x(0)
            dve.wait_ge(vec_in, 16)
            dve.wait_ge(x_out_a, 2)
            dve.wait_ge(x_out_v, 2)
            xs_build(0, 0, V_PREMIX, 0)
            copy_x(1)
            lo(1)
            mean_x(1)
            to_diag(14, hroot, 2, hdiag, hrow, 1)
            dve.wait_ge(x_out_a, 4)
            dve.wait_ge(x_out_v, 4)
            xs_build(0, 1, V_PREMIX)
            dve.wait_ge(gate_w_in, 64)
            dve.tensor_scalar(bif[0:40, 1:2], bif[0:40, 0:1], 1.0 / GATE_CAP, None, ALU.mult).then_inc(gates_dve, 1)

            def q_out(i):
                dve.wait_ge(*in_ready(i))
                q, m0 = i // 2, 2 * (i % 2)
                dve.tensor_scalar(qT[:, m0:m0 + 2, q * HALF:(q + 1) * HALF],
                                  bank[i][:, :].rearrange("p (m t) -> p m t", m=2), float(DK) ** -0.5, None,
                                  ALU.mult).then_inc(proj_out, 1)

            for i in range(3):
                q_out(i)
            lo(2)
            q_out(3)
            lo(3)
            G = HEADS
            dve.wait_ge(gates_act, 2)
            dve.tensor_scalar(gli[0:G, :], tg[0:G, :], GATE_CAP, None, ALU.mult)
            dve.tensor_scalar(gy[0:G, :], ge[0:G, :], 1.0, None, ALU.add).then_inc(gates_dve, 1)
            dve.memset(gz[0:G, :], 0.0)
            dve.wait_ge(gates_dve, 2)
            dve.scalar_tensor_tensor(out=gd[0:G, :], in0=gy[0:G, :], scalar=-1.0, in1=ge[0:G, :],
                                     op0=ALU.add, op1=ALU.subtract).then_inc(gates_dve, 1)
            dve.wait_ge(gates_act, 4)
            dve.wait_ge(gates_dve, 3)
            dve.tensor_tensor(gd[0:G, :], gd[0:G, :], gi[0:G, :], ALU.mult).then_inc(gates_turned, 1)
            dve.wait_ge(gates_turned, 1)
            dve.tensor_tensor(glf[0:G, :], gd[0:G, :], gl_[0:G, :], ALU.subtract).then_inc(gates_turned, 1)
            dve.wait_ge(gates_turned, 2)
            dve.tensor_tensor_scan(out=gB[0:G, :], data0=glf[0:G, :], data1=gz[0:G, :], initial=0.0,
                                   op0=ALU.add, op1=ALU.add).then_inc(gates_dve, 1)
            dve.tensor_tensor_scan(out=gm[0:G, :], data0=glf[0:G, :], data1=gli[0:G, :], initial=NEG,
                                   op0=ALU.add, op1=ALU.max).then_inc(gates_dve, 1)
            dve.wait_ge(gates_dve, 5)
            dve.tensor_tensor(z[:, :], gB[0:G, :], gm[0:G, :], ALU.subtract)
            dve.tensor_tensor(gc[0:G, :], gli[0:G, :], gB[0:G, :], ALU.subtract).then_inc(gates_dve, 1)
            dve.wait_ge(k_zeroed, 2)
            for i in range(4, 8):
                dve.wait_ge(*in_ready(i))
                for e in range(2):
                    p = slice(DK * e, DK * (e + 1))
                    last = dve.tensor_copy(kT[p, 2 * (i - 4) + e, :], bank[i - 4][p, :])
                last.then_inc(proj_out, 1)
                if i % 2:
                    lo(4 + (i - 5) // 2)
            dve.wait_ge(gates_turned, 3)
            dve.tensor_copy(ct[:, :, :], SUM[1][:, 0:32].rearrange("p (j h) -> p j h", j=TT))
            dve.tensor_copy(emt[:, :, :], SUM[1][:, 32:64].rearrange("p (j h) -> p j h", j=TT)).then_inc(gates_kept, 1)
            for i in range(8, 16):
                dve.wait_ge(*in_ready(i))
                blk, b = (i - 8) // 2, (i - 8) % 2
                for j in range(2):
                    last = dve.tensor_copy(v[:, 2 * b + j, 2 * blk:2 * blk + 2, 0:DV],
                                           bank[i % 4][:, j * 256:(j + 1) * 256].rearrange("p (h d) -> p h d", h=2))
                last.then_inc(proj_out, 1)
                if b:
                    lo(6 + blk)
            OFF = [0, 512, 1024, 896]

            def add_mask(t):
                dve.wait_ge(row_done, t + 1)
                if t >= 2:
                    dve.wait_ge(decay_done, t - 1)
                dve.tensor_tensor(masked[t % 2][:, :, :], SUM[0][:, :].rearrange("p (j l) -> p j l", j=TT),
                                  mask[:, None, :].to_broadcast([P, TT, P]), ALU.add).then_inc(mask_added, 1)

            def weigh(t):
                dve.wait_ge(decay_done, t + 1)
                dve.wait_ge(score, t + 1)
                if t >= 2:
                    dve.wait_ge(numer_done, t - 1)
                dve.tensor_tensor(pt[t % 2][:, 0:512], dec[:, 0:512], M[0][:, :], ALU.mult)
                dve.tensor_tensor(pt[t % 2][:, 512:1024], dec[:, 512:1024], M[1][:, :], ALU.mult)
                dve.tensor_tensor(pt[t % 2][:, 1024:1280], dec[:, 1024:1280], M[2][:, 0:256],
                                  ALU.mult).then_inc(weighed, 1)

            def denominators(t):
                dve.wait_ge(numer_sq, t + 1)
                if t >= 2:
                    dve.wait_ge(normalised, t - 1)
                d = den[:, t % 2]
                for b in range(2):
                    src = ROW[b][:, 0:2 * (DV + 1)].rearrange("p (j c) -> p j c", j=2)[:, :, DV]
                    last = dve.tensor_copy(d[:, 1, 2 * b:2 * b + 2], src)
                last.then_inc(den_step, 1)
                dve.wait_ge(den_step, 3 * t + 1)
                dve.tensor_tensor(d[:, 1, :], d[:, 1, :], d[:, 1, :], ALU.mult).then_inc(den_step, 1)
                dve.wait_ge(den_step, 3 * t + 2)
                dve.tensor_tensor(d[:, 1, :], d[:, 1, :], emt[:, :, t], ALU.max).then_inc(den_step, 1)
                dve.wait_ge(den_step, 3 * t + 3)
                dve.scalar_tensor_tensor(out=d[:, 2, :], in0=d[:, 1, :], scalar=EPS, in1=d[:, 0, :],
                                         op0=ALU.mult, op1=ALU.add).then_inc(denom_done, 1)

            def normalise(t):
                dve.wait_ge(denom_root, t + 1)
                if t >= 2:
                    dve.wait_ge(turned, t - 1)
                for j in range(TT):
                    src = ROW[j // 2][:, (j % 2) * (DV + 1):(j % 2) * (DV + 1) + DV]
                    last = dve.tensor_scalar(nsc[t % 2][:, j, :], src, den[:, t % 2, 3, j:j + 1], None, ALU.mult)
                last.then_inc(normalised, 1)

            def gate_out(t):
                dve.wait_ge(turned, t + 1)
                dve.wait_ge(ogate_out, t + 1)
                dve.scalar_tensor_tensor(out=y[:, t, :], in0=M[3][:, :], scalar=vt[:, V_HEAD + t:V_HEAD + t + 1],
                                         in1=sigo[:, t, :], op0=ALU.mult, op1=ALU.mult).then_inc(mixed, 1)

            for t in range(HEADS + 2):
                if t < HEADS:
                    add_mask(t)
                    weigh(t)
                if t == HEADS:
                    mix_lo(LO_DVE[0], mixed_hi, y, mlh, mll, mixed_lo_v)
                if 1 <= t <= HEADS:
                    denominators(t - 1)
                    normalise(t - 1)
                if t in (2, 4, 6):
                    lo(9 + t // 2)
                if t >= 2:
                    gate_out(t - 2)
                if t == HEADS:
                    mix_lo(LO_DVE[1], mixed_hi, y, mlh, mll, mixed_lo_v)
            mix_lo(LO_DVE[2], mixed_hi, y, mlh, mll, mixed_lo_v)
            mix_lo(LO_DVE[3], mixed_hi, y, mlh, mll, mixed_lo_v)
            lo(13)
            clear_acc(0)
            for i in range(4):
                if i % 2:
                    lo(14 + i // 2)
                accumulate(0, i, ITEMS_OUT)
            boundary(0, ITEMS_OUT, N_UP0, V_POSTMIX, V_PREFFN)
            ffn(0, N_UP0, N_DOWN0)
            boundary(1, ITEMS_DOWN, N_U, V_POSTFFN, V_PREMIX + KT)
            def u_in(k0, nk, t0, nt, bk, i):
                dve.wait_ge(*u_ready(i))
                dve.wait_ge(row_in, 3 if t0 + nt == HALF else 4)
                if nk == 1:
                    dve.tensor_tensor(upad[:, k0, CONV - 1:CONV - 1 + S], bank[bk][:, :], hrow_s[:, :],
                                      ALU.mult).then_inc(u_out, 1)
                else:
                    dve.tensor_tensor(upad[:, k0:k0 + nk, CONV - 1 + t0:CONV - 1 + t0 + nt],
                                      bank[bk][:, :].rearrange("p (m t) -> p m t", m=2),
                                      hrow_s[:, None, t0:t0 + nt].to_broadcast([P, nk, nt]), ALU.mult).then_inc(u_out, 1)

            def gb_row(g, b0):
                for m in range(2):
                    dve.wait_ge(*gb_ready(g, m))
                    dve.tensor_tensor(gel[:, 2 * g + m, :], bank[b0 + m][:, :], hrow_s[:, :],
                                      ALU.mult).then_inc(branch_in, 1)

            def convolve(k, ready):
                dve.wait_ge(uc_out, ready)
                for j in range(CONV - 1):
                    if j:
                        dve.wait_ge(conv, 3 * k + j)
                    w = V_CONVW + j * KT + k
                    dve.scalar_tensor_tensor(out=uc[:, k, :], in0=upad[:, k, j:j + S], scalar=vt[:, w:w + 1],
                                             in1=uc[:, k, :], op0=ALU.mult, op1=ALU.add).then_inc(conv, 1)

            u_in(0, 2, 0, HALF, 0, 0)
            u_in(2, 2, 0, HALF, 1, 1)
            row_copy(1, 1)
            u_in(0, 2, HALF, HALF, 2, 2)
            u_in(2, 2, HALF, HALF, 3, 3)
            lo(N_U + 3)
            dve.scalar_tensor_tensor(out=lamc[:, 0, :], in0=vt[:, V_LAM:V_LAM + KT], scalar=-1.0,
                                     in1=vt[:, V_LAM:V_LAM + KT], op0=ALU.mult, op1=ALU.max).then_inc(lam_v, 1)
            dve.wait_ge(lam_a, 1)
            dve.tensor_scalar(lamc[:, 2, :], lamc[:, 1, :], 1.0, None, ALU.add).then_inc(lam_v, 1)
            dve.memset(upad[:, :, 0:CONV - 1], 0.0).then_inc(pad_zeroed, 1)
            dve.wait_ge(pad_zeroed, 1)
            for k in range(KT):
                if k == 3:
                    lo(N_GB0)
                if k == 4:
                    u_in(4, 1, 0, S, 0, 4)
                    u_in(5, 1, 0, S, 1, 5)
                if k == 6:
                    u_in(6, 1, 0, S, 2, 6)
                    u_in(7, 1, 0, S, 3, 7)
                    lo(N_GA)
                if k == 7:
                    lo(N_GX)
                convolve(k, 3 if k < 2 else 4 if k < 4 else k + 1)
            gb_row(0, 0)
            dve.wait_ge(lam_a, 2)
            dve.reciprocal(lamc[:, 4, :], lamc[:, 2, :])
            dve.scalar_tensor_tensor(out=lamc[:, 5, :], in0=lamc[:, 2, :], scalar=-1.0, in1=lamc[:, 1, :],
                                     op0=ALU.add, op1=ALU.subtract).then_inc(pad_zeroed, 1)
            dve.wait_ge(pad_zeroed, 2)
            dve.tensor_tensor(lamc[:, 4, :], lamc[:, 4, :], lamc[:, 5, :], ALU.mult).then_inc(pad_zeroed, 1)
            dve.wait_ge(pad_zeroed, 3)
            dve.tensor_tensor(lamc[:, 3, :], lamc[:, 4, :], lamc[:, 3, :], ALU.subtract).then_inc(pad_zeroed, 1)
            dve.wait_ge(pad_zeroed, 4)
            dve.scalar_tensor_tensor(out=lamc[:, 2, :], in0=vt[:, V_LAM:V_LAM + KT], scalar=0.0, in1=lamc[:, 3, :],
                                     op0=ALU.min, op1=ALU.add).then_inc(pad_zeroed, 1)
            dve.wait_ge(pad_zeroed, 5)
            dve.tensor_scalar(lamc[:, 4, :], lamc[:, 2, :], LRU_C, None, ALU.mult)
            dve.tensor_scalar(lamc[:, 5, :], lamc[:, 2, :], -LRU_C, None, ALU.mult).then_inc(lam_v, 1)
            def one_minus_a2(b):
                for m in range(4 * b, 4 * b + 4):
                    dve.wait_ge(a_done, m + 1)
                    dve.tensor_tensor(y[:, m, :], la[:, m, :], la[:, m, :], ALU.mult).then_inc(a2_done, 1)
                    dve.wait_ge(a2_done, m + 1)
                    dve.scalar_tensor_tensor(out=lt[:, m, :], in0=y[:, m, :], scalar=1.0, in1=lt[:, m, :],
                                             op0=ALU.add, op1=ALU.mult).then_inc(one_a2, 1)

            def recurrence(m0, m1):
                for m in range(m0, m1):
                    dve.wait_ge(scan_in, m + 1)
                    dve.tensor_tensor_scan(out=y[:, m, :], data0=la[:, m, :], data1=uc[:, m, :], initial=0.0,
                                           op0=ALU.mult, op1=ALU.add).then_inc(scanned, 1)

            def gated(m):
                dve.wait_ge(scanned, m + 1)
                dve.wait_ge(branch_out, m + 1)
                dve.tensor_tensor(lt[:, m, :], y[:, m, :], gel[:, m, :], ALU.mult).then_inc(rg_out, 1)

            lo(N_GB1)
            lo(N_GB1 + 1)
            one_minus_a2(0)
            one_minus_a2(1)
            gb_row(1, 2)
            lo(N_GB1 + 2)
            recurrence(0, 4)
            gb_row(2, 0)
            gated(0)
            gated(1)
            recurrence(4, 6)
            gated(2)
            gated(3)
            lo(N_RGOUT)
            recurrence(6, 8)
            gated(4)
            gated(5)
            mix_lo(2, rg_out_hi, lt, rgh, rgl, rg_out_lo_v)
            mix_lo(4, rg_out_hi, lt, rgh, rgl, rg_out_lo_v)
            gb_row(3, 4)
            gated(6)
            gated(7)
            mix_lo(6, rg_out_hi, lt, rgh, rgl, rg_out_lo_v)
            mix_lo(7, rg_out_hi, lt, rgh, rgl, rg_out_lo_v)
            lo(N_RGOUT + 1)
            clear_acc(2)
            for i in range(4):
                if i % 2:
                    lo(N_RGOUT + 2 + i // 2)
                accumulate(2, i, ITEMS_OUT)
            boundary(2, ITEMS_OUT, N_UP1, V_POSTMIX + KT, V_PREFFN + KT)
            ffn(1, N_UP1, N_DOWN1)
            def times_gain(i):
                j, c = i // 2, slice(S * (i % 2), S * (i % 2 + 1))
                dve.wait_ge(tile_sq, i + 1)
                dve.tensor_tensor(yg[:, j, c], bank[i], grow[:, c], ALU.mult).then_inc(tile_g, 1)

            dve.wait_ge(hT_out, 2 * TT + 2)
            for j in range(TT):
                times_gain(2 * j)
                dve.wait_ge(tile_sq, 2 * j + 2)
                dve.tensor_scalar(small[:, 24 + j:25 + j], small[:, 16 + 2 * j:17 + 2 * j],
                                  small[:, 17 + 2 * j:18 + 2 * j], EPS, ALU.add, ALU.add).then_inc(tile_mean, 1)
                times_gain(2 * j + 1)
                dve.wait_ge(tile_root, j + 1)
                for i in (2 * j, 2 * j + 1):
                    c = slice(S * (i % 2), S * (i % 2 + 1))
                    dve.wait_ge(tile_g, i + 1)
                    dve.scalar_tensor_tensor(out=outT[:, j, c], in0=yg[:, j, c], scalar=small[:, 28 + j:29 + j],
                                             in1=hT[j][:, c], op0=ALU.mult, op1=ALU.add).then_inc(result, 1)

        @block.tensor
        def _(pe):
            def products(dst, sh, sl, mh, ml, first, last):
                pe.matmul(dst, sh, mh, start=first, stop=False)
                pe.matmul(dst, sh, ml, start=False, stop=False)
                return pe.matmul(dst, sl, mh, start=False, stop=last)

            def split_block(n, mm, dst, t0, nt, ready=None, between={}, x=(xsh, xsl), ks=range(KT)):
                s = n % 2
                for k in ks:
                    if k in between:
                        between[k]()
                    if ready is not None:
                        ready(k)
                    c = slice(mm * P, (mm + 1) * P)
                    last = products(dst, kview(wh[s])[:, k, c], kview(wl[s])[:, k, c],
                                    x[0][:, k, t0:t0 + nt], x[1][:, k, t0:t0 + nt], k == 0, k == KT - 1)
                return last

            def full_block(n, banks, done, waits=None, ready=None, x=(xsh, xsl)):
                pe.wait_ge(lo_done, n + 1)
                for mm in range(2):
                    if waits is not None:
                        waits(mm)
                    last = split_block(n, mm, banks[mm], 0, S, ready if mm == 0 else None, x=x)
                    last.then_inc(w_used if mm else done, 1)

            def sum_y(bd, q, accs):
                pe.wait_ge(item_acc, accs)
                for j in range(2):
                    t = q * HALF + j * P
                    last = pe.matmul(SUM[q][:, j:j + 1], accy[:, t:t + P], ones[:, 0:1], start=(j == 0),
                                     stop=(j == 1), skip_group_check=True)
                last.then_inc(ysum, 1)

            def row_y(bd, q):
                pe.wait_ge(ydiag, 2 * bd + q + 1)
                pe.matmul(ROW[q][:, 0:HALF], ones[:, :], diag[:, :, :].rearrange("p a t -> p (a t)"),
                          start=True, stop=True).then_inc(yrow, 1)

            def sum_h(bd, q):
                pe.wait_ge(h_acc, 3 * (2 * bd + q) + 3)
                for j in range(2):
                    t = q * HALF + j * P
                    last = pe.matmul(SUM[q][:, 4 + j:5 + j], accy[:, t:t + P], ones[:, 0:1], start=(j == 0),
                                     stop=(j == 1), skip_group_check=True)
                last.then_inc(hsum, 1)

            def row_h(p, q):
                pe.wait_ge(hdiag, 2 * p + q + 1)
                pe.matmul(ROW[q][:, HALF:S], ones[:, :], diag[:, :, :].rearrange("p a t -> p (a t)"),
                          start=True, stop=True).then_inc(hrow, 1)

            def mix_ready(by_dve, by_pool):
                return lambda k: (pe.wait_ge(by_dve, LO_DVE.index(k) + 1) if k in LO_DVE
                                  else pe.wait_ge(by_pool, LO_POOL.index(k) + 1))

            def xs_ready(p, q):
                def ready(k):
                    if p:
                        pe.wait_ge(x_lo, 16 * (p - 1) + 8 * q + k + 1)
                    elif k % 2 == 0:
                        pe.wait_ge(x0_lo_v, 8 * p + 4 * q + k // 2 + 1)
                    else:
                        pe.wait_ge(x0_lo_p, 8 * p + 4 * q + k // 2 + 1)
                return ready

            def first_two(n, p, done, bd=None):
                dn = done if isinstance(done, tuple) else (done, done)
                for b in range(2):
                    pe.wait_ge(lo_done, n + b + 1)
                    for mm in range(2):
                        between = {}
                        if bd is not None and b == 1:
                            between = {3: lambda: sum_y_b(bd), 7: lambda: row_y(bd, 1)} if mm == 0 else {}
                        if bd is None and b == 1 and mm == 0:
                            between = {4: lambda: row_h(0, 1)}
                        last = split_block(n + b, mm, M[b][:, mm * HALF:(mm + 1) * HALF], 0, HALF,
                                           xs_ready(p, 0) if b == 0 and mm == 0 else None, between)
                    last.then_inc(dn[b], 1)
                for b in range(2):
                    for mm in range(2):
                        between = {}
                        if bd is not None:
                            between = [[{}, {5: lambda: sum_h(bd, 0)}],
                                       [{5: lambda: row_h(p, 0)}, {0: lambda: sum_h(bd, 1), 7: lambda: row_h(p, 1)}]][b][mm]
                        last = split_block(n + b, mm, M[2 + b][:, mm * HALF:(mm + 1) * HALF], HALF, HALF,
                                           xs_ready(p, 1) if b == 0 and mm == 0 else None, between)
                    last.then_inc(w_used, 1)

            accs_after = {0: (ITEMS_OUT, 6, 8), 1: (ITEMS_DOWN, 8, 9), 2: (ITEMS_OUT, 6, 8)}

            def sum_y_b(bd):
                lst, _, nb = accs_after[bd]
                sum_y(bd, 1, accs_before[bd] + 1 + acc_ops(lst[:nb]))

            def sum_y_a(bd):
                lst, na, _ = accs_after[bd]
                sum_y(bd, 0, accs_before[bd] + 1 + acc_ops(lst[:na]))

            def out_proj(bd, n, ready, x):
                base = items_before[bd]
                full_block(n, [M[0], M[1]], item_done, ready=ready, x=x)
                full_block(n + 1, [M[2], M[3]], item_done, x=x)
                for b in range(2):
                    pe.wait_ge(lo_done, n + 3 + b)
                    pe.wait_ge(item_out, base + b + 1)
                    for mm in range(2):
                        last = split_block(n + 2 + b, mm, M[b][:, mm * HALF:(mm + 1) * HALF], 0, HALF, x=x)
                    last.then_inc(item_done, 1)
                for b in range(2):
                    pe.wait_ge(item_out, base + b + 3)
                    for mm in range(2):
                        between = {}
                        if b == 0 and mm == 1:
                            between = {0: lambda: sum_y_a(bd), 5: lambda: row_y(bd, 0)}
                        last = split_block(n + 2 + b, mm, M[2 + b][:, mm * HALF:(mm + 1) * HALF], HALF, HALF,
                                           between=between, x=x)
                    last.then_inc(w_used, 1)

            def down_part(s, part, dst, t0, nt, between={}):
                for k in range(DKT):
                    if k in between:
                        between[k]()
                    kk = part * DKT + k
                    last = products(dst, kview(wh[s], P)[:, k, :], kview(wl[s], P)[:, k, :],
                                    acth[:, kk, t0:t0 + nt], actl[:, kk, t0:t0 + nt],
                                    kk == 0, kk == FT - 1)
                return last

            def down_last(base, nd):
                def tile(j, c, s, kk, first, last):
                    return products(bank[2 * j + c], acth_at(kk, j, acth), acth_at(kk, j, actl),
                                    kview(wh[s], D)[:, kk[1], c * S:(c + 1) * S], kview(wl[s], D)[:, kk[1], c * S:(c + 1) * S],
                                    first, last)

                def acth_at(kk, j, t):
                    return t[:, kk[0] + kk[1], j * P:(j + 1) * P]

                def row_tiles(b, s, order, first=False, last=False):
                    for j in order:
                        for c in range(2):
                            for i in range(2):
                                done = tile(j, c, s, (2 * b, i), first and i == 0, last and i == 1)
                            if last:
                                done.then_inc(tile_done, 1)
                    return done

                pe.wait_ge(lo_done, nd + 1)
                pe.wait_ge(act_l, base + 20)
                pe.wait_ge(hT_out, 2 * TT + 2)
                row_tiles(0, 0, (2, 3), first=True)
                pe.wait_ge(gate_in, base + 22)
                pe.wait_ge(up_in, base + 22)
                row_tiles(0, 0, (0, 1), first=True).then_inc(w_used, 1)
                for b in range(1, FP - 1):
                    pe.wait_ge(lo_done, nd + b + 1)
                    row_tiles(b, b % 2, range(TT)).then_inc(w_used, 1)
                pe.wait_ge(lo_done, nd + FP)
                pe.wait_ge(act_l, base + 22)
                row_tiles(FP - 1, 0, range(TT), last=True)

            def ffn(layer, nu, nd):
                base = 22 * layer
                bd = 2 * layer + 1
                first_two(nu, bd, (gate_done, up_done), bd - 1)
                if layer == 1:
                    pe.wait_ge(row_in, 6)
                    pe.wait_ge(h_up, 48)
                    for i in range(2 * TT + 2):
                        if i >= 4:
                            pe.wait_ge(hT_out, i - 3)
                        j, b = i // 2, i % 2
                        if i < 2 * TT:
                            for k in range(4):
                                last = pe.transpose(bank[4 + i % 4][:, k * P:(k + 1) * P],
                                                    h[:, 4 * b + k, j * P:(j + 1) * P], ident[:, :])
                        else:
                            pe.wait_ge(gdiag_done, 1)
                            last = pe.matmul(bank[4 + i % 4], ones[:, :], gdiag[:, S * b:S * (b + 1)], start=True, stop=True)
                        last.then_inc(hT_done, 1)
                with pe.Fori(1, FP) as j:
                    for b, done in ((0, gate_done), (1, up_done)):
                        pe.wait_ge(lo_done, nu + 1 + b + 2 * j)
                        for mm in range(2):
                            if b == 0:
                                pe.wait_ge(gate_in, base + 2 * j - 1 + mm)
                                if mm:
                                    pe.wait_ge(up_in, base + 2 * j - 1)
                            else:
                                pe.wait_ge(up_in, base + 2 * j - 1 + mm)
                            for k in range(KT):
                                c = slice(mm * P, (mm + 1) * P)
                                last = products(M[2 * b + mm][:, :], kview(wh[b])[:, k, c], kview(wl[b])[:, k, c],
                                                xsh[:, k, :], xsl[:, k, :], k == 0, k == KT - 1)
                            last.then_inc(w_used if mm else done, 1)
                if layer == 1:
                    down_last(base, nd)
                    return
                pe.wait_ge(gate_in, base + 22)
                pe.wait_ge(act_l, base + 20)
                it = items_before[bd]
                with pe.Fori(0, 3) as i:
                    for t in range(2):
                        pe.wait_ge(item_out, it - 1 + t + 2 * i)
                        for part in range(2):
                            pe.wait_ge(lo_done, nd + 1 + part + 2 * t + 4 * i)
                            if part:
                                pe.wait_ge(act_l, base + 22)
                            down_part(part, part, M[t][:, :], 0, S).then_inc(w_used, 1)
                pe.wait_ge(item_out, it + 5)
                for part in range(2):
                    pe.wait_ge(lo_done, nd + 13 + part)
                    down_part(part, part, M[0][:, :], 0, S).then_inc(w_used, 1)
                pe.wait_ge(item_out, it + 6)
                for part in range(2):
                    pe.wait_ge(lo_done, nd + 15 + part)
                    last = down_part(part, part, M[1][:, 0:HALF], 0, HALF)
                last.then_inc(item_done, 1)
                pe.wait_ge(up_in, base + 22)
                down_part(0, 0, M[2][:, 0:HALF], HALF, HALF,
                          {5: lambda: sum_y_a(bd), 9: lambda: row_y(bd, 0)}).then_inc(w_used, 1)
                down_part(1, 1, M[2][:, 0:HALF], HALF, HALF).then_inc(w_used, 1)

            def turn_x(q):
                if q:
                    pe.wait_ge(x_out_v, 2)
                    pe.wait_ge(x_out_a, 2)
                for j in range(2):
                    pe.wait_ge(x_in[2 * q + j], 16)
                    for k in range(KT):
                        last = pe.transpose(X_BANKS[q][k // 2][:, (k % 2) * HALF + j * P:(k % 2) * HALF + (j + 1) * P],
                                            xin[:, 2 * q + j, k * P:(k + 1) * P], ident[:, :])
                        if j == 1 and k % 2 == 1:
                            last.then_inc(x_turned, 1)

            pe.wait_ge(consts, 9)
            turn_x(0)
            row_h(0, 0)
            turn_x(1)
            first_two(N_Q, 0, proj_done)
            pe.wait_ge(gate_w_in, 64)
            for k in range(KT):
                last = pe.matmul(SUM[0][0:40, :], gw[:, k, :], y[:, k, :], start=(k == 0), stop=(k == KT - 1))
            last.then_inc(gates_mm, 1)
            for b in range(2):
                full_block(N_K + b, [M[2 * b], M[2 * b + 1]], proj_done,
                           waits=lambda mm, b=b: pe.wait_ge(proj_out, 2 * b + mm + 1))
            pe.wait_ge(gates_dve, 6)
            pe.wait_ge(gates_act, 5)
            for j in range(TT):
                pe.transpose(SUM[1][:, 8 * j:8 * j + 8], gc[0:8, j * P:(j + 1) * P], ident[0:8, 0:8])
            for j in range(TT):
                last = pe.transpose(SUM[1][:, 32 + 8 * j:40 + 8 * j], gem[0:8, j * P:(j + 1) * P], ident[0:8, 0:8])
            last.then_inc(gates_turned, 1)
            for b in range(4):
                n = N_V + b
                pe.wait_ge(lo_done, n + 1)
                for bb in range(2):
                    i = 8 + 2 * b + bb
                    pe.wait_ge(proj_out, i - 3)
                    for j in range(2):
                        for k in range(KT):
                            t = slice((2 * bb + j) * P, (2 * bb + j + 1) * P)
                            last = products(M[i % 4][:, j * 256:(j + 1) * 256], xsh[:, k, t], xsl[:, k, t],
                                            kview(wh[n % 2])[:, k, :], kview(wl[n % 2])[:, k, :],
                                            k == 0, k == KT - 1)
                    last.then_inc(w_used if bb else proj_done, 1)
            OFF = [0, 512, 1024, 896]

            def scores(t):
                if t:
                    pe.wait_ge(decay_done, t)
                pe.matmul(SUM[0][:, :], sel[:, t, :], z[:, :], start=True, stop=True).then_inc(row_done, 1)
                if t:
                    pe.wait_ge(weighed, t)
                for i in (0, 1, 2, 3):
                    dst = [M[0][:, :], M[1][:, 0:384], M[2][:, 0:256], M[1][:, 384:512]][i]
                    last = pe.matmul(dst, kT[:, t, i * P:(i + 1) * P], qT[:, t // 2, i * P:S],
                                     start=True, stop=True)
                last.then_inc(score, 1)

            def outputs(t):
                pe.wait_ge(weighed, t + 1)
                if t:
                    pe.wait_ge(normalised, t)
                for j in range(TT):
                    for i in range(j + 1):
                        o = OFF[i] + (j - i) * P
                        last = pe.matmul(ROW[j // 2][:, (j % 2) * (DV + 1):(j % 2 + 1) * (DV + 1)],
                                         pt[t % 2][:, o:o + P], v[:, i, t, :], start=(i == 0), stop=(i == j))
                last.then_inc(numer_done, 1)

            def turn(t):
                pe.wait_ge(normalised, t + 1)
                if t:
                    pe.wait_ge(mixed, t)
                for j in range(TT):
                    last = pe.transpose(M[3][:, j * P:(j + 1) * P], nsc[t % 2][:, j, :], ident[:, :])
                last.then_inc(turned, 1)

            def out_gate(t, ks=range(KT)):
                if t % 2 == 0:
                    pe.wait_ge(lo_done, N_O + t // 2 + 1)
                if t:
                    pe.wait_ge(ogate_out, t)
                last = split_block(N_O + t // 2, t % 2, SUM[1], 0, S, ks=ks)
                if ks[-1] == KT - 1:
                    last.then_inc(w_used if t % 2 else proj_done, 1)

            pe.wait_ge(gates_kept, 1)
            pe.wait_ge(proj_out, 16)
            for t in range(HEADS + 2):
                if t < HEADS:
                    scores(t)
                if 1 <= t <= HEADS:
                    outputs(t - 1)
                if t < HEADS - 1:
                    out_gate(t)
                elif t <= HEADS:
                    out_gate(HEADS - 1, range(0, 4) if t < HEADS else range(4, KT))
                if t >= 2:
                    turn(t - 2)
            out_proj(0, N_MLOUT, mix_ready(mixed_lo_v, mixed_lo_p), (mlh, mll))
            ffn(0, N_UP0, N_DOWN0)
            first_two(N_U, 2, u_done, 1)
            for b in range(2):
                full_block(N_U + 2 + b, [M[2 * b], M[2 * b + 1]], u_done,
                           waits=lambda mm, b=b: pe.wait_ge(u_out, 2 * b + mm + 1))
            full_block(N_GB0, [M[0], M[1]], branch_done, waits=lambda mm: pe.wait_ge(u_out, 5 + mm))
            pe.wait_ge(u_out, 8)
            for half in range(2):
                for g, n in ((0, N_GA), (1, N_GX)):
                    pe.wait_ge(lo_done, n + 1)
                    for m in range(4 * half, 4 * half + 4):
                        i = gate_index(m, g)
                        if g == 0:
                            pe.wait_ge(u_low, 2 * (m // 2) + 2)
                        if i >= KT:
                            pe.wait_ge(rgate_out, i - KT + 1)
                        elif i >= 6:
                            pe.wait_ge(branch_in, i - 5)
                        for k in range(2):
                            kk, c = 2 * (m // 2) + k, slice((m % 2) * P, (m % 2 + 1) * P)
                            last = products(gate_bank(m, g), kview(wh[n % 2])[:, kk, c],
                                            kview(wl[n % 2])[:, kk, c], uch[:, kk, :], ucl[:, kk, :], k == 0, k == 1)
                        last.then_inc(w_used if m == KT - 1 else rgate_done, 1)
            for b in range(3):
                b0 = (2, 0, 4)[b]

                def bank_read(mm, b0=b0):
                    pe.wait_ge(rgate_out, KT + (b0 - 2) % 8 + mm + 1)
                full_block(N_GB1 + b, [bank[b0], bank[b0 + 1]], branch_done, waits=bank_read)
            pe.wait_ge(branch_in, 6)
            out_proj(2, N_RGOUT, mix_ready(rg_out_lo_v, rg_out_lo_p), (rgh, rgl))
            ffn(1, N_UP1, N_DOWN1)


NAMES = ["x", "ml_w_in", "ml_b_if", "ml_w_out", "lru_w_in", "lru_w_gate_a", "lru_w_gate_x", "lru_w_out",
         "ffn_w_gate", "ffn_w_up", "ffn_w_down"]


def kernel(**inputs):
    import numpy as _np
    import concourse.bacc as _bacc
    from concourse.bass_utils import run_bass_kernel_spmd as _run

    nc = _bacc.Bacc("TRN2", target_bir_lowering=False, num_devices=1, dynamic_dma_scratch_size=1024)
    arrays, aps = {}, {}
    data = {name: inputs[name] for name in NAMES}
    data["vectors"] = _np.concatenate([_np.asarray(inputs[name]).reshape(-1, P) for name, _ in VECTORS]).T
    for name, arr in data.items():
        arr = _np.ascontiguousarray(arr)
        arrays[f"in_{name}"] = arr
        aps[name] = nc.dram_tensor(f"in_{name}", arr.shape, F32, kind="ExternalInput").ap()
    out = nc.dram_tensor("out_0", (1, S, D), F32, kind="ExternalOutput").ap()
    build(nc, aps, out)
    r = _run(nc, [arrays], core_ids=[0])
    return r.results[0]["out_0"]
```
